# Optimizing a Trainium2 kernel written in Bass

```python
import math
import jax
import jax.numpy as jnp
from jax import lax
import numpy as np

D_MODEL = 1024
BATCH = 1
SEQ = 128
DEPTH = 2
DEC_BATCH = 1
DEC_SEQ = 256
PAST_LEN = 128

GRID_W = 64
POS_BASE = 10000.0
N_MIXERS = 2
N_LAYERS_A = (DEPTH + 1) // 2
N_LAYERS_B = DEPTH // 2
N_DIR = 2
CHUNK = 64
HA = 8
DKA = 128
DVA = 128
CONV_K = 3
HB = 8
DKB = 128
DVB = 128
N_EXPERTS = 16
N_GROUPS = 4
EXP_PER_GROUP = N_EXPERTS // N_GROUPS
TOP_K = 2
D_FF = 512
EPS = 1e-6

PA = 2 * HA * DKA + 2 * HA * DVA + 2 * N_DIR * HA
CONV_CH = 2 * HA * DKA + HA * DVA
PB = 2 * HB * DKB + 2 * HB * DVB + 2 * N_DIR * HB

kernel_name = "bidir_gdn_mlstm_prefix_diffusion_step"

def _rms_norm(x, g):
    xf = x.astype(jnp.float32)
    y = xf * lax.rsqrt(jnp.mean(xf * xf, axis=-1, keepdims=True) + EPS)
    return (y * g.astype(jnp.float32)).astype(x.dtype)

def _l2_normalize(x):
    return x * lax.rsqrt(jnp.sum(x * x, axis=-1, keepdims=True) + EPS)

def _grid_pos_embed(n_tokens):
    rows = n_tokens // GRID_W
    r = jnp.repeat(jnp.arange(rows, dtype=jnp.float32), GRID_W)
    col = jnp.tile(jnp.arange(GRID_W, dtype=jnp.float32), rows)
    quarter = D_MODEL // 4
    freq = jnp.exp(jnp.arange(quarter, dtype=jnp.float32) * (-math.log(POS_BASE) / quarter))

    def axis_embed(pos):
        a = pos[:, None] * freq[None, :]
        return jnp.concatenate([jnp.sin(a), jnp.cos(a)], axis=-1)

    return jnp.concatenate([axis_embed(r), axis_embed(col)], axis=-1)

def _centred_depthwise_conv(x, w):
    pad = CONV_K // 2
    return lax.conv_general_dilated(x, w[:, None, :].astype(x.dtype), window_strides=(1,),
                                    padding=[(pad, pad)], dimension_numbers=('NWC', 'WIO', 'NWC'),
                                    feature_group_count=x.shape[-1])

def _gated_delta_chunked(q, k, v, g, beta, s0):
    B, H, T, DK = q.shape
    DV = v.shape[-1]
    nc = T // CHUNK
    ch = lambda a: jnp.moveaxis(a.reshape(B, H, nc, CHUNK, *a.shape[3:]), 2, 0)
    q, k, v, g, beta = map(ch, (q, k, v, g, beta))
    idx = jnp.arange(CHUNK)
    causal = idx[:, None] >= idx[None, :]
    strict = idx[:, None] > idx[None, :]
    G = jnp.cumsum(g, axis=-1)
    decay = jnp.exp(jnp.where(causal, G[..., :, None] - G[..., None, :], -jnp.inf))
    kb = k * beta[..., None]
    lower = jnp.where(strict, jnp.einsum('nbhcd,nbhsd->nbhcs', kb, k) * decay, 0.0)
    unit_lower = lower + jnp.eye(CHUNK, dtype=lower.dtype)
    rhs = jnp.concatenate([v * beta[..., None], kb * jnp.exp(G)[..., None]], axis=-1)
    sol = lax.linalg.triangular_solve(unit_lower, rhs, left_side=True, lower=True, unit_diagonal=True)
    u, w = sol[..., :DV], sol[..., DV:]
    qk = jnp.where(causal, jnp.einsum('nbhcd,nbhsd->nbhcs', q, k) * decay, 0.0)
    q_dec = q * jnp.exp(G)[..., None]
    k_end = k * jnp.exp(G[..., -1:] - G)[..., None]
    g_end = jnp.exp(G[..., -1])

    def step(S, inp):
        qdc, kec, uc, wc, qkc, gec = inp
        v_new = uc - jnp.einsum('bhcd,bhde->bhce', wc, S)
        o = jnp.einsum('bhcd,bhde->bhce', qdc, S) + jnp.einsum('bhcs,bhse->bhce', qkc, v_new)
        S = gec[..., None, None] * S + jnp.einsum('bhcd,bhce->bhde', kec, v_new)
        return S, o

    S, o = lax.scan(step, s0, (q_dec, k_end, u, w, qk, g_end))
    return jnp.moveaxis(o, 0, 2).reshape(B, H, T, DV), S

def _mlstm_chunked(q, k, v, i_pre, logf, c0, n0, m0):
    B, H, T, DK = q.shape
    DV = v.shape[-1]
    nc = T // CHUNK
    ch = lambda a: jnp.moveaxis(a.reshape(B, H, nc, CHUNK, *a.shape[3:]), 2, 0)
    q, k, v, i_pre, logf = map(ch, (q, k, v, i_pre, logf))
    idx = jnp.arange(CHUNK)
    causal = idx[:, None] >= idx[None, :]
    b = jnp.cumsum(logf, axis=-1)
    log_d = jnp.where(causal, b[..., :, None] - b[..., None, :] + i_pre[..., None, :], -jnp.inf)
    log_d_max = jnp.max(log_d, axis=-1)
    qk = jnp.einsum('nbhcd,nbhsd->nbhcs', q, k)
    log_w_end = b[..., -1:] - b + i_pre

    def step(carry, inp):
        C, nvec, m = carry
        qc, kc, vc, bc, ldc, ldmax, qkc, lwe = inp
        log_inter = bc + m[..., None]
        mt = jnp.maximum(log_inter, ldmax)
        s_inter = jnp.exp(log_inter - mt)
        P = jnp.exp(ldc - mt[..., None]) * qkc
        num = s_inter[..., None] * jnp.einsum('bhcd,bhde->bhce', qc, C) + jnp.einsum('bhcs,bhse->bhce', P, vc)
        den = s_inter * jnp.einsum('bhcd,bhd->bhc', qc, nvec) + jnp.sum(P, axis=-1)
        hc = num / jnp.maximum(jnp.abs(den), jnp.exp(-mt))[..., None]
        log_last = bc[..., -1] + m
        m_new = jnp.maximum(log_last, jnp.max(lwe, axis=-1))
        dec = jnp.exp(log_last - m_new)
        kw = kc * jnp.exp(lwe - m_new[..., None])[..., None]
        C = dec[..., None, None] * C + jnp.einsum('bhcd,bhce->bhde', kw, vc)
        nvec = dec[..., None] * nvec + jnp.sum(kw, axis=-2)
        return (C, nvec, m_new), hc

    (C, nvec, m), hs = lax.scan(step, (c0, n0, m0), (q, k, v, b, log_d, log_d_max, qk, log_w_end))
    return jnp.moveaxis(hs, 0, 2).reshape(B, H, T, DV), C, nvec, m

def _flip_t(a):
    return jnp.flip(a, axis=2)

def _gdn_mixer(h, s0, w_in, conv_w, a_log, dt_bias, norm_g, w_out):
    B, T, _ = h.shape
    f32 = jnp.float32
    nqk, nv = HA * DKA, HA * DVA
    proj = jnp.einsum('btd,dp->btp', h, w_in)
    qkv = jax.nn.silu(_centred_depthwise_conv(proj[..., :2 * nqk + nv], conv_w)).astype(f32)
    z = proj[..., 2 * nqk + nv:2 * nqk + 2 * nv].astype(f32).reshape(B, T, HA, DVA)
    ab = proj[..., 2 * nqk + 2 * nv:].astype(f32).reshape(B, T, 2, N_DIR, HA)
    heads = lambda a, d: a.reshape(B, T, -1, d).transpose(0, 2, 1, 3)
    q = _l2_normalize(heads(qkv[..., :nqk], DKA)) * (DKA ** -0.5)
    k = _l2_normalize(heads(qkv[..., nqk:2 * nqk], DKA))
    v = heads(qkv[..., 2 * nqk:], DVA)
    g = -jnp.exp(a_log.astype(f32)) * jax.nn.softplus(ab[:, :, 0] + dt_bias.astype(f32))
    beta = jax.nn.sigmoid(ab[:, :, 1])
    g = g.transpose(0, 2, 3, 1)
    beta = beta.transpose(0, 2, 3, 1)
    s0 = s0.astype(f32)
    o_f, s_f = _gated_delta_chunked(q, k, v, g[:, 0], beta[:, 0], s0[:, 0])
    o_b, s_b = _gated_delta_chunked(_flip_t(q), _flip_t(k), _flip_t(v), _flip_t(g[:, 1]), _flip_t(beta[:, 1]), s0[:, 1])
    o = (o_f + _flip_t(o_b)).transpose(0, 2, 1, 3)
    o = _rms_norm(o, norm_g) * jax.nn.silu(z)
    out = jnp.einsum('bte,ed->btd', o.reshape(B, T, nv).astype(h.dtype), w_out)
    return out, jnp.stack([s_f, s_b], axis=1)

def _mlstm_mixer(h, c0, n0, m0, w_in, gate_b, norm_g, w_out):
    B, T, _ = h.shape
    f32 = jnp.float32
    nqk, nv = HB * DKB, HB * DVB
    proj = jnp.einsum('btd,dp->btp', h, w_in).astype(f32)
    heads = lambda a, d: a.reshape(B, T, -1, d).transpose(0, 2, 1, 3)
    q = heads(proj[..., :nqk], DKB) * (DKB ** -0.5)
    k = heads(proj[..., nqk:2 * nqk], DKB)
    v = heads(proj[..., 2 * nqk:2 * nqk + nv], DVB)
    o_gate = jax.nn.sigmoid(proj[..., 2 * nqk + nv:2 * nqk + 2 * nv].reshape(B, T, HB, DVB))
    gates = proj[..., 2 * nqk + 2 * nv:].reshape(B, T, 2, N_DIR, HB) + gate_b.astype(f32)
    i_pre = gates[:, :, 0].transpose(0, 2, 3, 1)
    logf = jax.nn.log_sigmoid(gates[:, :, 1]).transpose(0, 2, 3, 1)
    c0, n0, m0 = c0.astype(f32), n0.astype(f32), m0.astype(f32)
    h_f, C_f, n_f, m_f = _mlstm_chunked(q, k, v, i_pre[:, 0], logf[:, 0], c0[:, 0], n0[:, 0], m0[:, 0])
    h_b, C_b, n_b, m_b = _mlstm_chunked(_flip_t(q), _flip_t(k), _flip_t(v), _flip_t(i_pre[:, 1]),
                                        _flip_t(logf[:, 1]), c0[:, 1], n0[:, 1], m0[:, 1])
    hs = (h_f + _flip_t(h_b)).transpose(0, 2, 1, 3)
    y = _rms_norm(hs, norm_g) * o_gate
    out = jnp.einsum('bte,ed->btd', y.reshape(B, T, nv).astype(h.dtype), w_out)
    return out, jnp.stack([C_f, C_b], axis=1), jnp.stack([n_f, n_b], axis=1), jnp.stack([m_f, m_b], axis=1)

def _moe(h, router_w, router_bias, w_gate, w_up, w_down):
    B, T, D = h.shape
    f32 = jnp.float32
    x = h.reshape(B * T, D)
    probs = jax.nn.softmax(jnp.einsum('nd,de->ne', x, router_w).astype(f32), axis=-1)
    sel = (probs + router_bias.astype(f32)).reshape(-1, N_GROUPS, EXP_PER_GROUP)
    group_score = jnp.sum(lax.top_k(sel, TOP_K)[0], axis=-1)
    grp = jnp.argmax(group_score, axis=-1)
    sel_in = jnp.take_along_axis(sel, grp[:, None, None], axis=1)[:, 0]
    _, local = lax.top_k(sel_in, TOP_K)
    expert = grp[:, None] * EXP_PER_GROUP + local
    w = jnp.take_along_axis(probs, expert, axis=-1)
    w = w / jnp.sum(w, axis=-1, keepdims=True)
    gates = jnp.sum(jax.nn.one_hot(expert, N_EXPERTS, dtype=f32) * w[..., None], axis=1).astype(h.dtype)
    hid = jax.nn.silu(jnp.einsum('nd,edf->nef', x, w_gate)) * jnp.einsum('nd,edf->nef', x, w_up)
    y = jnp.einsum('nef,efd->nd', hid * gates[..., None], w_down)
    return y.reshape(B, T, D)

def _trunk(x, cond, init_gdn, init_mC, init_mn, init_mm, p):
    cs = jax.nn.silu(cond.astype(jnp.float32)).astype(x.dtype)
    gdn_s, m_C, m_n, m_m = [], [], [], []
    for layer in range(DEPTH):
        mod = (cs @ p['ada_w'][layer] + p['ada_b'][layer])[:, None, :]
        sh1, sc1, g1, sh2, sc2, g2 = jnp.split(mod, 6, axis=-1)
        hn = _rms_norm(x, p['norm1_g'][layer]) * (1 + sc1) + sh1
        j = layer // N_MIXERS
        if layer % N_MIXERS == 0:
            out, s = _gdn_mixer(hn, init_gdn[:, j], p['gdn_w_in'][j], p['gdn_conv_w'][j], p['gdn_a_log'][j],
                                p['gdn_dt_bias'][j], p['gdn_norm_g'][j], p['gdn_w_out'][j])
            gdn_s.append(s)
        else:
            out, C, n, m = _mlstm_mixer(hn, init_mC[:, j], init_mn[:, j], init_mm[:, j], p['mlstm_w_in'][j],
                                        p['mlstm_gate_b'][j], p['mlstm_norm_g'][j], p['mlstm_w_out'][j])
            m_C.append(C)
            m_n.append(n)
            m_m.append(m)
        x = x + g1 * out.astype(x.dtype)
        hn = _rms_norm(x, p['norm2_g'][layer]) * (1 + sc2) + sh2
        x = x + g2 * _moe(hn, p['router_w'], p['router_bias'], p['exp_w_gate'][layer],
                          p['exp_w_up'][layer], p['exp_w_down'][layer])
    y = _rms_norm(x, p['final_norm_g'])
    return y, jnp.stack(gdn_s, axis=1), jnp.stack(m_C, axis=1), jnp.stack(m_n, axis=1), jnp.stack(m_m, axis=1)

def setup_inputs(seed: int = 0) -> dict:
    key = jax.random.key(seed)
    ks = jax.random.split(key, 32)
    f32 = jnp.float32
    nrm = lambda k, shape, scale: jax.random.normal(k, shape, f32) * scale
    dt = jnp.exp(jax.random.uniform(ks[13], (N_LAYERS_A, N_DIR, HA), f32, math.log(1e-3), math.log(1e-1)))
    return {
        'x_prompt': nrm(ks[0], (BATCH, SEQ, D_MODEL), 1.0),
        'x_sample': nrm(ks[1], (DEC_BATCH, DEC_SEQ, D_MODEL), 1.0),
        'state_gdn_S': nrm(ks[2], (DEC_BATCH, N_LAYERS_A, N_DIR, HA, DKA, DVA), DKA ** -0.5),
        'state_mlstm_C': nrm(ks[3], (DEC_BATCH, N_LAYERS_B, N_DIR, HB, DKB, DVB), 1.0),
        'state_mlstm_n': nrm(ks[4], (DEC_BATCH, N_LAYERS_B, N_DIR, HB, DKB), 1.0),
        'state_mlstm_m': nrm(ks[5], (DEC_BATCH, N_LAYERS_B, N_DIR, HB), 0.5),
        'c': nrm(ks[6], (DEC_BATCH, D_MODEL), 1.0),
        'c_ctx': nrm(ks[7], (D_MODEL,), 1.0),
        'ada_w': nrm(ks[8], (DEPTH, D_MODEL, 6 * D_MODEL), 0.5 * D_MODEL ** -0.5),
        'ada_b': nrm(ks[9], (DEPTH, 6 * D_MODEL), 0.02),
        'norm1_g': 1.0 + nrm(ks[10], (DEPTH, D_MODEL), 0.02),
        'norm2_g': 1.0 + nrm(ks[11], (DEPTH, D_MODEL), 0.02),
        'gdn_w_in': nrm(ks[12], (N_LAYERS_A, D_MODEL, PA), D_MODEL ** -0.5),
        'gdn_conv_w': nrm(ks[14], (N_LAYERS_A, CONV_K, CONV_CH), CONV_K ** -0.5),
        'gdn_a_log': jnp.log(jax.random.uniform(ks[15], (N_LAYERS_A, N_DIR, HA), f32, 1.0, 16.0)),
        'gdn_dt_bias': dt + jnp.log(-jnp.expm1(-dt)),
        'gdn_norm_g': 1.0 + nrm(ks[16], (N_LAYERS_A, DVA), 0.02),
        'gdn_w_out': nrm(ks[17], (N_LAYERS_A, HA * DVA, D_MODEL), (HA * DVA) ** -0.5),
        'mlstm_w_in': nrm(ks[18], (N_LAYERS_B, D_MODEL, PB), D_MODEL ** -0.5),
        'mlstm_gate_b': jnp.stack([nrm(ks[19], (N_LAYERS_B, N_DIR, HB), 0.1),
                                   3.0 + nrm(ks[20], (N_LAYERS_B, N_DIR, HB), 0.5)], axis=1),
        'mlstm_norm_g': 1.0 + nrm(ks[21], (N_LAYERS_B, DVB), 0.02),
        'mlstm_w_out': nrm(ks[22], (N_LAYERS_B, HB * DVB, D_MODEL), (HB * DVB) ** -0.5),
        'router_w': nrm(ks[23], (D_MODEL, N_EXPERTS), D_MODEL ** -0.5),
        'router_bias': nrm(ks[24], (N_EXPERTS,), 0.01),
        'exp_w_gate': nrm(ks[25], (DEPTH, N_EXPERTS, D_MODEL, D_FF), D_MODEL ** -0.5),
        'exp_w_up': nrm(ks[26], (DEPTH, N_EXPERTS, D_MODEL, D_FF), D_MODEL ** -0.5),
        'exp_w_down': nrm(ks[27], (DEPTH, N_EXPERTS, D_FF, D_MODEL), D_FF ** -0.5),
        'final_norm_g': 1.0 + nrm(ks[28], (D_MODEL,), 0.02),
    }

def reference(x_prompt, x_sample, state_gdn_S, state_mlstm_C, state_mlstm_n, state_mlstm_m, c, c_ctx,
              ada_w, ada_b, norm1_g, norm2_g, gdn_w_in, gdn_conv_w, gdn_a_log, gdn_dt_bias, gdn_norm_g,
              gdn_w_out, mlstm_w_in, mlstm_gate_b, mlstm_norm_g, mlstm_w_out, router_w, router_bias,
              exp_w_gate, exp_w_up, exp_w_down, final_norm_g):
    p = dict(ada_w=ada_w, ada_b=ada_b, norm1_g=norm1_g, norm2_g=norm2_g, gdn_w_in=gdn_w_in,
             gdn_conv_w=gdn_conv_w, gdn_a_log=gdn_a_log, gdn_dt_bias=gdn_dt_bias, gdn_norm_g=gdn_norm_g,
             gdn_w_out=gdn_w_out, mlstm_w_in=mlstm_w_in, mlstm_gate_b=mlstm_gate_b, mlstm_norm_g=mlstm_norm_g,
             mlstm_w_out=mlstm_w_out, router_w=router_w, router_bias=router_bias, exp_w_gate=exp_w_gate,
             exp_w_up=exp_w_up, exp_w_down=exp_w_down, final_norm_g=final_norm_g)
    f32 = jnp.float32
    bp = x_prompt.shape[0]
    z_S = jnp.zeros((bp, N_LAYERS_A, N_DIR, HA, DKA, DVA), f32)
    z_C = jnp.zeros((bp, N_LAYERS_B, N_DIR, HB, DKB, DVB), f32)
    z_n = jnp.zeros((bp, N_LAYERS_B, N_DIR, HB, DKB), f32)
    z_m = jnp.zeros((bp, N_LAYERS_B, N_DIR, HB), f32)
    y_prompt, new_gdn_S, new_mlstm_C, new_mlstm_n, new_mlstm_m = _trunk(
        x_prompt, c_ctx[None, :], z_S, z_C, z_n, z_m, p)
    pos = _grid_pos_embed(x_sample.shape[1]).astype(x_sample.dtype)
    y_sample = _trunk(x_sample + pos[None], c, state_gdn_S, state_mlstm_C, state_mlstm_n, state_mlstm_m, p)[0]
    return (y_prompt, y_sample, new_gdn_S, new_mlstm_C, new_mlstm_n, new_mlstm_m)


_drawn_inputs = setup_inputs


def setup_inputs(seed=0):
    import zlib

    import numpy as np

    out = dict(_drawn_inputs(seed))
    spreads = {}
    factors = {'state_mlstm_C': 3.154,
     'state_mlstm_n': 8.0,
     'state_mlstm_m': 8.0,
     'norm2_g': 2.878,
     'gdn_norm_g': 5.867,
     'mlstm_norm_g': 6.562,
     'final_norm_g': 2.727}
    for name, (base, spread) in spreads.items():
        noise = np.random.default_rng([zlib.crc32(name.encode()), seed]).standard_normal(out[name].shape)
        drawn = base * np.exp(spread * noise) if base else spread * noise
        out[name] = jnp.asarray(drawn.astype(out[name].dtype))
    for name, factor in factors.items():
        out[name] = (out[name] * factor).astype(out[name].dtype)
    return out
```

```python
from contextlib import ExitStack

import concourse.bass as bass
import numpy as np
from concourse import mybir

F32 = mybir.dt.float32
I32 = mybir.dt.int32
U32 = mybir.dt.uint32
ALU = mybir.AluOpType
ACT = mybir.ActivationFunctionType
AX_X = mybir.AxisListType.X

P = 128
D = 1024
KD = D // P
T_PROMPT = 128
T_SAMPLE = 256
T = T_PROMPT + T_SAMPLE
NT = T // P
DEPTH = 2
H = 8
N_DIR = 2
NU = N_DIR * NT
CHUNK = 64
NC = T // CHUNK
E = 16
GROUPS = 4
PER_GROUP = E // GROUPS
FF = 512
KF = FF // P
EPS = 1e-6
GRID_W = 64
POS_BASE = 10000.0
LEVELS = 6
SLOT = 4096
ADA_BLOCKS = DEPTH * 6 * D // 512
MAX_TILES = NT
FAR = 1 << 20
SPANS = ((0, 0, T_PROMPT), (1, T_PROMPT, T))

C_ID = 0
C_ONES = C_ID + P
C_INCL = C_ONES + P
C_LEV = C_INCL + N_DIR * P
C_BEFORE = C_LEV + LEVELS * N_DIR * P
C_RESET = C_BEFORE + P
C_ROWDIR = C_RESET + N_DIR * T
C_EPS = C_ROWDIR + N_DIR
C_FIRST16 = C_EPS + 1
C_INDEX16 = C_FIRST16 + E
C_FIRST4 = C_INDEX16 + E
C_ALL = C_FIRST4 + GROUPS


def constants():
    c = np.zeros((P, C_ALL), np.float32)
    c[:, C_ID:C_ID + P] = np.eye(P)
    c[:, C_ONES:C_ONES + P] = 1.0
    j, i = np.meshgrid(np.arange(P), np.arange(P), indexing="ij")
    same = (j // CHUNK) == (i // CHUNK)
    for d in range(N_DIR):
        before = (j <= i) if d == 0 else (j >= i)
        c[:, C_INCL + d * P:C_INCL + (d + 1) * P] = same & before
        for lev in range(LEVELS):
            s = 1 << lev
            pair = (j // (2 * s)) == (i // (2 * s))
            early, late = (j, i) if d == 0 else (i, j)
            m = pair & ((early // s) % 2 == 0) & ((late // s) % 2 == 1)
            at = C_LEV + (lev * N_DIR + d) * P
            c[:, at:at + P] = m
    c[:, C_BEFORE:C_BEFORE + P] = j < i
    t = np.arange(T)
    c[:, C_RESET:C_RESET + T] = t % CHUNK != 0
    c[:, C_RESET + T:C_RESET + 2 * T] = t % CHUNK != CHUNK - 1
    c[0:H, C_ROWDIR] = 1.0
    c[H:2 * H, C_ROWDIR + 1] = 1.0
    c[:, C_EPS] = EPS
    c[:, C_FIRST16:C_FIRST16 + E] = E - np.arange(E)
    c[:, C_INDEX16:C_INDEX16 + E] = np.arange(E)
    c[:, C_FIRST4:C_FIRST4 + GROUPS] = GROUPS - np.arange(GROUPS)
    return c


def grid_positions():
    t = np.arange(T_SAMPLE)
    freq = np.exp(np.arange(D // 4, dtype=np.float32) * np.float32(-np.log(POS_BASE) / (D // 4))).astype(np.float32)

    def axis(pos):
        a = pos.astype(np.float32)[:, None] * freq[None, :]
        return np.concatenate([np.sin(a), np.cos(a)], axis=-1)

    emb = np.concatenate([axis(t // GRID_W), axis(t % GRID_W)], axis=-1).astype(np.float32)
    return np.ascontiguousarray(emb.T.reshape(KD, P, T_SAMPLE).transpose(1, 0, 2))


def token_list_sources():
    tok = np.arange(T, dtype=np.float32).reshape(NT, P).T
    return np.ascontiguousarray(np.stack([np.stack([tok, k * T + tok], -1) for k in range(2)], 1))


class Chain:

    def __init__(self, eng, sem, base=0, turn=None, per=0):
        self.eng, self.sem, self.base, self.turn, self.per, self.n = eng, sem, base, turn, per, 0

    def value(self):
        return self.base + self.n + (0 if self.turn is None else self.turn * self.per)

    def __call__(self, ins):
        ins.then_inc(self.sem, 1)
        self.n += 1
        self.eng.wait_ge(self.sem, self.value())


def wait_turn(eng, sem, value, held, held_value):
    if not isinstance(value, int):
        value = eng.snap(eng.to_reg(value))
    eng.wait_ge(held, held_value)
    eng.wait_ge(sem, value)


def program(nc, a):
    with ExitStack() as ctx:
        def sb(name, shape, dt=F32):
            return ctx.enter_context(nc.sbuf_tensor(name, shape, dt))

        def sem(name):
            return ctx.enter_context(nc.semaphore(name))

        def dram(name, shape, dt=F32):
            return nc.dram_tensor(name, shape, dt, kind="Internal").ap()

        bank = ctx.enter_context(nc.psum_tensor("bank", [P, 8, 512], F32))

        slot = sb("slot", [P, 6, SLOT])
        const = sb("const", [P, C_ALL])
        xT = sb("xT", [P, KD, T])
        hnT = sb("hnT", [P, KD, T])
        yT = sb("yT", [P, KD, T])
        mod = sb("mod", [P, DEPTH, 6, KD, 2])
        gain = sb("gain", [P, 2 * DEPTH, KD, 2])
        norm_g = sb("norm_g", [P, 2 * DEPTH + 1, KD])
        ada_b = sb("ada_b", [P, DEPTH * 6 * KD])
        cond = sb("cond", [P, KD, 2])
        rs = sb("rs", [P, 2, T])
        head_g = sb("head_g", [P, DEPTH])
        conv_w = sb("conv_w", [P, H, 3, 3])
        w_gates = sb("w_gates", [P, DEPTH, KD, 2 * N_DIR * H])
        router = sb("router", [P, KD, E])
        router_b = sb("router_b", [P, E])
        row_bias = sb("row_bias", [N_DIR * H, 5])
        cols = sb("cols", [P, 4, NT, N_DIR * H])
        hcol = sb("hcol", [P, 4, NU])

        SCR = 13200
        scr = sb("scr", [P, SCR])
        at = [0]

        def take(n, where=None):
            lo = at[0]
            at[0] += n
            assert at[0] <= SCR, at[0]
            return scr[:, lo:lo + n]

        def units(x):
            return x.rearrange("p (u i) -> p u i", u=NU)

        def dirs(x):
            return x.rearrange("p (d t) -> p d t", d=N_DIR)

        rows_b = take(2 * N_DIR * T).rearrange("p (q d t) -> p q d t", q=2, d=N_DIR)
        decay_b = take(N_DIR * T)
        qkv = take(3 * T).rearrange("p (s t) -> p s t", s=3)
        gate_z = take(T)
        square = take(2 * T).rearrange("p (s t) -> p s t", s=2)
        qdT = take(N_DIR * T)
        vb = take(NU * P)
        kbe = take(NU * P)
        kend = take(NU * P)
        EM = take(NU * P)
        AT = take(NU * P)
        vnew = take(NU * P)
        Sp = take(N_DIR * 2 * P).rearrange("p (d s e) -> p d s e", d=N_DIR, s=2)
        Ss = take(N_DIR * 4 * P).rearrange("p (d s e) -> p d s e", d=N_DIR, s=4)
        levT = slot[:, 4, 0:5 * NU * P].rearrange("p (l n) -> p l n", l=5)
        Dm = slot[:, 5, 0:NU * P]
        DT = slot[:, 5, NU * P:2 * NU * P]
        X = slot[:, 5, 2 * NU * P:3 * NU * P]
        nwT = slot[:, 5, 3 * NU * P:4 * NU * P]
        kbT = slot[:, 5, 4 * NU * P:5 * NU * P]
        LT = slot[:, 1, 0:NU * P]
        qnT = slot[:, 1, NU * P:NU * P + T]
        knT = slot[:, 1, NU * P + T:NU * P + 2 * T]
        tmpT = slot[:, 1, NU * P + 2 * T:NU * P + 3 * T]
        R = N_DIR * H
        work = [slot[0:R, 1 + 3 * (i // 10), (i % 10) * T:(i % 10 + 1) * T] for i in range(20)]
        small = sb("small", [R, 8, NC])
        m_fin = sb("m_fin", [R, 3])

        rows_d = dram("rows_d", [DEPTH, 3, R, T])
        hn_d = [dram(f"hn_d{i}", [T, D]) for i in range(DEPTH)]
        list_d = [dram(f"list_d{i}", [MAX_TILES * E * P, 2]) for i in range(DEPTH)]
        out_d = [dram(f"out_d{i}", [2 * T, D]) for i in range(DEPTH)]

        ident = const[:, C_ID:C_ID + P]
        ones = const[:, C_ONES:C_ONES + P]
        eps_col = const[:, C_EPS:C_EPS + 1]
        incl = const[:, C_INCL:C_INCL + N_DIR * P].rearrange("p (d i) -> p d i", d=N_DIR)

        def level_mask(lev):
            m = const[:, C_LEV + lev * N_DIR * P:C_LEV + (lev + 1) * N_DIR * P]
            return m.rearrange("p (d o i) -> p d o i", d=N_DIR, o=1)

        const_in = sem("const_in")
        x_in = sem("x_in")
        dve_step = sem("dve_step")
        act_step = sem("act_step")
        ada_in = [sem(f"ada_in{i}") for i in range(6)]
        cond_ready = sem("cond_ready")
        ada_used = sem("ada_used")
        mod_ready = sem("mod_ready")
        x_ready = sem("x_ready")
        sq_ready = sem("sq_ready")
        ss_ready = sem("ss_ready")
        rs_ready = sem("rs_ready")
        hn_scaled = sem("hn_scaled")
        hn_ready = sem("hn_ready")
        gate_mm = sem("gate_mm")
        gate_act = sem("gate_act")
        gate_dve = sem("gate_dve")
        rows_out = sem("rows_out")
        cols_mm = sem("cols_mm")
        cols_ready = sem("cols_ready")
        wout_in = sem("wout_in")
        delta_mm = sem("delta_mm")
        moved = sem("moved")
        stored = sem("stored")

        n_static = {"dve": 0, "act": 0}

        def block_norm_act(act, n, after):
            act.wait_ge(moved, after)
            for k in range(KD):
                nc.scalar.activation(yT[:, k, :], xT[:, k, :], ACT.Square).then_inc(sq_ready, 1)
            act.wait_ge(ss_ready, n + 1)
            nc.scalar.activation(rs[:, 1, :], bank[:, 0, 0:T], ACT.Ln, bias=eps_col,
                                 scale=1.0 / D).then_inc(rs_ready, 1)
            act.wait_ge(rs_ready, 2 * n + 1)
            nc.scalar.activation(rs[:, 0, :], rs[:, 1, :], ACT.Exp, scale=-0.5).then_inc(rs_ready, 1)
            if n < 2 * DEPTH:
                layer, sub = n // 2, n % 2
                for k in range(KD):
                    act.wait_ge(hn_scaled, 2 * (n * KD + k + 1))
                    for g, lo, hi in SPANS:
                        nc.scalar.activation(hnT[:, k, lo:hi], hnT[:, k, lo:hi], ACT.Identity,
                                             bias=mod[:, layer, 3 * sub, k, g:g + 1]).then_inc(hn_ready, 1)

        def block_norm_pe(pe, n):
            for k in range(KD):
                pe.wait_ge(sq_ready, n * KD + k + 1)
                mm = nc.tensor.matmul(bank[:, 0, 0:T], ones, yT[:, k, :], start=(k == 0), stop=(k == KD - 1))
            mm.then_inc(ss_ready, 1)

        def block_norm_dve(dve, n):
            dve.wait_ge(rs_ready, 2 * n + 2)
            for k in range(KD):
                for g, lo, hi in SPANS:
                    g_col = gain[:, n, k, g:g + 1] if n < 2 * DEPTH else norm_g[:, n, k:k + 1]
                    nc.vector.scalar_tensor_tensor(
                        out=hnT[:, k, lo:hi], in0=xT[:, k, lo:hi], scalar=g_col, in1=rs[:, 0, lo:hi],
                        op0=ALU.mult, op1=ALU.mult).then_inc(hn_scaled, 1)

        def residual_dve(dve, n):
            layer, sub = n // 2, n % 2
            for c in range(KD):
                dve.wait_ge(delta_mm, n * KD + c + 1)
                for g, lo, hi in SPANS:
                    nc.vector.scalar_tensor_tensor(
                        out=xT[:, c, lo:hi], in0=bank[:, c, lo:hi], scalar=mod[:, layer, 3 * sub + 2, c, g:g + 1],
                        in1=xT[:, c, lo:hi], op0=ALU.mult, op1=ALU.add).then_inc(moved, 1)

        MOVED_X = 1
        def moved_after(n):
            return MOVED_X + 2 * KD * n

        def chunks(x):
            return x.rearrange("p (c t) -> p c t", t=CHUNK)

        def last_of(x):
            return chunks(x)[:, :, CHUNK - 1], chunks(x)[:, :, 0]

        rowdir = [const[0:R, C_ROWDIR + d:C_ROWDIR + d + 1] for d in range(N_DIR)]
        reset = [const[0:R, C_RESET + d * T:C_RESET + (d + 1) * T] for d in range(N_DIR)]

        def choose(step, out, fwd, bwd, tmp):
            step(nc.vector.tensor_scalar(tmp, fwd, rowdir[0], None, ALU.mult))
            step(nc.vector.scalar_tensor_tensor(out=out, in0=bwd, scalar=rowdir[1], in1=tmp,
                                                op0=ALU.mult, op1=ALU.add))

        def chunk_sums(step, out, x, fwd, bwd, tmp):
            step(nc.vector.tensor_tensor_scan(fwd, reset[0], x, 0.0, ALU.mult, ALU.add))
            step(nc.vector.tensor_tensor_scan(bwd[:, ::-1], reset[1][:, ::-1], x[:, ::-1], 0.0, ALU.mult, ALU.add))
            choose(step, out, fwd, bwd, tmp)

        def gates_pe(pe, layer):
            pe.wait_ge(hn_ready, 2 * KD * (2 * layer + 1))
            pe.wait_ge(const_in, CONST_DMAS * 16)
            for half in range(2):
                for k in range(KD):
                    mm = nc.tensor.matmul(bank[0:R, half, 0:T], w_gates[:, layer, k, half * R:(half + 1) * R],
                                          hnT[:, k, :], start=(k == 0), stop=(k == KD - 1))
            mm.then_inc(gate_mm, 1)

        def columns_pe(pe, sources):
            for q, row in enumerate(sources):
                for t in range(NT):
                    mm = nc.tensor.transpose(bank[:, 2, (q * NT + t) * R:(q * NT + t + 1) * R],
                                             row[:, t * P:(t + 1) * P], ident[0:R, 0:R])
            mm.then_inc(cols_mm, 1)

        W = work
        def gdn_gates_act(act):
            act.wait_ge(gate_dve, 1)
            nc.scalar.activation(W[1], W[0], ACT.Abs).then_inc(gate_act, 1)
            act.wait_ge(gate_act, 1)
            nc.scalar.activation(W[1], W[1], ACT.Exp, scale=-1.0).then_inc(gate_act, 1)
            act.wait_ge(gate_act, 2)
            nc.scalar.activation(W[2], W[1], ACT.Ln, bias=ones[0:R, 0:1]).then_inc(gate_act, 1)
            nc.scalar.activation(row_bias[:, 4:5], row_bias[:, 0:1], ACT.Exp).then_inc(gate_act, 1)
            nc.scalar.activation(W[3], bank[0:R, 1, 0:T], ACT.Exp, scale=-1.0).then_inc(gate_act, 1)
            act.wait_ge(gate_dve, 2)
            nc.scalar.activation(W[10], W[7], ACT.Exp).then_inc(gate_act, 1)
            nc.scalar.activation(W[11], W[9], ACT.Exp).then_inc(gate_act, 1)
            act.wait_ge(cols_mm, 1)
            nc.scalar.activation(cols.rearrange("p q t r -> p (q t r)")[:, 0:4 * NT * R],
                                 bank[:, 2, 0:4 * NT * R], ACT.Copy).then_inc(cols_ready, 1)

        def gdn_gates_dve(dve, step):
            dve.wait_ge(gate_mm, 1)
            nc.vector.tensor_scalar(W[0], bank[0:R, 0, 0:T], row_bias[:, 1:2], None, ALU.add).then_inc(gate_dve, 1)
            dve.wait_ge(gate_dve, 1)
            step(nc.vector.tensor_scalar(W[4], W[0], 0.0, None, ALU.max))
            dve.wait_ge(gate_act, 5)
            step(nc.vector.tensor_tensor(W[4], W[4], W[2], ALU.add))
            step(nc.vector.tensor_scalar(W[4], W[4], row_bias[:, 4:5], -1.0, ALU.mult, ALU.mult))
            step(nc.vector.tensor_scalar(W[8], W[3], 1.0, None, ALU.add))
            step(nc.vector.reciprocal(W[8], W[8]))
            chunk_sums(step, W[7], W[4], W[5], W[6], W[0])
            g_last, g_first = last_of(W[7])
            choose(step, small[:, 0, :], g_last, g_first, small[:, 1, :])
            nc.vector.tensor_tensor(chunks(W[9]), small[:, 0, :].unsqueeze(2).to_broadcast([R, NC, CHUNK]),
                                    chunks(W[7]), ALU.subtract).then_inc(gate_dve, 1)
            dve.wait_ge(gate_act, 7)
            nc.vector.tensor_tensor(W[12], W[8], W[10], ALU.mult).then_inc(gate_dve, 1)

        def mlstm_gates_act(act):
            act.wait_ge(gate_dve, G0 + 1)
            nc.scalar.activation(W[2], W[1], ACT.Abs).then_inc(gate_act, 1)
            act.wait_ge(gate_act, A0 + 1)
            nc.scalar.activation(W[2], W[2], ACT.Exp, scale=-1.0).then_inc(gate_act, 1)
            act.wait_ge(gate_act, A0 + 2)
            nc.scalar.activation(W[3], W[2], ACT.Ln, bias=ones[0:R, 0:1]).then_inc(gate_act, 1)
            act.wait_ge(gate_dve, G0 + 2)
            nc.scalar.activation(W[15], W[12], ACT.Exp).then_inc(gate_act, 1)
            nc.scalar.activation(W[16], W[13], ACT.Exp, scale=-1.0).then_inc(gate_act, 1)
            nc.scalar.activation(W[17], W[14], ACT.Exp).then_inc(gate_act, 1)
            act.wait_ge(cols_mm, 2)
            nc.scalar.activation(cols.rearrange("p q t r -> p (q t r)")[:, 0:2 * NT * R],
                                 bank[:, 2, 0:2 * NT * R], ACT.Copy).then_inc(cols_ready, 1)

        A0, G0 = 7, 3

        def mlstm_gates_dve(dve, step):
            dve.wait_ge(gate_mm, 2)
            step(nc.vector.tensor_scalar(W[0], bank[0:R, 0, 0:T], row_bias[:, 2:3], None, ALU.add))
            nc.vector.tensor_scalar(W[1], bank[0:R, 1, 0:T], row_bias[:, 3:4], None, ALU.add).then_inc(gate_dve, 1)
            dve.wait_ge(gate_dve, G0 + 1)
            dve.wait_ge(gate_act, A0 + 3)
            step(nc.vector.scalar_tensor_tensor(out=W[4], in0=W[1], scalar=0.0, in1=W[3],
                                                op0=ALU.min, op1=ALU.subtract))
            chunk_sums(step, W[7], W[4], W[5], W[6], W[8])
            step(nc.vector.tensor_tensor(W[8], W[0], W[7], ALU.subtract))
            starts = ({0: 0, 2: 1}, {1: 0, 5: 1})
            order = ((0, 1, 2, 3, 4, 5), (1, 0, 5, 4, 3, 2))
            b_last = last_of(W[7])
            for d in range(N_DIR):
                run, carried = W[9 + d], small[:, 2 + d, :]
                r_last = last_of(run)[d]
                for n, c in enumerate(order[d]):
                    if c in starts[d]:
                        step(nc.vector.tensor_copy(carried[:, c:c + 1], m_fin[:, starts[d][c]:starts[d][c] + 1]))
                    cs = slice(c * CHUNK, (c + 1) * CHUNK)
                    flip = (lambda v: v) if d == 0 else (lambda v: v[:, ::-1])
                    step(nc.vector.tensor_tensor_scan(flip(run[:, cs]), flip(W[8][:, cs]), flip(W[8][:, cs]),
                                                      carried[:, c:c + 1], ALU.max, ALU.max))
                    if n == 1:
                        to = small[:, 4 + d, 0:1]
                    elif n < NC - 1:
                        to = carried[:, order[d][n + 1]:order[d][n + 1] + 1]
                    else:
                        continue
                    step(nc.vector.tensor_tensor(to, r_last[:, c:c + 1], b_last[d][:, c:c + 1], ALU.add))
            choose(step, W[11], W[9], W[10], W[12])
            choose(step, small[:, 6, :], small[:, 2, :], small[:, 3, :], small[:, 7, :])
            choose(step, m_fin[:, 2:3], small[:, 4, 0:1], small[:, 5, 0:1], small[:, 7, 0:1])
            m_last, m_first = last_of(W[11])
            choose(step, small[:, 0, :], m_last, m_first, small[:, 1, :])
            step(nc.vector.tensor_tensor(chunks(W[12]), small[:, 6, :].unsqueeze(2).to_broadcast([R, NC, CHUNK]),
                                         chunks(W[11]), ALU.subtract))
            step(nc.vector.tensor_tensor(W[13], W[7], W[11], ALU.add))
            nc.vector.tensor_tensor(chunks(W[14]), chunks(W[8]),
                                    small[:, 0, :].unsqueeze(2).to_broadcast([R, NC, CHUNK]),
                                    ALU.subtract).then_inc(gate_dve, 1)

        g_w = sem("g_w")
        g_rows = sem("g_rows")
        g_state = sem("g_state")
        g_proj = sem("g_proj")
        g_mid = sem("g_mid")
        g_conv = sem("g_conv")
        g_silu = sem("g_silu")
        g_sq = sem("g_sq")
        g_ss = sem("g_ss")
        g_rs = sem("g_rs")
        g_qk = sem("g_qk")
        g_kb = sem("g_kb")
        g_col = sem("g_col")
        g_arg = sem("g_arg")
        g_exp = sem("g_exp")
        g_em = sem("g_em")
        g_lt = sem("g_lt")
        g_lev = sem("g_lev")
        g_at = sem("g_at")
        g_qd = sem("g_qd")
        g_tr = sem("g_tr")
        g_kk = sem("g_kk")
        g_tok = sem("g_tok")
        g_inv = sem("g_inv")
        g_ips = sem("g_ips")
        g_x = sem("g_x")
        g_wps = sem("g_wps")
        g_w2 = sem("g_w2")
        g_vps = sem("g_vps")
        g_vsb = sem("g_vsb")
        g_sps = sem("g_sps")
        g_ssb = sem("g_ssb")
        g_o = sem("g_o")
        g_ors = sem("g_ors")
        g_y = sem("g_y")
        g_dve = sem("g_dve")

        CHAINS = (("s", 0, (2, 3, 4, 5)), ("s", 1, (5, 4, 3, 2)), ("p", 0, (0, 1)), ("p", 1, (1, 0)))
        CHAIN_BANK = (0, 1, 6, 7)

        def state_of(ch, j):
            kind, d, _ = CHAINS[ch]
            if kind == "s":
                return Ss[:, d, j, :]
            return None if j == 0 else Sp[:, d, j - 1, :]

        def steps():
            v = s = 0
            for j in range(4):
                for ch, (_, _, cs) in enumerate(CHAINS):
                    if j < len(cs):
                        updates = CHAINS[ch][0] == "p" or j < 3
                        yield ch, j, v, s if updates else None
                        v += 1
                        s += updates

        STEPS = list(steps())
        STATE_AT = {(ch, j): s for ch, j, _, s in STEPS}

        GDN_DVE = 4

        def gdn_pe(pe):
            with pe.Fori(0, H) as h:
                pe.wait_ge(g_w, h * 16 + 16)
                for s in range(4):
                    for k in range(KD):
                        mm = nc.tensor.matmul(bank[:, s, 0:T], slot[:, 0, (k * 4 + s) * P:(k * 4 + s + 1) * P],
                                              hnT[:, k, :], start=(k == 0), stop=(k == KD - 1))
                    mm.then_inc(g_proj, 1)
                for s in range(2):
                    pe.wait_ge(g_sq, h * 2 + s + 1)
                    nc.tensor.matmul(bank[:, s, 0:T], ones, square[:, s, :], start=True, stop=True).then_inc(g_ss, 1)
                pe.wait_ge(g_silu, h * 4 + 4)
                for t in range(NT):
                    mm = nc.tensor.transpose(bank[:, 4, t * P:(t + 1) * P], qkv[:, 2, t * P:(t + 1) * P], ident)
                mm.then_inc(g_tr, 1)
                pe.wait_ge(g_qk, h * 2 + 2)
                for t in range(NT):
                    mm = nc.tensor.transpose(bank[:, 5, t * P:(t + 1) * P], knT[:, t * P:(t + 1) * P], ident)
                mm.then_inc(g_tr, 1)
                pe.wait_ge(g_kb, h + 1)
                for u in range(NU):
                    t = u % NT
                    mm = nc.tensor.matmul(bank[:, 6 + u // NT, t * P:(t + 1) * P], knT[:, t * P:(t + 1) * P],
                                          kbT[:, u * P:(u + 1) * P], start=True, stop=True)
                mm.then_inc(g_kk, 1)
                for t in range(NT):
                    mm = nc.tensor.matmul(bank[:, 2, t * P:(t + 1) * P], knT[:, t * P:(t + 1) * P],
                                          qnT[:, t * P:(t + 1) * P], start=True, stop=True)
                mm.then_inc(g_kk, 1)
                pe.wait_ge(g_tok, h + 1)
                for g in range(N_DIR):
                    pe.wait_ge(g_inv, h * 14 + g + 1)
                    for t in range(NT):
                        u = g * NT + t
                        mm = nc.tensor.transpose(bank[:, 4 + g, t * P:(t + 1) * P], DT[:, u * P:(u + 1) * P], ident)
                    mm.then_inc(g_ips, 1)
                for lev in range(1, LEVELS):
                    pe.wait_ge(g_lev, h * 5 + lev)
                    for g in range(N_DIR):
                        pe.wait_ge(g_inv, h * 14 + 2 * lev + g + 1)
                        for t in range(NT):
                            us = slice((g * NT + t) * P, (g * NT + t + 1) * P)
                            mm = nc.tensor.matmul(bank[:, g, t * P:(t + 1) * P], levT[:, lev - 1, us], Dm[:, us],
                                                  start=True, stop=True)
                        mm.then_inc(g_ips, 1)
                    for g in range(N_DIR):
                        pe.wait_ge(g_x, h * 10 + 2 * (lev - 1) + g + 1)
                        for t in range(NT):
                            us = slice((g * NT + t) * P, (g * NT + t + 1) * P)
                            if lev < LEVELS - 1:
                                nc.tensor.matmul(bank[:, 4 + g, t * P:(t + 1) * P], DT[:, us], X[:, us],
                                                 start=True, stop=True)
                            mm = nc.tensor.matmul(bank[:, 6 + g, t * P:(t + 1) * P], X[:, us], DT[:, us],
                                                  start=True, stop=True)
                        mm.then_inc(g_ips, 1)
                for g in range(N_DIR):
                    pe.wait_ge(g_inv, h * 14 + 12 + g + 1)
                    for t in range(NT):
                        us = slice((g * NT + t) * P, (g * NT + t + 1) * P)
                        mm = nc.tensor.matmul(bank[:, 4 + g, t * P:(t + 1) * P], kbe[:, us], DT[:, us],
                                              start=True, stop=True)
                    mm.then_inc(g_wps, 1)
                pe.wait_ge(g_w2, h * 2 + 2)
                pe.wait_ge(g_state, h * 16 + 16)
                pe.wait_ge(g_at, h + 1)
                pe.wait_ge(g_qd, h + 1)
                first = [True]

                def into_output(lhsT, rhs, lo, hi):
                    mm = nc.tensor.matmul(bank[:, 2, lo:hi], lhsT, rhs, start=first[0], stop=False,
                                          skip_group_check=True)
                    first[0] = False
                    return mm

                for j in range(4):
                    now = [x for x in STEPS if x[1] == j]
                    for ch, _, v, _ in now:
                        _, d, cs = CHAINS[ch]
                        c = cs[j]
                        u, r = d * NT + c // 2, (c % 2) * CHUNK
                        S = state_of(ch, j)
                        if j > 0:
                            pe.wait_ge(g_ssb, h * 10 + STATE_AT[(ch, j - 1)] + 1)
                        out = bank[r:r + CHUNK, CHAIN_BANK[ch], 0:P]
                        mm = nc.tensor.matmul(out, DT[:, u * P + r:u * P + r + CHUNK], vb[:, u * P:(u + 1) * P],
                                              start=True, stop=S is None)
                        if S is not None:
                            mm = nc.tensor.matmul(out, nwT[:, u * P + r:u * P + r + CHUNK], S, start=False, stop=True)
                        mm.then_inc(g_vps, 1)
                    for ch, _, v, s in now:
                        _, d, cs = CHAINS[ch]
                        c = cs[j]
                        u, r = d * NT + c // 2, (c % 2) * CHUNK
                        S = state_of(ch, j)
                        pe.wait_ge(g_vsb, h * 12 + v + 1)
                        if s is not None:
                            nc.tensor.matmul(bank[:, CHAIN_BANK[ch], P:2 * P], kend[r:r + CHUNK, u * P:(u + 1) * P],
                                             vnew[r:r + CHUNK, u * P:(u + 1) * P], start=True,
                                             stop=True).then_inc(g_sps, 1)
                    for ch, _, v, s in now:
                        _, d, cs = CHAINS[ch]
                        c = cs[j]
                        u = d * NT + c // 2
                        S = state_of(ch, j)
                        if S is not None:
                            mm = into_output(S, qdT[:, d * T + c * CHUNK:d * T + (c + 1) * CHUNK], c * CHUNK, (c + 1) * CHUNK)
                        if j % 2 == 1:
                            mm = into_output(vnew[:, u * P:(u + 1) * P], AT[:, u * P:(u + 1) * P],
                                             (c // 2) * P, (c // 2 + 1) * P)
                mm.then_inc(g_o, 1)
                pe.wait_ge(g_ors, h * 3 + 1)
                nc.tensor.matmul(bank[:, 3, 0:T], ones, square[:, 0, :], start=True, stop=True).then_inc(g_o, 1)
                pe.wait_ge(g_ors, h * 3 + 2)
                pe.wait_ge(g_y, h * 2 + 2)

        def gdn_act(act):
            with act.Fori(0, H) as h:
                for s in range(3):
                    act.wait_ge(g_proj, h * 4 + s + 1)
                    nc.scalar.activation(qkv[:, s, :], bank[:, s, 0:T], ACT.Identity,
                                         scale=conv_w[:, bass.ds(h, 1), 1, s]).then_inc(g_mid, 1)
                act.wait_ge(g_proj, h * 4 + 4)
                nc.scalar.activation(gate_z, bank[:, 3, 0:T], ACT.Silu).then_inc(g_silu, 1)
                for s in range(3):
                    act.wait_ge(g_conv, h * 3 + s + 1)
                    nc.scalar.activation(qkv[:, s, :], qkv[:, s, :], ACT.Silu).then_inc(g_silu, 1)
                for s in range(2):
                    act.wait_ge(g_silu, h * 4 + 2 + s)
                    nc.scalar.activation(square[:, s, :], qkv[:, s, :], ACT.Square).then_inc(g_sq, 1)
                for s in range(2):
                    act.wait_ge(g_ss, h * 2 + s + 1)
                    nc.scalar.activation(rs[:, s, :], bank[:, s, 0:T], ACT.Ln, bias=eps_col).then_inc(g_rs, 1)
                    act.wait_ge(g_rs, h * 4 + 2 * s + 1)
                    nc.scalar.activation(rs[:, s, :], rs[:, s, :], ACT.Exp, scale=-0.5).then_inc(g_rs, 1)
                act.wait_ge(cols_ready, 1)
                nc.scalar.activation(hcol[:, :, :].rearrange("p q (d t) -> p q t d", d=N_DIR),
                                     cols[:, :, :, :].rearrange("p q t (d h) -> p q t d h", h=H)[:, :, :, :, bass.ds(h, 1)]
                                     .rearrange("p q t d h -> p q t (d h)"), ACT.Copy).then_inc(g_col, 1)
                act.wait_ge(g_rows, h * 32 + 32)
                nc.scalar.activation(dirs(decay_b), rows_b[:, 0, :, :], ACT.Exp).then_inc(g_col, 1)
                act.wait_ge(g_arg, h * 2 + 2)
                nc.scalar.activation(EM, EM, ACT.Exp).then_inc(g_exp, 1)
                for g in range(N_DIR):
                    act.wait_ge(g_ips, h * 22 + g + 1)
                    nc.scalar.activation(Dm[:, g * T:(g + 1) * T], bank[:, 4 + g, 0:T], ACT.Copy).then_inc(g_inv, 1)
                for lev in range(1, LEVELS):
                    for g in range(N_DIR):
                        act.wait_ge(g_ips, h * 22 + 2 + 4 * (lev - 1) + g + 1)
                        nc.scalar.activation(X[:, g * T:(g + 1) * T], bank[:, g, 0:T], ACT.Copy).then_inc(g_x, 1)
                for g in range(N_DIR):
                    act.wait_ge(g_wps, h * 2 + g + 1)
                    nc.scalar.activation(nwT[:, g * T:(g + 1) * T], bank[:, 4 + g, 0:T], ACT.Copy,
                                         scale=-1.0).then_inc(g_w2, 1)
                for ch, j, v, _ in STEPS:
                    _, d, cs = CHAINS[ch]
                    c = cs[j]
                    u, r = d * NT + c // 2, (c % 2) * CHUNK
                    act.wait_ge(g_vps, h * 12 + v + 1)
                    nc.scalar.activation(vnew[r:r + CHUNK, u * P:(u + 1) * P], bank[r:r + CHUNK, CHAIN_BANK[ch], 0:P],
                                         ACT.Copy).then_inc(g_vsb, 1)
                act.wait_ge(g_o, h * 2 + 1)
                nc.scalar.activation(square[:, 0, :], bank[:, 2, 0:T], ACT.Square).then_inc(g_ors, 1)
                act.wait_ge(g_o, h * 2 + 2)
                nc.scalar.activation(rs[:, 0, :], bank[:, 3, 0:T], ACT.Ln, bias=eps_col,
                                     scale=1.0 / P).then_inc(g_ors, 1)
                act.wait_ge(g_ors, h * 3 + 2)
                nc.scalar.activation(rs[:, 0, :], rs[:, 0, :], ACT.Exp, scale=-0.5).then_inc(g_ors, 1)

        def gdn_dve(dve):
            with dve.Fori(0, H) as h:
                step = Chain(dve, g_dve, turn=h, per=GDN_DVE)
                for s in range(3):
                    dve.wait_ge(g_mid, h * 3 + s + 1)

                    def tap(lo, hi, shift, w):
                        return nc.vector.scalar_tensor_tensor(
                            out=qkv[:, s, lo:hi], in0=bank[:, s, lo + shift:hi + shift],
                            scalar=conv_w[:, bass.ds(h, 1), w, s], in1=qkv[:, s, lo:hi],
                            op0=ALU.mult, op1=ALU.add)

                    tap(1, T_PROMPT, -1, 0)
                    step(tap(T_PROMPT + 1, T, -1, 0))
                    tap(0, T_PROMPT - 1, 1, 2)
                    tap(T_PROMPT, T - 1, 1, 2).then_inc(g_conv, 1)
                dve.wait_ge(g_rs, h * 4 + 2)
                nc.vector.scalar_tensor_tensor(out=qnT, in0=qkv[:, 0, :], scalar=float(P) ** -0.5, in1=rs[:, 0, :],
                                               op0=ALU.mult, op1=ALU.mult).then_inc(g_qk, 1)
                dve.wait_ge(g_rs, h * 4 + 4)
                nc.vector.tensor_tensor(knT, qkv[:, 1, :], rs[:, 1, :], ALU.mult).then_inc(g_qk, 1)
                dve.wait_ge(g_qk, h * 2 + 2)
                dve.wait_ge(g_rows, h * 32 + 32)
                nc.vector.tensor_tensor(dirs(kbT), knT.unsqueeze(1).to_broadcast([P, N_DIR, T]), rows_b[:, 1, :, :],
                                        ALU.mult).then_inc(g_kb, 1)
                dve.wait_ge(g_em, h + 1)
                dve.wait_ge(g_kk, h * 2 + 1)
                nc.vector.tensor_tensor(dirs(LT), bank[:, 6:8, 0:T], dirs(EM), ALU.mult).then_inc(g_lt, 1)
                dve.wait_ge(g_lt, h + 1)
                step(nc.vector.tensor_tensor(
                    DT.rearrange("p (d t i) -> p d t i", d=N_DIR, t=NT),
                    LT.rearrange("p (d t i) -> p d t i", d=N_DIR, t=NT),
                    level_mask(0).to_broadcast([P, N_DIR, NT, P]), ALU.mult))
                for g in range(N_DIR):
                    v3 = DT[:, g * T:(g + 1) * T].rearrange("p (t i) -> p t i", t=NT)
                    nc.vector.scalar_tensor_tensor(out=v3, in0=v3, scalar=-1.0,
                                                   in1=ident.unsqueeze(1).to_broadcast([P, NT, P]),
                                                   op0=ALU.mult, op1=ALU.add).then_inc(g_inv, 1)
                dve.wait_ge(g_col, h * 2 + 2)
                dve.wait_ge(g_tr, h * 2 + 2)

                def by_column(out, b, q):
                    src = bank[:, b, 0:T].rearrange("p (o t i) -> p o t i", o=1, t=NT)
                    return nc.vector.tensor_tensor(
                        out.rearrange("p (d t i) -> p d t i", d=N_DIR, t=NT), src.to_broadcast([P, N_DIR, NT, P]),
                        hcol[:, q, :].rearrange("p (d t o) -> p d t o", d=N_DIR, o=1).to_broadcast([P, N_DIR, NT, P]),
                        ALU.mult)

                by_column(vb, 4, 1)
                by_column(kbe, 5, 2)
                by_column(kend, 5, 3).then_inc(g_tok, 1)
                dve.wait_ge(g_kk, h * 2 + 2)
                nc.vector.tensor_tensor(dirs(AT), bank[:, 2, 0:T].unsqueeze(1).to_broadcast([P, N_DIR, T]), dirs(EM),
                                        ALU.mult).then_inc(g_at, 1)
                for lev in range(1, LEVELS):
                    for g in range(N_DIR):
                        gs = slice(g * T, (g + 1) * T)
                        dve.wait_ge(g_ips, h * 22 + 2 + 4 * (lev - 1) + 2 + g + 1)
                        if lev < LEVELS - 1:
                            nc.vector.tensor_tensor(Dm[:, gs], Dm[:, gs], bank[:, 4 + g, 0:T], ALU.subtract)
                        nc.vector.tensor_tensor(DT[:, gs], DT[:, gs], bank[:, 6 + g, 0:T],
                                                ALU.subtract).then_inc(g_inv, 1)
                for ch, j, _, s in STEPS:
                    if s is None:
                        continue
                    kind, d, cs = CHAINS[ch]
                    c = cs[j]
                    end = d * T + (c * CHUNK + CHUNK - 1 if d == 0 else c * CHUNK)
                    new = Ss[:, d, j + 1, :] if kind == "s" else Sp[:, d, j, :]
                    dve.wait_ge(g_sps, h * 10 + s + 1)
                    src = bank[:, CHAIN_BANK[ch], P:2 * P]
                    old = state_of(ch, j)
                    if old is None:
                        nc.vector.tensor_copy(new, src).then_inc(g_ssb, 1)
                    else:
                        if j == 0:
                            dve.wait_ge(g_state, h * 16 + 16)
                        else:
                            dve.wait_ge(g_ssb, h * 10 + STATE_AT[(ch, j - 1)] + 1)
                        nc.vector.scalar_tensor_tensor(out=new, in0=old, scalar=decay_b[:, end:end + 1], in1=src,
                                                       op0=ALU.mult, op1=ALU.add).then_inc(g_ssb, 1)
                dve.wait_ge(g_ors, h * 3 + 3)
                nc.vector.scalar_tensor_tensor(out=tmpT, in0=bank[:, 2, 0:T], scalar=head_g[:, 0:1], in1=rs[:, 0, :],
                                               op0=ALU.mult, op1=ALU.mult).then_inc(g_y, 1)
                dve.wait_ge(g_y, h * 2 + 1)
                nc.vector.tensor_tensor(yT[:, bass.ds(h, 1), :].rearrange("p a t -> p (a t)"), tmpT, gate_z,
                                        ALU.mult).then_inc(g_y, 1)
                dve.wait_ge(g_stored, h * 16 + 16)
                dve.wait_ge(g_y, h * 2 + 2)
                assert step.n == GDN_DVE

        g_stored = sem("g_stored")

        def gdn_pool(pool):
            with pool.Fori(0, H) as h:
                pool.wait_ge(g_col, h * 2 + 2)
                em4 = EM.rearrange("p (d t i) -> p d t i", d=N_DIR, t=NT)
                nc.gpsimd.tensor_tensor(em4, rows_b[:, 0, :, :].rearrange("p d (t i) -> p d t i", t=NT),
                                        hcol[:, 0, :].rearrange("p (d t o) -> p d t o", d=N_DIR, o=1)
                                        .to_broadcast([P, N_DIR, NT, P]), ALU.subtract).then_inc(g_arg, 1)
                wait_turn(pool, g_arg, h * 2 + 1, const_in, 16 * CONST_DMAS)
                nc.gpsimd.tensor_scalar(EM, EM, 0.0, None, ALU.min).then_inc(g_arg, 1)
                pool.wait_ge(g_exp, h + 1)
                nc.gpsimd.tensor_tensor(em4, em4, incl.rearrange("p d (o i) -> p d o i", o=1)
                                        .to_broadcast([P, N_DIR, NT, P]), ALU.mult).then_inc(g_em, 1)
                pool.wait_ge(g_lt, h + 1)
                for lev in range(1, LEVELS):
                    nc.gpsimd.tensor_tensor(
                        levT[:, lev - 1, :].rearrange("p (d t i) -> p d t i", d=N_DIR, t=NT),
                        LT.rearrange("p (d t i) -> p d t i", d=N_DIR, t=NT),
                        level_mask(lev).to_broadcast([P, N_DIR, NT, P]), ALU.mult).then_inc(g_lev, 1)
                nc.gpsimd.tensor_tensor(dirs(qdT), qnT.unsqueeze(1).to_broadcast([P, N_DIR, T]), dirs(decay_b),
                                        ALU.mult).then_inc(g_qd, 1)

        def gdn_sync(sp):
            def weights(h):
                sp.dma_start(slot[:, 0, :], a["gdn_w"][bass.ds(h, 1), :, :].rearrange("a p n -> p (a n)")).then_inc(g_w, 16)

            def rows_and_states(h):
                for q in range(2):
                    src = rows_d[0, q].rearrange("(d h) t -> h d t", d=N_DIR)[bass.ds(h, 1), :, :]
                    sp.dma_start(rows_b[:, q, :, :], src.to_broadcast([P, N_DIR, T])).then_inc(g_rows, 16)
                src = a["gdn_S"].rearrange("(d h) k v -> h k d v", d=N_DIR)[bass.ds(h, 1)]
                sp.dma_start(Ss[:, :, 0, :], src.rearrange("a k d v -> (a k) d v")).then_inc(g_state, 16)

            def store(h):
                wait_turn(sp, g_ssb, h * 10 + 10, rows_out, 32)
                dst = a["o_S"].rearrange("(d h) k v -> h k d v", d=N_DIR)[bass.ds(h, 1)]
                sp.dma_start(dst.rearrange("a k d v -> (a k) d v"), Sp[:, :, 1, :]).then_inc(g_stored, 16)

            weights(0)
            sp.wait_ge(rows_out, 32)
            rows_and_states(0)
            with sp.Fori(0, H - 1) as h:
                wait_turn(sp, g_proj, h * 4 + 4, rows_out, 32)
                weights(h + 1)
                store(h)
                wait_turn(sp, g_o, h * 2 + 1, rows_out, 32)
                wait_turn(sp, g_em, h + 1, rows_out, 32)
                wait_turn(sp, g_kb, h + 1, rows_out, 32)
                rows_and_states(h + 1)
            store(H - 1)

        def wout_sync(sp, layer):
            sp.dma_start(slot[:, 2:4, :], a["w_out"][layer].rearrange("p (s n) -> p s n", s=2)).then_inc(wout_in, 16)

        def wout_pe(pe, layer):
            pe.wait_ge(wout_in, 16 * (layer + 1))
            w = slot[:, 2:4, :].rearrange("p s n -> p (s n)").rearrange("p (h n) -> p h n", h=H)
            for c in range(KD):
                for h in range(H):
                    mm = nc.tensor.matmul(bank[:, c, 0:T], w[:, h, c * P:(c + 1) * P], yT[:, h, :],
                                          start=(h == 0), stop=(h == H - 1))
                mm.then_inc(delta_mm, 1)

        m_w = sem("m_w")
        m_rows = sem("m_rows")
        m_state = sem("m_state")
        m_proj = sem("m_proj")
        m_ev = sem("m_ev")
        m_tr = sem("m_tr")
        m_qk = sem("m_qk")
        m_v = sem("m_v")
        m_col = sem("m_col")
        m_arg = sem("m_arg")
        m_exp = sem("m_exp")
        m_em = sem("m_em")
        m_pt = sem("m_pt")
        m_qd = sem("m_qd")
        m_kw = sem("m_kw")
        m_sps = sem("m_sps")
        m_ssb = sem("m_ssb")
        m_nd = sem("m_nd")
        m_abs = sem("m_abs")
        m_h = sem("m_h")
        m_sq = sem("m_sq")
        m_ss = sem("m_ss")
        m_rs = sem("m_rs")
        m_y = sem("m_y")
        m_dve = sem("m_dve")
        m_stored = sem("m_stored")

        A1 = P + 1
        VA = P + 4
        at[0] = 0
        mrows = take(3 * N_DIR * T).rearrange("p (q d t) -> p q d t", q=3, d=N_DIR)
        mqT = take(T)
        mkT = take(T)
        mvT = take(T)
        og = take(T)
        v_aug = take(NT * VA).rearrange("p (t e) -> p t e", t=NT)
        mEM = take(NU * P)
        PT = take(NU * P)
        mqd = take(N_DIR * T)
        kw = take(NU * P)
        hd = take(N_DIR * T)
        den = take(N_DIR * T)
        hs = take(T)
        msq = take(T)
        Cp = take(N_DIR * 2 * VA).rearrange("p (d s e) -> p d s e", d=N_DIR, s=2)
        Cs = take(N_DIR * 4 * VA).rearrange("p (d s e) -> p d s e", d=N_DIR, s=4)

        def cell_of(ch, j):
            kind, d, _ = CHAINS[ch]
            if kind == "s":
                return Cs[:, d, j, :]
            return None if j == 0 else Cp[:, d, j - 1, :]

        MCH = [(ch, j, s) for ch, j, _, s in STEPS]
        MLSTM_DVE = 5

        def mlstm_pe(pe):
            with pe.Fori(0, H) as h:
                pe.wait_ge(m_w, h * 16 + 16)
                for s in range(4):
                    for k in range(KD):
                        mm = nc.tensor.matmul(bank[:, s, 0:T], slot[:, 0, (k * 4 + s) * P:(k * 4 + s + 1) * P],
                                              hnT[:, k, :], start=(k == 0), stop=(k == KD - 1))
                    mm.then_inc(m_proj, 1)
                pe.wait_ge(m_ev, h * 4 + 3)
                for b, src in ((4, mkT), (5, mvT)):
                    for t in range(NT):
                        mm = nc.tensor.transpose(bank[:, b, t * P:(t + 1) * P], src[:, t * P:(t + 1) * P], ident)
                    mm.then_inc(m_tr, 1)
                for t in range(NT):
                    mm = nc.tensor.matmul(bank[:, 6, t * P:(t + 1) * P], mkT[:, t * P:(t + 1) * P],
                                          mqT[:, t * P:(t + 1) * P], start=True, stop=True)
                mm.then_inc(m_qk, 1)
                pe.wait_ge(m_kw, h + 1)
                pe.wait_ge(m_v, h + 1)
                pe.wait_ge(m_ones, 1)
                pe.wait_ge(m_ev, h * 4 + 4)
                for ch, j, s in MCH:
                    if s is None:
                        continue
                    _, d, cs = CHAINS[ch]
                    c = cs[j]
                    u, r = d * NT + c // 2, (c % 2) * CHUNK
                    if j > 0:
                        pe.wait_ge(m_ssb, h * 10 + STATE_AT[(ch, j - 1)] + 1)
                    nc.tensor.matmul(bank[:, ch, 0:A1], kw[r:r + CHUNK, u * P:(u + 1) * P],
                                     v_aug[r:r + CHUNK, c // 2, 0:A1], start=True, stop=True).then_inc(m_sps, 1)
                pe.wait_ge(m_pt, h + 1)
                pe.wait_ge(m_qd, h + 1)
                pe.wait_ge(m_ssb, h * 10 + 10)
                for d in range(N_DIR):
                    for t in range(NT):
                        u = d * NT + t
                        nc.tensor.matmul(bank[:, 4 + d, t * P:(t + 1) * P], v_aug[:, t, 0:P], PT[:, u * P:(u + 1) * P],
                                         start=(t == 0), stop=False, skip_group_check=True)
                    nc.tensor.matmul(bank[:, 6 + d, 0:T], ones, PT[:, d * T:(d + 1) * T], start=True, stop=False,
                                     skip_group_check=True)
                    for ch, j, _ in MCH:
                        _, dd, cs = CHAINS[ch]
                        C = cell_of(ch, j)
                        if dd != d or C is None:
                            continue
                        lo = cs[j] * CHUNK
                        q = mqd[:, d * T + lo:d * T + lo + CHUNK]
                        nc.tensor.matmul(bank[:, 4 + d, lo:lo + CHUNK], C[:, 0:P], q, start=False, stop=False,
                                         skip_group_check=True)
                        mm = nc.tensor.matmul(bank[:, 6 + d, lo:lo + CHUNK], C[:, P:P + 1].to_broadcast([P, P]), q,
                                              start=False, stop=False, skip_group_check=True)
                mm.then_inc(m_nd, 1)
                pe.wait_ge(m_sq, h + 1)
                nc.tensor.matmul(bank[:, 0, 0:T], ones, msq, start=True, stop=True).then_inc(m_ss, 1)
                pe.wait_ge(m_rs, h * 2 + 1)
                pe.wait_ge(m_y, h * 2 + 2)

        def mlstm_act(act):
            with act.Fori(0, H) as h:
                for s, dst, scale in ((0, mqT, float(P) ** -0.5), (1, mkT, 1.0), (2, mvT, 1.0)):
                    act.wait_ge(m_proj, h * 4 + s + 1)
                    nc.scalar.activation(dst, bank[:, s, 0:T], ACT.Copy, scale=scale).then_inc(m_ev, 1)
                act.wait_ge(m_proj, h * 4 + 4)
                nc.scalar.activation(og, bank[:, 3, 0:T], ACT.Exp, scale=-1.0).then_inc(m_ev, 1)
                act.wait_ge(cols_ready, 2)
                nc.scalar.activation(hcol[:, 0:2, :].rearrange("p q (d t) -> p q t d", d=N_DIR),
                                     cols[:, 0:2, :, :].rearrange("p q t (d h) -> p q t d h", h=H)[:, :, :, :, bass.ds(h, 1)]
                                     .rearrange("p q t d h -> p q t (d h)"), ACT.Copy).then_inc(m_col, 1)
                act.wait_ge(m_tr, h * 2 + 2)
                nc.scalar.activation(v_aug[:, :, 0:P], bank[:, 5, 0:T].rearrange("p (t e) -> p t e", t=NT),
                                     ACT.Copy).then_inc(m_v, 1)
                act.wait_ge(m_arg, h * 2 + 2)
                nc.scalar.activation(mEM, mEM, ACT.Exp).then_inc(m_exp, 1)
                act.wait_ge(m_nd, h + 1)
                nc.scalar.activation(dirs(den), bank[:, 6:8, 0:T], ACT.Abs).then_inc(m_abs, 1)
                act.wait_ge(m_h, h + 1)
                nc.scalar.activation(msq, hs, ACT.Square).then_inc(m_sq, 1)
                act.wait_ge(m_ss, h + 1)
                nc.scalar.activation(rs[:, 0, :], bank[:, 0, 0:T], ACT.Ln, bias=eps_col,
                                     scale=1.0 / P).then_inc(m_rs, 1)
                act.wait_ge(m_rs, h * 2 + 1)
                nc.scalar.activation(rs[:, 0, :], rs[:, 0, :], ACT.Exp, scale=-0.5).then_inc(m_rs, 1)

        def mlstm_dve(dve):
            with dve.Fori(0, H) as h:
                step = Chain(dve, m_dve, turn=h, per=MLSTM_DVE)
                dve.wait_ge(m_ev, h * 4 + 4)
                step(nc.vector.tensor_scalar(og, og, 1.0, None, ALU.add))
                step(nc.vector.reciprocal(og, og))
                dve.wait_ge(m_col, h + 1)
                dve.wait_ge(m_tr, h * 2 + 2)
                nc.vector.tensor_tensor(
                    kw.rearrange("p (d t i) -> p d t i", d=N_DIR, t=NT),
                    bank[:, 4, 0:T].rearrange("p (o t i) -> p o t i", o=1, t=NT).to_broadcast([P, N_DIR, NT, P]),
                    hcol[:, 1, :].rearrange("p (d t o) -> p d t o", d=N_DIR, o=1).to_broadcast([P, N_DIR, NT, P]),
                    ALU.mult).then_inc(m_kw, 1)
                dve.wait_ge(m_state, h * 16 + 16)
                for ch, j, s in MCH:
                    if s is None:
                        continue
                    kind, d, cs = CHAINS[ch]
                    c = cs[j]
                    end = c * CHUNK + CHUNK - 1 if d == 0 else c * CHUNK
                    new = Cs[:, d, j + 1, 0:A1] if kind == "s" else Cp[:, d, j, 0:A1]
                    dve.wait_ge(m_sps, h * 10 + s + 1)
                    old = cell_of(ch, j)
                    src = bank[:, ch, 0:A1]
                    if old is None:
                        nc.vector.tensor_copy(new, src).then_inc(m_ssb, 1)
                    else:
                        if j > 0:
                            dve.wait_ge(m_ssb, h * 10 + STATE_AT[(ch, j - 1)] + 1)
                        nc.vector.scalar_tensor_tensor(out=new, in0=old[:, 0:A1], scalar=mrows[:, 1, d, end:end + 1],
                                                       in1=src, op0=ALU.mult, op1=ALU.add).then_inc(m_ssb, 1)
                dve.wait_ge(m_em, h + 1)
                dve.wait_ge(m_qk, h + 1)
                nc.vector.tensor_tensor(dirs(PT), bank[:, 6, 0:T].unsqueeze(1).to_broadcast([P, N_DIR, T]), dirs(mEM),
                                        ALU.mult).then_inc(m_pt, 1)
                dve.wait_ge(m_abs, h + 1)
                step(nc.vector.tensor_tensor(dirs(den), dirs(den), mrows[:, 2, :, :], ALU.max))
                step(nc.vector.reciprocal(den, den))
                step(nc.vector.tensor_tensor(dirs(hd), bank[:, 4:6, 0:T], dirs(den), ALU.mult))
                nc.vector.tensor_tensor(hs, hd[:, 0:T], hd[:, T:2 * T], ALU.add).then_inc(m_h, 1)
                dve.wait_ge(m_h, h + 1)
                dve.wait_ge(m_rs, h * 2 + 2)
                nc.vector.scalar_tensor_tensor(out=hd[:, 0:T], in0=hs, scalar=head_g[:, 1:2], in1=rs[:, 0, :],
                                               op0=ALU.mult, op1=ALU.mult).then_inc(m_y, 1)
                dve.wait_ge(m_y, h * 2 + 1)
                nc.vector.tensor_tensor(yT[:, bass.ds(h, 1), :].rearrange("p a t -> p (a t)"), hd[:, 0:T], og,
                                        ALU.mult).then_inc(m_y, 1)
                dve.wait_ge(m_stored, h * 16 + 16)
                dve.wait_ge(m_y, h * 2 + 2)
                assert step.n == MLSTM_DVE

        def mlstm_pool(pool):
            with pool.Fori(0, H) as h:
                em4 = mEM.rearrange("p (d t i) -> p d t i", d=N_DIR, t=NT)
                pool.wait_ge(m_col, h + 1)
                pool.wait_ge(m_rows, h * 48 + 48)
                nc.gpsimd.tensor_tensor(em4, hcol[:, 0, :].rearrange("p (d t o) -> p d t o", d=N_DIR, o=1)
                                        .to_broadcast([P, N_DIR, NT, P]),
                                        mrows[:, 0, :, :].rearrange("p d (t i) -> p d t i", t=NT),
                                        ALU.subtract).then_inc(m_arg, 1)
                wait_turn(pool, m_arg, h * 2 + 1, const_in, 16 * CONST_DMAS)
                nc.gpsimd.tensor_scalar(mEM, mEM, 0.0, None, ALU.min).then_inc(m_arg, 1)
                pool.wait_ge(m_exp, h + 1)
                nc.gpsimd.tensor_tensor(em4, em4, incl.rearrange("p d (o i) -> p d o i", o=1)
                                        .to_broadcast([P, N_DIR, NT, P]), ALU.mult).then_inc(m_em, 1)
                pool.wait_ge(m_ev, h * 4 + 1)
                nc.gpsimd.tensor_tensor(dirs(mqd), mqT.unsqueeze(1).to_broadcast([P, N_DIR, T]), mrows[:, 1, :, :],
                                        ALU.mult).then_inc(m_qd, 1)

        def mlstm_sync(sp):
            def weights(h):
                sp.dma_start(slot[:, 0, :], a["mlstm_w"][bass.ds(h, 1), :, :].rearrange("a p n -> p (a n)")).then_inc(m_w, 16)

            def rows_and_states(h):
                for q in range(3):
                    src = rows_d[1, q].rearrange("(d h) t -> h d t", d=N_DIR)[bass.ds(h, 1), :, :]
                    sp.dma_start(mrows[:, q, :, :], src.to_broadcast([P, N_DIR, T])).then_inc(m_rows, 16)
                src = a["mlstm_C"].rearrange("(d h) k v -> h k d v", d=N_DIR)[bass.ds(h, 1)]
                sp.dma_start(Cs[:, :, 0, 0:A1], src.rearrange("a k d v -> (a k) d v")).then_inc(m_state, 16)

            def store(h):
                wait_turn(sp, m_ssb, h * 10 + 10, rows_out, 80)
                dst = a["o_C"].rearrange("(d h) k v -> h k d v", d=N_DIR)[bass.ds(h, 1)]
                sp.dma_start(dst.rearrange("a k d v -> (a k) d v"), Cp[:, :, 1, 0:A1]).then_inc(m_stored, 16)

            weights(0)
            sp.wait_ge(rows_out, 80)
            rows_and_states(0)
            with sp.Fori(0, H - 1) as h:
                wait_turn(sp, m_proj, h * 4 + 4, rows_out, 80)
                weights(h + 1)
                store(h)
                wait_turn(sp, m_h, h + 1, rows_out, 80)
                rows_and_states(h + 1)
            store(H - 1)

        at[0] = 0
        htok = take(2 * D).rearrange("p (s n) -> p s n", s=2)
        XG = take(2 * D).rearrange("p (s n) -> p s n", s=2)
        xgT = take(D)
        sl = take(FF)
        hid = take(FF)
        hidT = take(FF)
        ysb = take(D)
        NE3 = NT * E
        N_LISTS = MAX_TILES * E
        rt = [take(NE3) for _ in range(9)]
        r4 = [take(NT * GROUPS) for _ in range(8)]
        r1 = [take(NT) for _ in range(8)]
        g_tok_k = [take(NT) for _ in range(2)]
        place_f = take(2 * NT)
        n_f = take(4)
        lists = take(2 * P)
        far_f = sb("far_f", [P, 2 * N_LISTS])
        place = sb("place", [P, 2 * NT], U32)
        expl = sb("expl", [P, 2, N_LISTS + 4], U32)
        gidx = sb("gidx", [P, 2], U32)
        sidx = sb("sidx", [P, 1], U32)
        lsrc = sb("lsrc", [P, 2, NT, 2])
        n_more = sb("n_more", [1, 1], I32)
        yk = slot[:, 0:2, :].rearrange("p s n -> p (s n)")[:, 0:2 * NT * D].rearrange("p (k t n) -> p k t n", k=2, t=NT)

        e_tr = sem("e_tr")
        e_tok = sem("e_tok")
        e_hn_out = [sem(f"e_hn_out{i}") for i in range(NT)]
        e_logit = sem("e_logit")
        e_shift = sem("e_shift")
        e_prob = sem("e_prob")
        e_count = sem("e_count")
        e_pos = sem("e_pos")
        e_place = sem("e_place")
        far_out = sem("far_out")
        list_clear = sem("list_clear")
        m_ones = sem("m_ones")
        xg_clear = sem("xg_clear")
        e_listed = [sem(f"e_listed{i}") for i in range(DEPTH)]
        e_list_in = sem("e_list_in")
        e_lt = sem("e_lt")
        e_expl = sem("e_expl")
        e_yk = sem("e_yk")
        e_comb = sem("e_comb")
        PASS = ("gu_in0", "gu_in1", "d_in0", "d_in1", "got0", "got1", "put", "idx", "xp",
                "xga", "xgd", "up", "silu", "hid", "ht_ps", "ht", "y_ps", "ya", "yd", "y_free")
        moe = [{name: sem(f"e{layer}_{name}") for name in PASS} for layer in range(DEPTH)]

        w_gate = [slot[:, 0, :].rearrange("p (k f) -> p k f", k=KD), slot[:, 5, :].rearrange("p (k f) -> p k f", k=KD)]
        w_up = [slot[:, 1, :].rearrange("p (k f) -> p k f", k=KD), slot[:, 2, :].rearrange("p (k f) -> p k f", k=KD)]
        w_down = [slot[:, 4, :].rearrange("p (k n) -> p k n", k=KF), slot[:, 3, :].rearrange("p (k n) -> p k n", k=KF)]

        def passes(eng, layer):
            eng.wait_ge(e_place, 2 * layer + 2)
            return eng.snap(eng.value_load(n_more[0:1, 0:1], min_val=0, max_val=(MAX_TILES - 1) * E) + E)

        def route_pe(pe, layer):
            pe.wait_ge(hn_ready, 2 * KD * (2 * layer + 2))
            for t in range(NT):
                if t == 2:
                    pe.wait_ge(e_tok, 6 * layer + 2)
                for k in range(KD):
                    mm = nc.tensor.transpose(bank[:, 2 * (t % 2) + k // 4, (k % 4) * P:(k % 4 + 1) * P],
                                             hnT[:, k, t * P:(t + 1) * P], ident)
                mm.then_inc(e_tr, 1)
                if t == 1:
                    for tt in range(NT):
                        for k in range(KD):
                            mm = nc.tensor.matmul(bank[:, 7, tt * E:(tt + 1) * E], hnT[:, k, tt * P:(tt + 1) * P],
                                                  router[:, k, :], start=(k == 0), stop=(k == KD - 1))
                    mm.then_inc(e_logit, 1)
            pe.wait_ge(e_count, layer + 1)
            cnt = rt[6].rearrange("p (t e) -> p t e", t=NT)
            before = const[:, C_BEFORE:C_BEFORE + P]
            for t in range(NT):
                for tt in range(t):
                    nc.tensor.matmul(bank[:, 6, t * E:(t + 1) * E], ones, cnt[:, tt, :], start=(tt == 0), stop=False)
                nc.tensor.matmul(bank[:, 6, t * E:(t + 1) * E], before, cnt[:, t, :], start=(t == 0), stop=True)
            for t in range(NT):
                mm = nc.tensor.matmul(bank[:, 6, NT * E:(NT + 1) * E], ones, cnt[:, t, :], start=(t == 0),
                                      stop=(t == NT - 1))
            mm.then_inc(e_pos, 1)
            pe.wait_ge(e_list_in, 16 * (layer + 1))
            lv = lists[0:N_LISTS, :].rearrange("n (p k) -> n k p", k=2)
            for k in range(2):
                mm = nc.tensor.transpose(bank[:, 7, k * N_LISTS:(k + 1) * N_LISTS], lv[:, k, :],
                                         ident[0:N_LISTS, 0:N_LISTS])
            mm.then_inc(e_lt, 1)

        def route_act(act, layer):
            for t in range(NT):
                act.wait_ge(e_tr, 3 * layer + t + 1)
                if t == 2:
                    act.wait_ge(e_hn_out[0], 16 * (layer + 1))
                for b in range(2):
                    nc.scalar.activation(htok[:, t % 2, b * 512:(b + 1) * 512], bank[:, 2 * (t % 2) + b, :],
                                         ACT.Copy).then_inc(e_tok, 1)
            act.wait_ge(e_shift, layer + 1)
            nc.scalar.activation(rt[0], rt[0], ACT.Exp).then_inc(e_prob, 1)

        def route_dve(dve, layer, step):
            def te(x):
                return x.rearrange("p (t e) -> p t e", t=NT)

            def tg(x):
                return x.rearrange("p (t g) -> p t g", t=NT)

            def each(x, n=E):
                return x.unsqueeze(2).to_broadcast([P, NT, n])

            def row(c, n=E):
                return const[:, c:c + n].unsqueeze(1).to_broadcast([P, NT, n])

            TT = nc.vector.tensor_tensor
            RED = nc.vector.tensor_reduce
            dve.wait_ge(e_logit, layer + 1)
            step(RED(r1[0], te(bank[:, 7, 0:NE3]), AX_X, ALU.max))
            TT(te(rt[0]), te(bank[:, 7, 0:NE3]), each(r1[0]), ALU.subtract).then_inc(e_shift, 1)
            dve.wait_ge(e_prob, layer + 1)
            step(RED(r1[1], te(rt[0]), AX_X, ALU.add))
            step(nc.vector.reciprocal(r1[1], r1[1]))
            step(TT(te(rt[1]), te(rt[0]), each(r1[1]), ALU.mult))
            step(TT(te(rt[2]), te(rt[1]), router_b[:, :].unsqueeze(1).to_broadcast([P, NT, E]), ALU.add))
            v = rt[2].rearrange("p (n i) -> p n i", i=PER_GROUP)
            step(TT(r4[0], v[:, :, 0], v[:, :, 1], ALU.max))
            step(TT(r4[1], v[:, :, 0], v[:, :, 1], ALU.min))
            step(TT(r4[2], v[:, :, 2], v[:, :, 3], ALU.max))
            step(TT(r4[3], v[:, :, 2], v[:, :, 3], ALU.min))
            step(TT(r4[4], r4[0], r4[2], ALU.max))
            step(TT(r4[5], r4[0], r4[2], ALU.min))
            step(TT(r4[6], r4[1], r4[3], ALU.max))
            step(TT(r4[6], r4[5], r4[6], ALU.max))
            step(TT(r4[4], r4[4], r4[6], ALU.add))
            step(RED(r1[2], tg(r4[4]), AX_X, ALU.max))
            step(TT(tg(r4[5]), tg(r4[4]), each(r1[2], GROUPS), ALU.is_equal))
            step(TT(tg(r4[5]), tg(r4[5]), row(C_FIRST4, GROUPS), ALU.mult))
            step(RED(r1[2], tg(r4[5]), AX_X, ALU.max))
            step(TT(tg(r4[7]), tg(r4[5]), each(r1[2], GROUPS), ALU.is_equal))
            step(nc.vector.tensor_scalar(r4[5], r4[7], 1.0, 1e30, ALU.subtract, ALU.mult))
            v3 = rt[3].rearrange("p (n i) -> p n i", i=PER_GROUP)
            step(TT(v3, v, r4[7].unsqueeze(2).to_broadcast([P, NT * GROUPS, PER_GROUP]), ALU.mult))
            step(TT(v3, v3, r4[5].unsqueeze(2).to_broadcast([P, NT * GROUPS, PER_GROUP]), ALU.add))
            for k in range(2):
                step(RED(r1[2], te(rt[3]), AX_X, ALU.max))
                step(TT(te(rt[7]), te(rt[3]), each(r1[2]), ALU.is_equal))
                step(TT(te(rt[7]), te(rt[7]), row(C_FIRST16), ALU.mult))
                step(RED(r1[2], te(rt[7]), AX_X, ALU.max))
                step(TT(te(rt[4 + k]), te(rt[7]), each(r1[2]), ALU.is_equal))
                if k == 0:
                    step(nc.vector.scalar_tensor_tensor(out=rt[3], in0=rt[4], scalar=-2e30, in1=rt[3],
                                                        op0=ALU.mult, op1=ALU.add))
                step(TT(rt[8], rt[1], rt[4 + k], ALU.mult))
                step(RED(r1[3 + k], te(rt[8]), AX_X, ALU.add))
            TT(rt[6], rt[4], rt[5], ALU.add).then_inc(e_count, 1)
            step(TT(r1[5], r1[3], r1[4], ALU.add))
            step(nc.vector.reciprocal(r1[5], r1[5]))
            for k in range(2):
                step(TT(g_tok_k[k], r1[3 + k], r1[5], ALU.mult))
            dve.wait_ge(e_pos, layer + 1)
            for k in range(2):
                step(TT(rt[7], bank[:, 6, 0:NE3], rt[4 + k], ALU.mult))
                step(RED(r1[6], te(rt[7]), AX_X, ALU.add))
                step(TT(te(rt[7]), te(rt[4 + k]), row(C_INDEX16), ALU.mult))
                step(RED(r1[7], te(rt[7]), AX_X, ALU.add))
                out = place_f[:, k * NT:(k + 1) * NT]
                step(nc.vector.scalar_tensor_tensor(out=out, in0=r1[7], scalar=float(P), in1=r1[6],
                                                    op0=ALU.mult, op1=ALU.add))
                for m in range(1, MAX_TILES):
                    step(nc.vector.tensor_scalar(r1[2], r1[6], float(m * P), float(E * P - P), ALU.is_ge, ALU.mult))
                    step(TT(out, out, r1[2], ALU.add))
            nc.vector.tensor_copy(place[:, :], place_f).then_inc(e_place, 1)
            step(RED(n_f[:, 0:1], bank[:, 6, NE3:NE3 + E], AX_X, ALU.max))
            step(nc.vector.tensor_scalar(n_f[:, 1:2], n_f[:, 0:1], float(P + 1), float(E), ALU.is_ge, ALU.mult))
            step(nc.vector.tensor_scalar(n_f[:, 2:3], n_f[:, 0:1], float(2 * P + 1), float(E), ALU.is_ge, ALU.mult))
            step(TT(n_f[:, 1:2], n_f[:, 1:2], n_f[:, 2:3], ALU.add))
            nc.vector.tensor_copy(n_more[0:1, 0:1], n_f[0:1, 1:2]).then_inc(e_place, 1)
            dve.wait_ge(e_lt, layer + 1)
            nc.vector.tensor_copy(expl[:, :, 0:N_LISTS], bank[:, 7, 0:2 * N_LISTS].rearrange("p (k n) -> p k n", k=2))\
                .then_inc(e_expl, 1)

        def route_sync(sp, layer):
            for t in range(NT):
                sp.wait_ge(e_tok, 6 * layer + 2 * t + 2)
                sp.dma_start(hn_d[layer][t * P:(t + 1) * P, :], htok[:, t % 2, :]).then_inc(e_hn_out[t], 16)

        def lists_sync(sp, layer):
            sp.wait_ge(e_listed[layer], 16 * 2 * NT)
            sp.dma_start(lists[0:N_LISTS, :], list_d[layer].rearrange("(n p) k -> n (p k)", p=P)).then_inc(e_list_in, 16)

        def moe_pe(pe, layer, n):
            e = moe[layer]

            def loads(q, par, each):
                return (q + 1 if par else q + 2) * (each // 2)

            def gate_up(p, par):
                pe.wait_ge(e["xga"], p + 1)
                pe.wait_ge(e["xgd"], p + 1)
                pe.wait_ge(e[f"gu_in{par}"], loads(p, par, 32))
                for b, w in ((0, w_gate[par]), (1, w_up[par])):
                    for k in range(KD):
                        mm = nc.tensor.matmul(bank[:, b, :], xgT[:, k * P:(k + 1) * P], w[:, k, :],
                                              start=(k == 0), stop=(k == KD - 1))
                    mm.then_inc(e["up"], 1)

            def turn_tokens(p, par):
                pe.wait_ge(e[f"got{par}"], loads(p, par, 16))
                for k in range(KD):
                    mm = nc.tensor.transpose(bank[:, 2 + k // 4, (k % 4) * P:(k % 4 + 1) * P],
                                             XG[:, par, k * P:(k + 1) * P], ident)
                mm.then_inc(e["xp"], 1)

            def down(p, par):
                pe.wait_ge(e["ht"], p + 1)
                pe.wait_ge(e[f"d_in{par}"], loads(p, par, 16))
                for b in range(2):
                    for k in range(KF):
                        mm = nc.tensor.matmul(bank[:, 5 + b, :], hidT[:, k * P:(k + 1) * P],
                                              w_down[par][:, k, b * 512:(b + 1) * 512],
                                              start=(k == 0), stop=(k == KF - 1))
                    mm.then_inc(e["y_ps"], 1)

            def turn_hidden(p):
                pe.wait_ge(e["hid"], p + 1)
                for k in range(KF):
                    mm = nc.tensor.transpose(bank[:, 4, k * P:(k + 1) * P], hid[:, k * P:(k + 1) * P], ident)
                mm.then_inc(e["ht_ps"], 1)

            def outputs_taken(p):
                pe.wait_ge(e["ya"], p + 1)
                pe.wait_ge(e["yd"], p + 1)

            turn_tokens(0, 0)
            gate_up(0, 0)
            turn_tokens(1, 1)
            turn_hidden(0)
            with pe.Fori(1, n - 1, 2) as p:
                gate_up(p, 1)
                turn_tokens(p + 1, 0)
                down(p - 1, 0)
                turn_hidden(p)
                gate_up(p + 1, 0)
                turn_tokens(p + 2, 1)
                outputs_taken(p - 1)
                down(p, 1)
                turn_hidden(p + 1)
                outputs_taken(p)
            gate_up(n - 1, 1)
            down(n - 2, 0)
            turn_hidden(n - 1)
            outputs_taken(n - 2)
            down(n - 1, 1)

        def moe_act(act, layer, n):
            e = moe[layer]

            def tokens(p):
                act.wait_ge(e["xp"], p + 1)
                nc.scalar.activation(xgT[:, 0:512], bank[:, 2, :], ACT.Copy).then_inc(e["xga"], 1)

            def gate(p):
                act.wait_ge(e["up"], 2 * p + 1)
                nc.scalar.activation(sl, bank[:, 0, :], ACT.Silu).then_inc(e["silu"], 1)

            def out(p):
                act.wait_ge(e["y_ps"], 2 * p + 1)
                act.wait_ge(e["y_free"], p + 1)
                nc.scalar.activation(ysb[:, 0:512], bank[:, 5, :], ACT.Copy).then_inc(e["ya"], 1)

            def hidden(p):
                act.wait_ge(e["ht_ps"], p + 1)
                nc.scalar.activation(hidT, bank[:, 4, :], ACT.Copy).then_inc(e["ht"], 1)

            tokens(0)
            gate(0)
            tokens(1)
            hidden(0)
            with act.Fori(1, n - 1) as p:
                gate(p)
                tokens(p + 1)
                out(p - 1)
                hidden(p)
            gate(n - 1)
            out(n - 2)
            hidden(n - 1)
            out(n - 1)

        def moe_dve(dve, layer, n):
            e = moe[layer]

            def tokens(p):
                dve.wait_ge(e["xp"], p + 1)
                nc.vector.tensor_copy(xgT[:, 512:1024], bank[:, 3, :]).then_inc(e["xgd"], 1)

            def product(p):
                dve.wait_ge(e["up"], 2 * p + 2)
                dve.wait_ge(e["silu"], p + 1)
                nc.vector.tensor_tensor(hid, sl, bank[:, 1, :], ALU.mult).then_inc(e["hid"], 1)

            def out(p):
                dve.wait_ge(e["y_ps"], 2 * p + 2)
                dve.wait_ge(e["y_free"], p + 1)
                nc.vector.tensor_copy(ysb[:, 512:1024], bank[:, 6, :]).then_inc(e["yd"], 1)

            tokens(0)
            product(0)
            tokens(1)
            with dve.Fori(1, n - 1) as p:
                product(p)
                tokens(p + 1)
                out(p - 1)
            product(n - 1)
            out(n - 2)
            out(n - 1)

        def moe_start_pool(pool, layer):
            pool.wait_ge(e_place, 2 * layer + 1)
            pool.wait_ge(list_clear, 16 * DEPTH)
            for k in range(2):
                for t in range(NT):
                    i = k * NT + t
                    nc.gpsimd.indirect_dma_start(list_d[layer], bass.IndirectOffsetOnAxis(ap=place[:, i:i + 1], axis=0),
                                                 lsrc[:, k, t, :], None).then_inc(e_listed[layer], 16)
            nc.gpsimd.memset(XG[:, :, :], 0.0).then_inc(xg_clear, 1)
            pool.wait_ge(xg_clear, layer + 1)
            pool.wait_ge(e_expl, layer + 1)
            for t in range(NT):
                pool.wait_ge(e_hn_out[t], 16 * (layer + 1))

        def moe_pool(pool, layer, n):
            e = moe[layer]

            def gather(p, par, idx_count):
                nc.gpsimd.tensor_copy(gidx[:, par:par + 1], expl[:, 0, bass.ds(p, 1)]).then_inc(e["idx"], 1)
                wait_turn(pool, e["idx"], idx_count, e_expl, layer + 1)
                nc.gpsimd.indirect_dma_start(XG[:, par, :], None, hn_d[layer],
                                             bass.IndirectOffsetOnAxis(ap=gidx[:, par:par + 1], axis=0),
                                             bounds_check=T - 1, oob_is_err=False).then_inc(e[f"got{par}"], 16)

            def scatter(p, idx_count):
                nc.gpsimd.tensor_copy(sidx[:, :], expl[:, 1, bass.ds(p, 1)]).then_inc(e["idx"], 1)
                wait_turn(pool, e["idx"], idx_count, e_expl, layer + 1)
                wait_turn(pool, e["ya"], p + 1, e_expl, layer + 1)
                wait_turn(pool, e["yd"], p + 1, e_expl, layer + 1)
                nc.gpsimd.indirect_dma_start(out_d[layer], bass.IndirectOffsetOnAxis(ap=sidx[:, 0:1], axis=0),
                                             ysb, None, bounds_check=2 * T - 1, oob_is_err=False).then_inc(e["put"], 16)
                wait_turn(pool, e["put"], p * 16 + 16, e_expl, layer + 1)
                pool.sem_inc(e["y_free"], 1)

            pool.sem_inc(e["y_free"], 1)
            gather(0, 0, 1)
            gather(1, 1, 2)
            with pool.Fori(0, n - 2, 2) as p:
                wait_turn(pool, e["xp"], p + 1, e_expl, layer + 1)
                gather(p + 2, 0, p * 2 + 3)
                scatter(p, p * 2 + 4)
                wait_turn(pool, e["xp"], p + 2, e_expl, layer + 1)
                gather(p + 3, 1, p * 2 + 5)
                scatter(p + 1, p * 2 + 6)
            scatter(n - 2, n * 2 - 1)
            scatter(n - 1, n * 2)

        def moe_weights(sp, layer):
            e = moe[layer]

            def expert(p):
                return p % E + layer * E

            def gate_up(x, par):
                for dst, name in ((w_gate, "w_g"), (w_up, "w_u")):
                    sp.dma_start(dst[par].rearrange("p k f -> p (k f)"),
                                 a[name][bass.ds(x, 1)].rearrange("a p n -> (a p) n")).then_inc(e[f"gu_in{par}"], 16)

            def down(x, par):
                sp.dma_start(w_down[par].rearrange("p k n -> p (k n)"),
                             a["w_d"][bass.ds(x, 1)].rearrange("a p n -> (a p) n")).then_inc(e[f"d_in{par}"], 16)

            return e, expert, gate_up, down

        def moe_first_sync(sp, layer):
            e, expert, gate_up, down = moe_weights(sp, layer)
            for p in range(2):
                gate_up(layer * E + p, p)
                down(layer * E + p, p)

        def moe_sync(sp, layer, n):
            e, expert, gate_up, down = moe_weights(sp, layer)
            sp.wait_ge(e["up"], 2)
            gate_up(layer * E + 2, 0)
            with sp.Fori(1, n - 3, 2) as p:
                x = [sp.snap(expert(p + i)) for i in range(1, 4)]
                wait_turn(sp, e["up"], p * 2 + 2, e_place, 2 * layer + 2)
                gate_up(x[1], 1)
                wait_turn(sp, e["y_ps"], p * 2, e_place, 2 * layer + 2)
                down(x[0], 0)
                wait_turn(sp, e["up"], p * 2 + 4, e_place, 2 * layer + 2)
                gate_up(x[2], 0)
                wait_turn(sp, e["y_ps"], p * 2 + 2, e_place, 2 * layer + 2)
                down(x[1], 1)
            wait_turn(sp, e["up"], n * 2 - 4, e_place, 2 * layer + 2)
            gate_up(layer * E + E - 1, 1)
            wait_turn(sp, e["y_ps"], n * 2 - 6, e_place, 2 * layer + 2)
            down(layer * E + E - 2, 0)
            wait_turn(sp, e["y_ps"], n * 2 - 4, e_place, 2 * layer + 2)
            down(layer * E + E - 1, 1)
            wait_turn(sp, e["up"], n * 2, e_place, 2 * layer + 2)
            wait_turn(sp, e["y_free"], n + 1, e_place, 2 * layer + 2)
            src = out_d[layer].rearrange("(k t p) n -> p k t n", k=2, t=NT)
            for k in range(2):
                sp.dma_start(yk[:, k], src[:, k]).then_inc(e_yk, 16)

        def combine_dve(dve, layer, step):
            dve.wait_ge(e_yk, 32 * (layer + 1))
            for t in range(NT):
                step(nc.vector.tensor_scalar(yk[:, 0, t, :], yk[:, 0, t, :], g_tok_k[0][:, t:t + 1], None, ALU.mult))
                nc.vector.scalar_tensor_tensor(out=yk[:, 0, t, :], in0=yk[:, 1, t, :], scalar=g_tok_k[1][:, t:t + 1],
                                               in1=yk[:, 0, t, :], op0=ALU.mult, op1=ALU.add).then_inc(e_comb, 1)

        def combine_pe(pe, layer):
            pe.wait_ge(e_comb, 3 * (layer + 1))
            for c in range(KD):
                for t in range(NT):
                    mm = nc.tensor.transpose(bank[:, c, t * P:(t + 1) * P], yk[:, 0, t, c * P:(c + 1) * P], ident)
                mm.then_inc(delta_mm, 1)

        LOADS = (("const", const[:, :]), ("xT", xT[:, :, :]), ("posT", hnT[:, :, 0:T_SAMPLE]), ("cond", cond[:, :, :]),
                 ("norm_g", norm_g[:, :, :]), ("ada_b", ada_b[:, :]), ("head_g", head_g[:, :]),
                 ("conv_w", conv_w[:, :, :, :]), ("w_gates", w_gates[:, :, :, :]), ("router", router[:, :, :]),
                 ("row_bias", row_bias[:, 0:4]), ("lsrc", lsrc[:, :, :, :]))
        CONST_DMAS = len(LOADS) + 2

        block = ctx.enter_context(nc.Block())

        @block.sync
        def _(sp):
            for i in range(6):
                sp.dma_start(slot[:, i, :], a["ada_w"][i]).then_inc(ada_in[i], 16)
                if i == 0:
                    for name, dst in LOADS:
                        sp.dma_start(dst, a[name]).then_inc(const_in, 16)
                    sp.dma_start(router_b[:, :], a["router_b"].to_broadcast([P, E])).then_inc(const_in, 16)
                    sp.dma_start(m_fin[:, 1:2], a["mlstm_m"]).then_inc(const_in, 16)
            with sp.Fori(0, ADA_BLOCKS // 6 - 1) as b:
                for i in range(6):
                    wait_turn(sp, ada_used, b * 6 + i + 1, ada_used, 1)
                    sp.dma_start(slot[:, i, :], a["ada_w"][bass.ds(b * 6 + 6 + i, 1)].rearrange("a p n -> (a p) n"))\
                        .then_inc(ada_in[i], 16)
            sp.wait_ge(ada_used, ADA_BLOCKS)
            sp.wait_ge(far_out, 1)
            for layer in range(DEPTH):
                sp.dma_start(list_d[layer].rearrange("(p n) k -> p (n k)", p=P), far_f[:, :]).then_inc(list_clear, 16)
            sp.wait_ge(gate_dve, 2)
            sp.dma_start(rows_d[0, 0], W[7]).then_inc(rows_out, 16)
            sp.dma_start(rows_d[0, 1], W[8]).then_inc(rows_out, 16)
            wout_sync(sp, 0)
            gdn_sync(sp)
            sp.wait_ge(delta_mm, KD)
            moe_first_sync(sp, 0)
            route_sync(sp, 0)
            lists_sync(sp, 0)
            moe_sync(sp, 0, passes(sp, 0))
            sp.wait_ge(gate_dve, G0 + 2)
            sp.dma_start(rows_d[1, 0], W[11]).then_inc(rows_out, 16)
            sp.wait_ge(gate_act, A0 + 6)
            sp.dma_start(rows_d[1, 1], W[15]).then_inc(rows_out, 16)
            sp.dma_start(rows_d[1, 2], W[16]).then_inc(rows_out, 16)
            wout_sync(sp, 1)
            mlstm_sync(sp)
            sp.wait_ge(delta_mm, 3 * KD)
            moe_first_sync(sp, 1)
            route_sync(sp, 1)
            lists_sync(sp, 1)
            moe_sync(sp, 1, passes(sp, 1))
            sp.dma_start(a["o_m"], m_fin[:, 2:3]).then_inc(stored, 16)
            sp.wait_ge(hn_scaled, 2 * KD * (2 * DEPTH + 1))
            sp.dma_start(a["o_y"], hnT[:, :, :]).then_inc(stored, 16)
            sp.wait_ge(stored, 32)
            sp.wait_ge(g_stored, 16 * H)
            sp.wait_ge(m_stored, 16 * H)

        @block.tensor
        def _(pe):
            pe.wait_ge(cond_ready, 1)
            with pe.Fori(0, ADA_BLOCKS // 6) as b:
                for i in range(6):
                    pe.wait_ge(ada_in[i], b * 16 + 16)
                    w = slot[:, i, :].rearrange("p (k n) -> p k n", k=KD)
                    for j in range(4):
                        for k in range(KD):
                            mm = nc.tensor.matmul(bank[:, 0, bass.ds(b * 48 + (i * 4 + j) * 2, 2)],
                                                  w[:, k, j * P:(j + 1) * P], cond[:, k, :],
                                                  start=(k == 0), stop=(k == KD - 1))
                    mm.then_inc(ada_used, 1)
            pe.wait_ge(mod_ready, 1)
            for layer in range(DEPTH):
                block_norm_pe(pe, 2 * layer)
                gates_pe(pe, layer)
                if layer == 0:
                    pe.wait_ge(gate_dve, 3)
                    columns_pe(pe, (W[7], W[8], W[12], W[11]))
                    pe.wait_ge(cols_ready, 1)
                    gdn_pe(pe)
                else:
                    pe.wait_ge(gate_act, A0 + 6)
                    columns_pe(pe, (W[8], W[17]))
                    pe.wait_ge(cols_ready, 2)
                    mlstm_pe(pe)
                wout_pe(pe, layer)
                pe.wait_ge(moved, moved_after(2 * layer + 1))
                block_norm_pe(pe, 2 * layer + 1)
                route_pe(pe, layer)
                n = passes(pe, layer)
                pe.wait_ge(e_expl, layer + 1)
                moe_pe(pe, layer, n)
                pe.wait_ge(moe[layer]["ya"], n)
                pe.wait_ge(moe[layer]["yd"], n)
                combine_pe(pe, layer)
                pe.wait_ge(moved, moved_after(2 * layer + 2))
            block_norm_pe(pe, 2 * DEPTH)

        @block.scalar
        def _(act):
            act.wait_ge(const_in, 16 * CONST_DMAS)
            nc.scalar.activation(cond[:, :, :], cond[:, :, :], ACT.Silu).then_inc(cond_ready, 1)
            block_norm_act(act, 0, MOVED_X)
            gdn_gates_act(act)
            gdn_act(act)
            block_norm_act(act, 1, moved_after(1))
            route_act(act, 0)
            moe_act(act, 0, passes(act, 0))
            block_norm_act(act, 2, moved_after(2))
            mlstm_gates_act(act)
            mlstm_act(act)
            block_norm_act(act, 3, moved_after(3))
            route_act(act, 1)
            moe_act(act, 1, passes(act, 1))
            block_norm_act(act, 4, moved_after(4))

        @block.vector
        def _(dve):
            step = Chain(dve, dve_step)
            dve.wait_ge(const_in, 16 * CONST_DMAS)
            nc.vector.memset(m_fin[:, 0:1], 0.0)
            nc.vector.tensor_tensor(xT[:, :, T_PROMPT:T], xT[:, :, T_PROMPT:T], hnT[:, :, 0:T_SAMPLE],
                                    ALU.add).then_inc(moved, 1)
            dve.wait_ge(ada_used, ADA_BLOCKS)
            n_mod = DEPTH * 6 * KD
            nc.vector.tensor_tensor(mod.rearrange("p l s k c -> p (l s k) c"),
                                    bank[:, 0, 0:2 * n_mod].rearrange("p (n c) -> p n c", c=2),
                                    ada_b[:, :].unsqueeze(2).to_broadcast([P, n_mod, 2]), ALU.add).then_inc(mod_ready, 1)
            dve.wait_ge(mod_ready, 1)
            dve.wait_ge(moved, 1)
            for n in range(2 * DEPTH):
                layer, sub = n // 2, n % 2
                step(nc.vector.tensor_scalar(gain[:, n], mod[:, layer, 3 * sub + 1], 1.0, None, ALU.add))
                step(nc.vector.tensor_tensor(gain[:, n], gain[:, n],
                                             norm_g[:, n, :].unsqueeze(2).to_broadcast([P, KD, 2]), ALU.mult))
            block_norm_dve(dve, 0)
            gdn_gates_dve(dve, step)
            gdn_dve(dve)
            residual_dve(dve, 0)
            dve.wait_ge(moved, moved_after(1))
            block_norm_dve(dve, 1)
            route_dve(dve, 0, step)
            moe_dve(dve, 0, passes(dve, 0))
            combine_dve(dve, 0, step)
            residual_dve(dve, 1)
            dve.wait_ge(moved, moved_after(2))
            block_norm_dve(dve, 2)
            mlstm_gates_dve(dve, step)
            mlstm_dve(dve)
            residual_dve(dve, 2)
            dve.wait_ge(moved, moved_after(3))
            block_norm_dve(dve, 3)
            route_dve(dve, 1, step)
            moe_dve(dve, 1, passes(dve, 1))
            combine_dve(dve, 1, step)
            residual_dve(dve, 3)
            dve.wait_ge(moved, moved_after(4))
            block_norm_dve(dve, 4)

        @block.gpsimd
        def _(pool):
            nc.gpsimd.memset(far_f[:, :], float(FAR)).then_inc(far_out, 1)
            gdn_pool(pool)
            moe_start_pool(pool, 0)
            moe_pool(pool, 0, passes(pool, 0))
            nc.gpsimd.memset(v_aug[:, :, P:VA], 1.0).then_inc(m_ones, 1)
            mlstm_pool(pool)
            moe_start_pool(pool, 1)
            moe_pool(pool, 1, passes(pool, 1))


_OUTS = [("o_y", (P, KD, T)), ("o_S", (N_DIR * H, P, P)), ("o_C", (N_DIR * H, P, P + 1)), ("o_m", (N_DIR * H, 1))]


def laid_out(v):
    f = np.ascontiguousarray
    x = np.concatenate([v["x_prompt"][0], v["x_sample"][0]], 0)

    def heads(w):
        w = w[0][:, :4 * D].reshape(KD, P, 4, H, P)
        return f(w.transpose(3, 1, 0, 2, 4).reshape(H, P, KD * 4 * P))

    def gates(w):
        return w[0][:, 4 * D:].reshape(KD, P, 2 * N_DIR * H).transpose(1, 0, 2)

    def experts(w, k):
        return f(w.reshape(DEPTH * E, k, P, -1).transpose(0, 2, 1, 3).reshape(DEPTH * E, P, -1))

    norms = np.stack([v["norm1_g"][0], v["norm2_g"][0], v["norm1_g"][1], v["norm2_g"][1], v["final_norm_g"]])
    return {
        "const": constants(), "posT": grid_positions(),
        "xT": f(x.T.reshape(KD, P, T).transpose(1, 0, 2)),
        "cond": f(np.stack([v["c_ctx"], v["c"][0]], -1).reshape(KD, P, 2).transpose(1, 0, 2)),
        "norm_g": f(norms.reshape(-1, KD, P).transpose(2, 0, 1)),
        "ada_w": f(v["ada_w"].reshape(DEPTH, KD, P, 6 * D // 512, 512).transpose(0, 3, 2, 1, 4).reshape(ADA_BLOCKS, P, -1)),
        "ada_b": f(v["ada_b"].reshape(-1, P).T),
        "head_g": f(np.stack([v["gdn_norm_g"][0], v["mlstm_norm_g"][0]], -1)),
        "conv_w": f(v["gdn_conv_w"][0].reshape(3, 3, H, P).transpose(3, 2, 0, 1)),
        "w_gates": f(np.stack([gates(v["gdn_w_in"]), gates(v["mlstm_w_in"])], 1)),
        "router": f(v["router_w"].reshape(KD, P, E).transpose(1, 0, 2)),
        "router_b": f(v["router_bias"].reshape(1, E)),
        "row_bias": f(np.stack([v["gdn_a_log"].ravel(), v["gdn_dt_bias"].ravel(), v["mlstm_gate_b"][0, 0].ravel(),
                                v["mlstm_gate_b"][0, 1].ravel()], -1)),
        "lsrc": token_list_sources(),
        "mlstm_m": f(v["state_mlstm_m"].reshape(-1, 1)),
        "gdn_w": heads(v["gdn_w_in"]), "mlstm_w": heads(v["mlstm_w_in"]),
        "w_out": f(np.stack([w[0].reshape(H, P, D).transpose(1, 0, 2).reshape(P, -1)
                             for w in (v["gdn_w_out"], v["mlstm_w_out"])])),
        "gdn_S": f(v["state_gdn_S"].reshape(N_DIR * H, P, P)),
        "mlstm_C": f(np.concatenate([v["state_mlstm_C"].reshape(N_DIR * H, P, P),
                                     v["state_mlstm_n"].reshape(N_DIR * H, P, 1)], -1)),
        "w_g": experts(v["exp_w_gate"], KD), "w_u": experts(v["exp_w_up"], KD), "w_d": experts(v["exp_w_down"], KF),
    }


def kernel(**inputs):
    import concourse.bacc as bacc
    from concourse.bass_utils import run_bass_kernel_spmd

    nc = bacc.Bacc("TRN2", target_bir_lowering=False, num_devices=1)
    arrays, args = {}, {}
    for name, x in laid_out({k: np.asarray(x) for k, x in inputs.items()}).items():
        arrays[f"in_{name}"] = x
        args[name] = nc.dram_tensor(f"in_{name}", x.shape, mybir.dt.from_np(x.dtype), kind="ExternalInput").ap()
    for name, shape in _OUTS:
        args[name] = nc.dram_tensor(f"out_{name}", shape, F32, kind="ExternalOutput").ap()
    program(nc, args)
    r = run_bass_kernel_spmd(nc, [arrays], core_ids=[0]).results[0]
    y = np.ascontiguousarray(r["out_o_y"].transpose(2, 1, 0).reshape(T, D))
    C = r["out_o_C"].reshape(1, 1, N_DIR, H, P, P + 1)
    return (y[:T_PROMPT].reshape(1, T_PROMPT, D), y[T_PROMPT:].reshape(1, T_SAMPLE, D),
            r["out_o_S"].reshape(1, 1, N_DIR, H, P, P), np.ascontiguousarray(C[..., :P]),
            np.ascontiguousarray(C[..., P]), r["out_o_m"].reshape(1, 1, N_DIR, H))
```

```python
from contextlib import ExitStack

import concourse.bass as bass
import numpy as np
from concourse import mybir

F32 = mybir.dt.float32
I32 = mybir.dt.int32
U32 = mybir.dt.uint32
ALU = mybir.AluOpType
ACT = mybir.ActivationFunctionType
AX_X = mybir.AxisListType.X

P = 128
D = 1024
KD = D // P
T_PROMPT = 128
T_SAMPLE = 256
T = T_PROMPT + T_SAMPLE
NT = T // P
DEPTH = 2
H = 8
N_DIR = 2
NU = N_DIR * NT
CHUNK = 64
NC = T // CHUNK
E = 16
TOP_K = 2
GROUPS = 4
PER_GROUP = E // GROUPS
FF = 512
KF = FF // P
EPS = 1e-6
GRID_W = 64
POS_BASE = 10000.0
LEVELS = 6
SLOT = 4096
ADA_BLOCKS = DEPTH * 6 * D // 512
MAX_MORE = (TOP_K * T // (P + 1) + 1) // 2 * 2
N_PASSES = E + MAX_MORE
FAR = 1 << 20
SPANS = ((0, 0, T_PROMPT), (1, T_PROMPT, T))

C_ID = 0
C_ONES = C_ID + P
C_INCL = C_ONES + P
C_LEV = C_INCL + N_DIR * P
C_BEFORE = C_LEV + LEVELS * N_DIR * P
C_RESET = C_BEFORE + P
C_ROWDIR = C_RESET + N_DIR * T
C_EPS = C_ROWDIR + N_DIR
C_FIRST16 = C_EPS + 1
C_INDEX16 = C_FIRST16 + E
C_FIRST4 = C_INDEX16 + E
C_MORE = C_FIRST4 + GROUPS
C_ALL = C_MORE + MAX_MORE


def constants():
    c = np.zeros((P, C_ALL), np.float32)
    c[:, C_ID:C_ID + P] = np.eye(P)
    c[:, C_ONES:C_ONES + P] = 1.0
    j, i = np.meshgrid(np.arange(P), np.arange(P), indexing="ij")
    same = (j // CHUNK) == (i // CHUNK)
    for d in range(N_DIR):
        before = (j <= i) if d == 0 else (j >= i)
        c[:, C_INCL + d * P:C_INCL + (d + 1) * P] = same & before
        for lev in range(LEVELS):
            s = 1 << lev
            pair = (j // (2 * s)) == (i // (2 * s))
            early, late = (j, i) if d == 0 else (i, j)
            m = pair & ((early // s) % 2 == 0) & ((late // s) % 2 == 1)
            at = C_LEV + (lev * N_DIR + d) * P
            c[:, at:at + P] = m
    c[:, C_BEFORE:C_BEFORE + P] = j < i
    t = np.arange(T)
    c[:, C_RESET:C_RESET + T] = t % CHUNK != 0
    c[:, C_RESET + T:C_RESET + 2 * T] = t % CHUNK != CHUNK - 1
    c[0:H, C_ROWDIR] = 1.0
    c[H:2 * H, C_ROWDIR + 1] = 1.0
    c[:, C_EPS] = EPS
    c[:, C_FIRST16:C_FIRST16 + E] = E - np.arange(E)
    c[:, C_INDEX16:C_INDEX16 + E] = np.arange(E)
    c[:, C_FIRST4:C_FIRST4 + GROUPS] = GROUPS - np.arange(GROUPS)
    c[:, C_MORE:C_MORE + MAX_MORE] = np.arange(MAX_MORE)
    return c


def grid_positions():
    t = np.arange(T_SAMPLE)
    freq = np.exp(np.arange(D // 4, dtype=np.float32) * np.float32(-np.log(POS_BASE) / (D // 4))).astype(np.float32)

    def axis(pos):
        a = pos.astype(np.float32)[:, None] * freq[None, :]
        return np.concatenate([np.sin(a), np.cos(a)], axis=-1)

    emb = np.concatenate([axis(t // GRID_W), axis(t % GRID_W)], axis=-1).astype(np.float32)
    return np.ascontiguousarray(emb.T.reshape(KD, P, T_SAMPLE).transpose(1, 0, 2))


def token_list_sources():
    tok = np.arange(T, dtype=np.float32).reshape(NT, P).T
    return np.ascontiguousarray(np.stack([np.stack([tok, k * T + tok], -1) for k in range(2)], 1))


class Chain:

    def __init__(self, eng, sem, base=0, turn=None, per=0):
        self.eng, self.sem, self.base, self.turn, self.per, self.n = eng, sem, base, turn, per, 0

    def value(self):
        return self.base + self.n + (0 if self.turn is None else self.turn * self.per)

    def __call__(self, ins):
        ins.then_inc(self.sem, 1)
        self.n += 1
        self.eng.wait_ge(self.sem, self.value())


def wait_turn(eng, sem, value, held, held_value):
    if not isinstance(value, int):
        value = eng.snap(eng.to_reg(value))
    eng.wait_ge(held, held_value)
    eng.wait_ge(sem, value)


def program(nc, a):
    with ExitStack() as ctx:
        def sb(name, shape, dt=F32):
            return ctx.enter_context(nc.sbuf_tensor(name, shape, dt))

        def sem(name):
            return ctx.enter_context(nc.semaphore(name))

        def dram(name, shape, dt=F32):
            return nc.dram_tensor(name, shape, dt, kind="Internal").ap()

        bank = ctx.enter_context(nc.psum_tensor("bank", [P, 8, 512], F32))

        slot = sb("slot", [P, 6, SLOT])
        const = sb("const", [P, C_ALL])
        xT = sb("xT", [P, KD, T])
        hnT = sb("hnT", [P, KD, T])
        yT = sb("yT", [P, KD, T])
        mod = sb("mod", [P, DEPTH, 6, KD, 2])
        gain = sb("gain", [P, 2 * DEPTH, KD, 2])
        norm_g = sb("norm_g", [P, 2 * DEPTH + 1, KD])
        ada_b = sb("ada_b", [P, DEPTH * 6 * KD])
        cond = sb("cond", [P, KD, 2])
        rs = sb("rs", [P, 2, T])
        ada_rows = sb("ada_rows", [2, 4, 512])
        head_g = sb("head_g", [P, DEPTH])
        conv_w = sb("conv_w", [P, H, 3, 3])
        w_gates = sb("w_gates", [P, DEPTH, KD, 2 * N_DIR * H])
        router = sb("router", [P, KD, E])
        router_b = sb("router_b", [P, E])
        row_bias = sb("row_bias", [N_DIR * H, 5])
        cols = sb("cols", [P, 4, NT, N_DIR * H])
        hcol = sb("hcol", [P, 4, NU])

        SCR = 11520
        scr = sb("scr", [P, SCR])
        at = [0]

        def take(n):
            lo = at[0]
            at[0] += n
            assert at[0] <= SCR, at[0]
            return scr[:, lo:lo + n]

        def dirs(x):
            return x.rearrange("p (d t) -> p d t", d=N_DIR)

        WORK_AT = 2 * N_DIR * T
        rows_b = take(2 * N_DIR * T).rearrange("p (q d t) -> p q d t", q=2, d=N_DIR)
        decay_b = take(N_DIR * T)
        qkv = take(3 * T).rearrange("p (s t) -> p s t", s=3)
        gate_z = take(T)
        square = take(2 * T).rearrange("p (s t) -> p s t", s=2)
        qdT = take(N_DIR * T)
        vb = take(NU * P)
        kbe = take(NU * P)
        kend = take(NU * P)
        EM = take(NU * P)
        AT = take(NU * P)
        vnew = take(NU * P)
        Sp = take(N_DIR * 2 * P).rearrange("p (d s e) -> p d s e", d=N_DIR, s=2)
        Ss = take(N_DIR * 4 * P).rearrange("p (d s e) -> p d s e", d=N_DIR, s=4)
        levT = slot[:, 4, 0:5 * NU * P].rearrange("p (l n) -> p l n", l=5)
        Dm = slot[:, 5, 0:NU * P]
        DT = slot[:, 5, NU * P:2 * NU * P]
        X = slot[:, 5, 2 * NU * P:3 * NU * P]
        nwT = slot[:, 5, 3 * NU * P:4 * NU * P]
        kbT = slot[:, 5, 4 * NU * P:5 * NU * P]
        LT = slot[:, 1, 0:NU * P]
        qnT = slot[:, 1, NU * P:NU * P + T]
        knT = slot[:, 1, NU * P + T:NU * P + 2 * T]
        tmpT = slot[:, 1, NU * P + 2 * T:NU * P + 3 * T]
        R = N_DIR * H
        work = [scr[0:R, WORK_AT + i * T:WORK_AT + (i + 1) * T] for i in range(20)]
        small = sb("small", [R, 8, NC])
        m_fin = sb("m_fin", [R, 3])

        rows_d = dram("rows_d", [DEPTH, 3, R, T])
        hn_d = [dram(f"hn_d{i}", [T, D]) for i in range(DEPTH)]
        list_d = [dram(f"list_d{i}", [N_PASSES * P, 2]) for i in range(DEPTH)]
        out_d = [dram(f"out_d{i}", [2 * T, D]) for i in range(DEPTH)]

        ident = const[:, C_ID:C_ID + P]
        ones = const[:, C_ONES:C_ONES + P]
        eps_col = const[:, C_EPS:C_EPS + 1]
        incl = const[:, C_INCL:C_INCL + N_DIR * P].rearrange("p (d i) -> p d i", d=N_DIR)

        def level_mask(lev):
            m = const[:, C_LEV + lev * N_DIR * P:C_LEV + (lev + 1) * N_DIR * P]
            return m.rearrange("p (d o i) -> p d o i", d=N_DIR, o=1)

        const_in = sem("const_in")
        cond_in = sem("cond_in")
        dve_step = sem("dve_step")
        ada_in = [sem(f"ada_in{i}") for i in range(6)]
        ada_rows_sb = sem("ada_rows_sb")
        ada_turned = sem("ada_turned")
        cond_ready = sem("cond_ready")
        ada_used = sem("ada_used")
        mod_ready = sem("mod_ready")
        sq_ready = sem("sq_ready")
        ss_ready = sem("ss_ready")
        rs_ready = sem("rs_ready")
        hn_scaled = sem("hn_scaled")
        hn_ready = sem("hn_ready")
        gate_mm = sem("gate_mm")
        gate_act = sem("gate_act")
        gate_dve = sem("gate_dve")
        rows_out = sem("rows_out")
        cols_mm = sem("cols_mm")
        cols_ready = sem("cols_ready")
        wout_in = sem("wout_in")
        delta_mm = sem("delta_mm")
        moved = sem("moved")
        stored = sem("stored")

        GROUP = 4
        mod_blocks = mod.rearrange("p l s (x j) c -> p (l s x) j c", j=4)
        ada_b_blocks = ada_b[:, :].rearrange("p (b j) -> p b j", j=4)
        ADA_SLOT = (0, 1, 2, 3, 4, 5, 2, 3)

        def ada_product(b, i, w, ks=range(KD)):
            w = w.rearrange("p (k n) -> p k n", k=KD)
            for k in ks:
                mm = nc.tensor.matmul(bank[32 * i:32 * i + 2, b, :], cond[:, k, :], w[:, k, :],
                                      start=(k == 0), stop=(k == KD - 1))
            return mm

        def ada_products_pe(pe, g):
            for i in range(GROUP):
                b = g * GROUP + i
                pe.wait_ge(ada_in[ADA_SLOT[b]], 32 if b >= 6 else 16)
                ada_product(4 + i, i, slot[:, ADA_SLOT[b], :]).then_inc(ada_used, 1)

        def ada_turn_pe(pe, g):
            for i in range(GROUP):
                pe.wait_ge(ada_rows_sb, g * GROUP + i + 1)
                for j in range(4):
                    mm = nc.tensor.transpose(bank[:, 3, (i * 4 + j) * 2:(i * 4 + j + 1) * 2],
                                             ada_rows[:, i, j * P:(j + 1) * P], ident[0:2, 0:2])
            mm.then_inc(ada_turned, 1)

        def ada_group_dve(dve, g):
            for i in range(GROUP):
                dve.wait_ge(ada_used, g * GROUP + i + 1)
                nc.vector.tensor_copy(ada_rows[:, i, :], bank[32 * i:32 * i + 2, 4 + i, :]).then_inc(ada_rows_sb, 1)
            dve.wait_ge(ada_turned, g + 1)
            bs = slice(g * GROUP, (g + 1) * GROUP)
            nc.vector.tensor_tensor(mod_blocks[:, bs], bank[:, 3, 0:GROUP * 8].rearrange("p (b j c) -> p b j c", b=GROUP, j=4),
                                    ada_b_blocks[:, bs].unsqueeze(3).to_broadcast([P, GROUP, 4, 2]),
                                    ALU.add).then_inc(mod_ready, 1)

        def gains_dve(step, norms):
            for n in norms:
                layer, sub = n // 2, n % 2
                step(nc.vector.tensor_scalar(gain[:, n], mod[:, layer, 3 * sub + 1], 1.0, None, ALU.add))
                step(nc.vector.tensor_tensor(gain[:, n], gain[:, n],
                                             norm_g[:, n, :].unsqueeze(2).to_broadcast([P, KD, 2]), ALU.mult))

        def block_norm_act(act, n):
            for k in range(KD):
                act.wait_ge(moved, MOVED_X if n == 0 else moved_after(n - 1) + 2 * (k + 1))
                nc.scalar.activation(hnT[:, k, :], xT[:, k, :], ACT.Square).then_inc(sq_ready, 1)
            act.wait_ge(ss_ready, n + 1)
            nc.scalar.activation(rs[:, 1, :], bank[:, 0, 0:T], ACT.Ln, bias=eps_col,
                                 scale=1.0 / D).then_inc(rs_ready, 1)
            act.wait_ge(rs_ready, 2 * n + 1)
            nc.scalar.activation(rs[:, 0, :], rs[:, 1, :], ACT.Exp, scale=-0.5).then_inc(rs_ready, 1)
            if n < 2 * DEPTH:
                layer, sub = n // 2, n % 2
                for k in range(KD):
                    act.wait_ge(hn_scaled, 2 * (n * KD + k + 1))
                    for g, lo, hi in SPANS:
                        nc.scalar.activation(hnT[:, k, lo:hi], hnT[:, k, lo:hi], ACT.Identity,
                                             bias=mod[:, layer, 3 * sub, k, g:g + 1]).then_inc(hn_ready, 1)

        def block_norm_pe(pe, n):
            for k in range(KD):
                pe.wait_ge(sq_ready, n * KD + k + 1)
                mm = nc.tensor.matmul(bank[:, 0, 0:T], ones, hnT[:, k, :], start=(k == 0), stop=(k == KD - 1))
            mm.then_inc(ss_ready, 1)

        def block_norm_dve(dve, n):
            dve.wait_ge(rs_ready, 2 * n + 2)
            for k in range(KD):
                for g, lo, hi in SPANS:
                    g_col = gain[:, n, k, g:g + 1] if n < 2 * DEPTH else norm_g[:, n, k:k + 1]
                    nc.vector.scalar_tensor_tensor(
                        out=hnT[:, k, lo:hi], in0=xT[:, k, lo:hi], scalar=g_col, in1=rs[:, 0, lo:hi],
                        op0=ALU.mult, op1=ALU.mult).then_inc(hn_scaled, 1)

        def residual_dve(dve, n):
            layer, sub = n // 2, n % 2
            for c in range(KD):
                dve.wait_ge(delta_mm, n * KD + c + 1)
                for g, lo, hi in SPANS:
                    nc.vector.scalar_tensor_tensor(
                        out=xT[:, c, lo:hi], in0=bank[:, c, lo:hi], scalar=mod[:, layer, 3 * sub + 2, c, g:g + 1],
                        in1=xT[:, c, lo:hi], op0=ALU.mult, op1=ALU.add).then_inc(moved, 1)

        MOVED_X = 1
        def moved_after(n):
            return MOVED_X + 2 * KD * n

        def chunks(x):
            return x.rearrange("p (c t) -> p c t", t=CHUNK)

        def last_of(x):
            return chunks(x)[:, :, CHUNK - 1], chunks(x)[:, :, 0]

        rowdir = [const[0:R, C_ROWDIR + d:C_ROWDIR + d + 1] for d in range(N_DIR)]
        reset = [const[0:R, C_RESET + d * T:C_RESET + (d + 1) * T] for d in range(N_DIR)]

        def choose(step, out, fwd, bwd, tmp):
            step(nc.vector.tensor_scalar(tmp, fwd, rowdir[0], None, ALU.mult))
            step(nc.vector.scalar_tensor_tensor(out=out, in0=bwd, scalar=rowdir[1], in1=tmp,
                                                op0=ALU.mult, op1=ALU.add))

        def chunk_sums(step, out, x, fwd, bwd, tmp):
            step(nc.vector.tensor_tensor_scan(fwd, reset[0], x, 0.0, ALU.mult, ALU.add))
            step(nc.vector.tensor_tensor_scan(bwd[:, ::-1], reset[1][:, ::-1], x[:, ::-1], 0.0, ALU.mult, ALU.add))
            choose(step, out, fwd, bwd, tmp)

        def gates_pe(pe, layer):
            pe.wait_ge(const_in, CONST_DMAS * 16)
            for half in range(2):
                for k in range(KD):
                    if half == 0:
                        pe.wait_ge(hn_ready, 2 * KD * 2 * layer + 2 * (k + 1))
                    mm = nc.tensor.matmul(bank[0:R, half, 0:T], w_gates[:, layer, k, half * R:(half + 1) * R],
                                          hnT[:, k, :], start=(k == 0), stop=(k == KD - 1))
            mm.then_inc(gate_mm, 1)

        def columns_pe(pe, sources, b):
            for q, row in enumerate(sources):
                for t in range(NT):
                    mm = nc.tensor.transpose(bank[:, b, (q * NT + t) * R:(q * NT + t + 1) * R],
                                             row[:, t * P:(t + 1) * P], ident[0:R, 0:R])
            mm.then_inc(cols_mm, 1)

        W = work
        def gdn_gates_act(act):
            act.wait_ge(gate_dve, 1)
            nc.scalar.activation(W[1], W[0], ACT.Abs).then_inc(gate_act, 1)
            act.wait_ge(gate_act, 1)
            nc.scalar.activation(W[1], W[1], ACT.Exp, scale=-1.0).then_inc(gate_act, 1)
            act.wait_ge(gate_act, 2)
            nc.scalar.activation(W[2], W[1], ACT.Ln, bias=ones[0:R, 0:1]).then_inc(gate_act, 1)
            nc.scalar.activation(row_bias[:, 4:5], row_bias[:, 0:1], ACT.Exp).then_inc(gate_act, 1)
            nc.scalar.activation(W[3], bank[0:R, 1, 0:T], ACT.Exp, scale=-1.0).then_inc(gate_act, 1)
            act.wait_ge(gate_dve, 2)
            nc.scalar.activation(W[10], W[7], ACT.Exp).then_inc(gate_act, 1)
            nc.scalar.activation(W[11], W[9], ACT.Exp).then_inc(gate_act, 1)
            act.wait_ge(cols_mm, 1)
            nc.scalar.activation(cols.rearrange("p q t r -> p (q t r)")[:, 0:4 * NT * R],
                                 bank[:, 2, 0:4 * NT * R], ACT.Copy).then_inc(cols_ready, 1)

        def gdn_gates_dve(dve, step):
            dve.wait_ge(gate_mm, 1)
            nc.vector.tensor_scalar(W[0], bank[0:R, 0, 0:T], row_bias[:, 1:2], None, ALU.add).then_inc(gate_dve, 1)
            dve.wait_ge(gate_dve, 1)
            step(nc.vector.tensor_scalar(W[4], W[0], 0.0, None, ALU.max))
            dve.wait_ge(gate_act, 5)
            step(nc.vector.tensor_tensor(W[4], W[4], W[2], ALU.add))
            step(nc.vector.tensor_scalar(W[4], W[4], row_bias[:, 4:5], -1.0, ALU.mult, ALU.mult))
            step(nc.vector.tensor_scalar(W[8], W[3], 1.0, None, ALU.add))
            step(nc.vector.reciprocal(W[8], W[8]))
            chunk_sums(step, W[7], W[4], W[5], W[6], W[0])
            g_last, g_first = last_of(W[7])
            choose(step, small[:, 0, :], g_last, g_first, small[:, 1, :])
            nc.vector.tensor_tensor(chunks(W[9]), small[:, 0, :].unsqueeze(2).to_broadcast([R, NC, CHUNK]),
                                    chunks(W[7]), ALU.subtract).then_inc(gate_dve, 1)
            dve.wait_ge(gate_act, 7)
            nc.vector.tensor_tensor(W[12], W[8], W[10], ALU.mult).then_inc(gate_dve, 1)

        def mlstm_gates_act(act):
            act.wait_ge(gate_dve, G0 + 1)
            nc.scalar.activation(W[2], W[1], ACT.Abs).then_inc(gate_act, 1)
            act.wait_ge(gate_act, A0 + 1)
            nc.scalar.activation(W[2], W[2], ACT.Exp, scale=-1.0).then_inc(gate_act, 1)
            act.wait_ge(gate_act, A0 + 2)
            nc.scalar.activation(W[3], W[2], ACT.Ln, bias=ones[0:R, 0:1]).then_inc(gate_act, 1)
            act.wait_ge(gate_dve, G0 + 2)
            nc.scalar.activation(W[15], W[12], ACT.Exp).then_inc(gate_act, 1)
            nc.scalar.activation(W[16], W[13], ACT.Exp, scale=-1.0).then_inc(gate_act, 1)
            nc.scalar.activation(W[17], W[14], ACT.Exp).then_inc(gate_act, 1)
            act.wait_ge(cols_mm, 2)
            nc.scalar.activation(cols.rearrange("p q t r -> p (q t r)")[:, 0:2 * NT * R],
                                 bank[:, 7, 0:2 * NT * R], ACT.Copy).then_inc(cols_ready, 1)

        A0, G0 = 7, 3

        def mlstm_gates_dve(dve, step):
            dve.wait_ge(gate_mm, 2)
            step(nc.vector.tensor_scalar(W[0], bank[0:R, 0, 0:T], row_bias[:, 2:3], None, ALU.add))
            nc.vector.tensor_scalar(W[1], bank[0:R, 1, 0:T], row_bias[:, 3:4], None, ALU.add).then_inc(gate_dve, 1)
            dve.wait_ge(gate_dve, G0 + 1)
            dve.wait_ge(gate_act, A0 + 3)
            step(nc.vector.scalar_tensor_tensor(out=W[4], in0=W[1], scalar=0.0, in1=W[3],
                                                op0=ALU.min, op1=ALU.subtract))
            chunk_sums(step, W[7], W[4], W[5], W[6], W[8])
            step(nc.vector.tensor_tensor(W[8], W[0], W[7], ALU.subtract))
            starts = ({0: 0, 2: 1}, {1: 0, 5: 1})
            order = ((0, 1, 2, 3, 4, 5), (1, 0, 5, 4, 3, 2))
            b_last = last_of(W[7])
            for d in range(N_DIR):
                run, carried = W[9 + d], small[:, 2 + d, :]
                r_last = last_of(run)[d]
                for n, c in enumerate(order[d]):
                    if c in starts[d]:
                        step(nc.vector.tensor_copy(carried[:, c:c + 1], m_fin[:, starts[d][c]:starts[d][c] + 1]))
                    cs = slice(c * CHUNK, (c + 1) * CHUNK)
                    flip = (lambda v: v) if d == 0 else (lambda v: v[:, ::-1])
                    step(nc.vector.tensor_tensor_scan(flip(run[:, cs]), flip(W[8][:, cs]), flip(W[8][:, cs]),
                                                      carried[:, c:c + 1], ALU.max, ALU.max))
                    if n == 1:
                        to = small[:, 4 + d, 0:1]
                    elif n < NC - 1:
                        to = carried[:, order[d][n + 1]:order[d][n + 1] + 1]
                    else:
                        continue
                    step(nc.vector.tensor_tensor(to, r_last[:, c:c + 1], b_last[d][:, c:c + 1], ALU.add))
            choose(step, W[11], W[9], W[10], W[12])
            choose(step, small[:, 6, :], small[:, 2, :], small[:, 3, :], small[:, 7, :])
            choose(step, m_fin[:, 2:3], small[:, 4, 0:1], small[:, 5, 0:1], small[:, 7, 0:1])
            m_last, m_first = last_of(W[11])
            choose(step, small[:, 0, :], m_last, m_first, small[:, 1, :])
            step(nc.vector.tensor_tensor(chunks(W[12]), small[:, 6, :].unsqueeze(2).to_broadcast([R, NC, CHUNK]),
                                         chunks(W[11]), ALU.subtract))
            step(nc.vector.tensor_tensor(W[13], W[7], W[11], ALU.add))
            nc.vector.tensor_tensor(chunks(W[14]), chunks(W[8]),
                                    small[:, 0, :].unsqueeze(2).to_broadcast([R, NC, CHUNK]),
                                    ALU.subtract).then_inc(gate_dve, 1)

        g_w = sem("g_w")
        g_rows = sem("g_rows")
        g_state = sem("g_state")
        g_proj = sem("g_proj")
        g_mid = sem("g_mid")
        g_conv = sem("g_conv")
        g_silu = sem("g_silu")
        g_sq = sem("g_sq")
        g_ss = sem("g_ss")
        g_rs = sem("g_rs")
        g_qk = sem("g_qk")
        g_kb = sem("g_kb")
        g_col = sem("g_col")
        g_arg = sem("g_arg")
        g_exp = sem("g_exp")
        g_em = sem("g_em")
        g_lt = sem("g_lt")
        g_lev = sem("g_lev")
        g_at = sem("g_at")
        g_qd = sem("g_qd")
        g_tr = sem("g_tr")
        g_kk = sem("g_kk")
        g_tok = sem("g_tok")
        g_inv = sem("g_inv")
        g_ips = sem("g_ips")
        g_x = sem("g_x")
        g_wps = sem("g_wps")
        g_w2 = sem("g_w2")
        g_vps = sem("g_vps")
        g_vsb = sem("g_vsb")
        g_sps = sem("g_sps")
        g_ssb = sem("g_ssb")
        g_o = sem("g_o")
        g_ors = sem("g_ors")
        g_y = sem("g_y")
        g_dve = sem("g_dve")
        g_ada_in = [sem(f"g_ada_in{i}") for i in range(2)]
        g_ada = sem("g_ada")
        g_ada_sb = sem("g_ada_sb")
        g_ada_tr = sem("g_ada_tr")
        g_mod = sem("g_mod")

        CHAINS = (("s", 0, (2, 3, 4, 5)), ("s", 1, (5, 4, 3, 2)), ("p", 0, (0, 1)), ("p", 1, (1, 0)))
        CHAIN_BANK = (0, 1, 6, 7)

        def state_of(ch, j):
            kind, d, _ = CHAINS[ch]
            if kind == "s":
                return Ss[:, d, j, :]
            return None if j == 0 else Sp[:, d, j - 1, :]

        def steps():
            v = s = 0
            for j in range(4):
                for ch, (_, _, cs) in enumerate(CHAINS):
                    if j < len(cs):
                        updates = CHAINS[ch][0] == "p" or j < 3
                        yield ch, j, v, s if updates else None
                        v += 1
                        s += updates

        STEPS = list(steps())
        STATE_AT = {(ch, j): s for ch, j, _, s in STEPS}

        GDN_DVE = 4

        def gdn_pe(pe):
            with pe.Fori(0, H) as h:
                pe.wait_ge(g_w, h * 16 + 16)
                for s in range(4):
                    if s == 2:
                        pe.wait_ge(g_y, h * 2 + 2)
                    for k in range(KD):
                        mm = nc.tensor.matmul(bank[:, s, 0:T], slot[:, 0, (k * 4 + s) * P:(k * 4 + s + 1) * P],
                                              hnT[:, k, :], start=(k == 0), stop=(k == KD - 1))
                    mm.then_inc(g_proj, 1)
                    if s == 2:
                        for i in range(2):
                            pe.wait_ge(g_sq, h * 2 + i + 1)
                            nc.tensor.matmul(bank[:, i, 0:T], ones, square[:, i, :], start=True,
                                             stop=True).then_inc(g_ss, 1)
                pe.wait_ge(g_qk, h * 2 + 2)
                for t in range(NT):
                    mm = nc.tensor.transpose(bank[:, 5, t * P:(t + 1) * P], knT[:, t * P:(t + 1) * P], ident)
                mm.then_inc(g_tr, 1)
                pe.wait_ge(g_kb, h + 1)
                for u in range(NU):
                    t = u % NT
                    mm = nc.tensor.matmul(bank[:, 6 + u // NT, t * P:(t + 1) * P], knT[:, t * P:(t + 1) * P],
                                          kbT[:, u * P:(u + 1) * P], start=True, stop=True)
                mm.then_inc(g_kk, 1)
                pe.wait_ge(g_silu, h * 4 + 4)
                for t in range(NT):
                    mm = nc.tensor.transpose(bank[:, 4, t * P:(t + 1) * P], qkv[:, 2, t * P:(t + 1) * P], ident)
                mm.then_inc(g_tr, 1)
                for t in range(NT):
                    mm = nc.tensor.matmul(bank[:, 2, t * P:(t + 1) * P], knT[:, t * P:(t + 1) * P],
                                          qnT[:, t * P:(t + 1) * P], start=True, stop=True)
                mm.then_inc(g_kk, 1)
                for i in range(2):
                    pe.wait_ge(g_ada_in[i], h * 16 + 16)
                for k in range(KD):
                    for i in range(2):
                        mm = ada_product(3, i, slot[:, 2 + i, :], (k,))
                        if k == KD - 1:
                            mm.then_inc(g_ada, 1)
                pe.wait_ge(g_tok, h + 1)
                pe.wait_ge(g_inv, h * 14 + 2)
                for g in range(N_DIR):
                    for t in range(NT):
                        u = g * NT + t
                        mm = nc.tensor.transpose(bank[:, 4 + g, t * P:(t + 1) * P], DT[:, u * P:(u + 1) * P], ident)
                    mm.then_inc(g_ips, 1)
                for lev in range(1, LEVELS):
                    pe.wait_ge(g_lev, h * 5 + lev)
                    for g in range(N_DIR):
                        pe.wait_ge(g_inv, h * 14 + 2 * lev + g + 1)
                        for t in range(NT):
                            us = slice((g * NT + t) * P, (g * NT + t + 1) * P)
                            mm = nc.tensor.matmul(bank[:, g, t * P:(t + 1) * P], levT[:, lev - 1, us], Dm[:, us],
                                                  start=True, stop=True)
                        mm.then_inc(g_ips, 1)
                    for g in range(N_DIR):
                        pe.wait_ge(g_x, h * 10 + 2 * (lev - 1) + g + 1)
                        for t in range(NT):
                            us = slice((g * NT + t) * P, (g * NT + t + 1) * P)
                            if lev < LEVELS - 1:
                                nc.tensor.matmul(bank[:, 4 + g, t * P:(t + 1) * P], DT[:, us], X[:, us],
                                                 start=True, stop=True)
                            mm = nc.tensor.matmul(bank[:, 6 + g, t * P:(t + 1) * P], X[:, us], DT[:, us],
                                                  start=True, stop=True)
                        mm.then_inc(g_ips, 1)
                    if lev == LEVELS - 2:
                        wait_turn(pe, g_ada_sb, h * 2 + 2, mod_ready, 2)
                        for i in range(2):
                            for j in range(4):
                                mm = nc.tensor.transpose(bank[:, 3, (i * 4 + j) * 2:(i * 4 + j + 1) * 2],
                                                         ada_rows[:, i, j * P:(j + 1) * P], ident[0:2, 0:2])
                        mm.then_inc(g_ada_tr, 1)
                for g in range(N_DIR):
                    pe.wait_ge(g_inv, h * 14 + 12 + g + 1)
                    for t in range(NT):
                        us = slice((g * NT + t) * P, (g * NT + t + 1) * P)
                        mm = nc.tensor.matmul(bank[:, 4 + g, t * P:(t + 1) * P], kbe[:, us], DT[:, us],
                                              start=True, stop=True)
                    mm.then_inc(g_wps, 1)
                pe.wait_ge(g_w2, h * 2 + 2)
                pe.wait_ge(g_state, h * 16 + 16)
                pe.wait_ge(g_at, h + 1)
                pe.wait_ge(g_qd, h + 1)
                first = [True]

                def into_output(lhsT, rhs, lo, hi):
                    mm = nc.tensor.matmul(bank[:, 2, lo:hi], lhsT, rhs, start=first[0], stop=False,
                                          skip_group_check=True)
                    first[0] = False
                    return mm

                for j in range(4):
                    now = [x for x in STEPS if x[1] == j]
                    for ch, _, v, _ in now:
                        _, d, cs = CHAINS[ch]
                        c = cs[j]
                        u, r = d * NT + c // 2, (c % 2) * CHUNK
                        S = state_of(ch, j)
                        if j > 0:
                            pe.wait_ge(g_ssb, h * 10 + STATE_AT[(ch, j - 1)] + 1)
                        out = bank[r:r + CHUNK, CHAIN_BANK[ch], 0:P]
                        mm = nc.tensor.matmul(out, DT[:, u * P + r:u * P + r + CHUNK], vb[:, u * P:(u + 1) * P],
                                              start=True, stop=S is None)
                        if S is not None:
                            mm = nc.tensor.matmul(out, nwT[:, u * P + r:u * P + r + CHUNK], S, start=False, stop=True)
                        mm.then_inc(g_vps, 1)
                    for ch, _, v, s in now:
                        _, d, cs = CHAINS[ch]
                        c = cs[j]
                        u, r = d * NT + c // 2, (c % 2) * CHUNK
                        S = state_of(ch, j)
                        pe.wait_ge(g_vsb, h * 12 + v + 1)
                        if s is not None:
                            nc.tensor.matmul(bank[:, CHAIN_BANK[ch], P:2 * P], kend[r:r + CHUNK, u * P:(u + 1) * P],
                                             vnew[r:r + CHUNK, u * P:(u + 1) * P], start=True,
                                             stop=True).then_inc(g_sps, 1)
                    for ch, _, v, s in now:
                        _, d, cs = CHAINS[ch]
                        c = cs[j]
                        u = d * NT + c // 2
                        S = state_of(ch, j)
                        if S is not None:
                            mm = into_output(S, qdT[:, d * T + c * CHUNK:d * T + (c + 1) * CHUNK], c * CHUNK, (c + 1) * CHUNK)
                        if j % 2 == 1:
                            mm = into_output(vnew[:, u * P:(u + 1) * P], AT[:, u * P:(u + 1) * P],
                                             (c // 2) * P, (c // 2 + 1) * P)
                mm.then_inc(g_o, 1)
                pe.wait_ge(g_mod, h + 1)
                pe.wait_ge(g_ors, h * 3 + 1)
                nc.tensor.matmul(bank[:, 3, 0:T], ones, square[:, 0, :], start=True, stop=True).then_inc(g_o, 1)
                pe.wait_ge(g_ssb, h * 10 + 10)

        def gdn_act(act):
            with act.Fori(0, H) as h:
                for s in range(3):
                    act.wait_ge(g_proj, h * 4 + s + 1)
                    nc.scalar.activation(qkv[:, s, :], bank[:, s, 0:T], ACT.Identity,
                                         scale=conv_w[:, bass.ds(h, 1), 1, s]).then_inc(g_mid, 1)
                    if s == 0:
                        act.wait_ge(cols_ready, 1)
                        nc.scalar.activation(
                            hcol[:, :, :].rearrange("p q (d t) -> p q t d", d=N_DIR),
                            cols[:, :, :, :].rearrange("p q t (d h) -> p q t d h", h=H)[:, :, :, :, bass.ds(h, 1)]
                            .rearrange("p q t d h -> p q t (d h)"), ACT.Copy).then_inc(g_col, 1)
                    if s < 2:
                        act.wait_ge(g_conv, h * 3 + s + 1)
                        nc.scalar.activation(qkv[:, s, :], qkv[:, s, :], ACT.Silu).then_inc(g_silu, 1)
                        act.wait_ge(g_silu, h * 4 + s + 1)
                        nc.scalar.activation(square[:, s, :], qkv[:, s, :], ACT.Square).then_inc(g_sq, 1)
                for s in range(2):
                    act.wait_ge(g_ss, h * 2 + s + 1)
                    nc.scalar.activation(rs[:, s, :], bank[:, s, 0:T], ACT.Ln, bias=eps_col).then_inc(g_rs, 1)
                for s in range(2):
                    act.wait_ge(g_rs, h * 4 + 1 + s)
                    nc.scalar.activation(rs[:, s, :], rs[:, s, :], ACT.Exp, scale=-0.5).then_inc(g_rs, 1)
                act.wait_ge(g_rows, h * 32 + 32)
                nc.scalar.activation(dirs(decay_b), rows_b[:, 0, :, :], ACT.Exp).then_inc(g_col, 1)
                act.wait_ge(g_arg, h * 2 + 2)
                nc.scalar.activation(EM, EM, ACT.Exp).then_inc(g_exp, 1)
                act.wait_ge(g_conv, h * 3 + 3)
                nc.scalar.activation(qkv[:, 2, :], qkv[:, 2, :], ACT.Silu).then_inc(g_silu, 1)
                act.wait_ge(g_proj, h * 4 + 4)
                nc.scalar.activation(gate_z, bank[:, 3, 0:T], ACT.Silu).then_inc(g_silu, 1)
                for g in range(N_DIR):
                    act.wait_ge(g_ips, h * 22 + g + 1)
                    nc.scalar.activation(Dm[:, g * T:(g + 1) * T], bank[:, 4 + g, 0:T], ACT.Copy).then_inc(g_inv, 1)
                for lev in range(1, LEVELS):
                    for g in range(N_DIR):
                        act.wait_ge(g_ips, h * 22 + 2 + 4 * (lev - 1) + g + 1)
                        nc.scalar.activation(X[:, g * T:(g + 1) * T], bank[:, g, 0:T], ACT.Copy).then_inc(g_x, 1)
                    if lev in (1, 2):
                        i = lev - 1
                        act.wait_ge(g_ada, h * 2 + 2)
                        nc.scalar.activation(ada_rows[:, i, :], bank[32 * i:32 * i + 2, 3, :], ACT.Copy).then_inc(g_ada_sb, 1)
                for g in range(N_DIR):
                    act.wait_ge(g_wps, h * 2 + g + 1)
                    nc.scalar.activation(nwT[:, g * T:(g + 1) * T], bank[:, 4 + g, 0:T], ACT.Copy,
                                         scale=-1.0).then_inc(g_w2, 1)
                for ch, j, v, _ in STEPS:
                    _, d, cs = CHAINS[ch]
                    c = cs[j]
                    u, r = d * NT + c // 2, (c % 2) * CHUNK
                    act.wait_ge(g_vps, h * 12 + v + 1)
                    nc.scalar.activation(vnew[r:r + CHUNK, u * P:(u + 1) * P], bank[r:r + CHUNK, CHAIN_BANK[ch], 0:P],
                                         ACT.Copy).then_inc(g_vsb, 1)
                act.wait_ge(g_o, h * 2 + 1)
                nc.scalar.activation(square[:, 0, :], bank[:, 2, 0:T], ACT.Square).then_inc(g_ors, 1)
                act.wait_ge(g_o, h * 2 + 2)
                nc.scalar.activation(rs[:, 0, :], bank[:, 3, 0:T], ACT.Ln, bias=eps_col,
                                     scale=1.0 / P).then_inc(g_ors, 1)
                act.wait_ge(g_ors, h * 3 + 2)
                nc.scalar.activation(rs[:, 0, :], rs[:, 0, :], ACT.Exp, scale=-0.5).then_inc(g_ors, 1)

        def gdn_dve(dve):
            with dve.Fori(0, H) as h:
                step = Chain(dve, g_dve, turn=h, per=GDN_DVE)
                for s in range(3):
                    dve.wait_ge(g_mid, h * 3 + s + 1)

                    def tap(lo, hi, shift, w):
                        return nc.vector.scalar_tensor_tensor(
                            out=qkv[:, s, lo:hi], in0=bank[:, s, lo + shift:hi + shift],
                            scalar=conv_w[:, bass.ds(h, 1), w, s], in1=qkv[:, s, lo:hi],
                            op0=ALU.mult, op1=ALU.add)

                    tap(1, T_PROMPT, -1, 0)
                    step(tap(T_PROMPT + 1, T, -1, 0))
                    tap(0, T_PROMPT - 1, 1, 2)
                    tap(T_PROMPT, T - 1, 1, 2).then_inc(g_conv, 1)
                dve.wait_ge(g_rs, h * 4 + 3)
                nc.vector.scalar_tensor_tensor(out=qnT, in0=qkv[:, 0, :], scalar=float(P) ** -0.5, in1=rs[:, 0, :],
                                               op0=ALU.mult, op1=ALU.mult).then_inc(g_qk, 1)
                dve.wait_ge(g_rs, h * 4 + 4)
                nc.vector.tensor_tensor(knT, qkv[:, 1, :], rs[:, 1, :], ALU.mult).then_inc(g_qk, 1)
                dve.wait_ge(g_qk, h * 2 + 2)
                dve.wait_ge(g_rows, h * 32 + 32)
                nc.vector.tensor_tensor(dirs(kbT), knT.unsqueeze(1).to_broadcast([P, N_DIR, T]), rows_b[:, 1, :, :],
                                        ALU.mult).then_inc(g_kb, 1)
                dve.wait_ge(g_em, h + 1)
                dve.wait_ge(g_kk, h * 2 + 1)
                nc.vector.tensor_tensor(dirs(LT), bank[:, 6:8, 0:T], dirs(EM), ALU.mult).then_inc(g_lt, 1)
                dve.wait_ge(g_lt, h + 1)
                step(nc.vector.tensor_tensor(
                    DT.rearrange("p (d t i) -> p d t i", d=N_DIR, t=NT),
                    LT.rearrange("p (d t i) -> p d t i", d=N_DIR, t=NT),
                    level_mask(0).to_broadcast([P, N_DIR, NT, P]), ALU.mult))
                for g in range(N_DIR):
                    v3 = DT[:, g * T:(g + 1) * T].rearrange("p (t i) -> p t i", t=NT)
                    nc.vector.scalar_tensor_tensor(out=v3, in0=v3, scalar=-1.0,
                                                   in1=ident.unsqueeze(1).to_broadcast([P, NT, P]),
                                                   op0=ALU.mult, op1=ALU.add).then_inc(g_inv, 1)
                dve.wait_ge(g_col, h * 2 + 2)
                dve.wait_ge(g_tr, h * 2 + 2)

                def by_column(out, b, q):
                    src = bank[:, b, 0:T].rearrange("p (o t i) -> p o t i", o=1, t=NT)
                    return nc.vector.tensor_tensor(
                        out.rearrange("p (d t i) -> p d t i", d=N_DIR, t=NT), src.to_broadcast([P, N_DIR, NT, P]),
                        hcol[:, q, :].rearrange("p (d t o) -> p d t o", d=N_DIR, o=1).to_broadcast([P, N_DIR, NT, P]),
                        ALU.mult)

                by_column(vb, 4, 1)
                by_column(kbe, 5, 2)
                by_column(kend, 5, 3).then_inc(g_tok, 1)
                dve.wait_ge(g_kk, h * 2 + 2)
                nc.vector.tensor_tensor(dirs(AT), bank[:, 2, 0:T].unsqueeze(1).to_broadcast([P, N_DIR, T]), dirs(EM),
                                        ALU.mult).then_inc(g_at, 1)
                for lev in range(1, LEVELS):
                    for g in range(N_DIR):
                        gs = slice(g * T, (g + 1) * T)
                        dve.wait_ge(g_ips, h * 22 + 2 + 4 * (lev - 1) + 2 + g + 1)
                        if lev < LEVELS - 1:
                            nc.vector.tensor_tensor(Dm[:, gs], Dm[:, gs], bank[:, 4 + g, 0:T], ALU.subtract)
                        nc.vector.tensor_tensor(DT[:, gs], DT[:, gs], bank[:, 6 + g, 0:T],
                                                ALU.subtract).then_inc(g_inv, 1)
                dve.wait_ge(g_ada_tr, h + 1)
                bs = bass.ds(h * 2 + 2 * GROUP, 2)
                nc.vector.tensor_tensor(mod_blocks[:, bs], bank[:, 3, 0:16].rearrange("p (b j c) -> p b j c", b=2, j=4),
                                        ada_b_blocks[:, bs].unsqueeze(3).to_broadcast([P, 2, 4, 2]),
                                        ALU.add).then_inc(g_mod, 1)
                for ch, j, _, s in STEPS:
                    if s is None:
                        continue
                    kind, d, cs = CHAINS[ch]
                    c = cs[j]
                    end = d * T + (c * CHUNK + CHUNK - 1 if d == 0 else c * CHUNK)
                    new = Ss[:, d, j + 1, :] if kind == "s" else Sp[:, d, j, :]
                    dve.wait_ge(g_sps, h * 10 + s + 1)
                    src = bank[:, CHAIN_BANK[ch], P:2 * P]
                    old = state_of(ch, j)
                    if old is None:
                        nc.vector.tensor_copy(new, src).then_inc(g_ssb, 1)
                    else:
                        if j == 0:
                            dve.wait_ge(g_state, h * 16 + 16)
                        else:
                            dve.wait_ge(g_ssb, h * 10 + STATE_AT[(ch, j - 1)] + 1)
                        nc.vector.scalar_tensor_tensor(out=new, in0=old, scalar=decay_b[:, end:end + 1], in1=src,
                                                       op0=ALU.mult, op1=ALU.add).then_inc(g_ssb, 1)
                dve.wait_ge(g_ors, h * 3 + 3)
                nc.vector.scalar_tensor_tensor(out=tmpT, in0=bank[:, 2, 0:T], scalar=head_g[:, 0:1], in1=rs[:, 0, :],
                                               op0=ALU.mult, op1=ALU.mult).then_inc(g_y, 1)
                dve.wait_ge(g_y, h * 2 + 3)
                nc.vector.tensor_tensor(yT[:, bass.ds(h, 1), :].rearrange("p a t -> p (a t)"), tmpT, gate_z,
                                        ALU.mult).then_inc(g_y, 1)
                dve.wait_ge(g_stored, h * 16 + 16)
                dve.wait_ge(g_y, h * 2 + 4)
                assert step.n == GDN_DVE

        g_stored = sem("g_stored")

        def gdn_pool(pool):
            with pool.Fori(0, H) as h:
                pool.wait_ge(g_col, h * 2 + 1)
                pool.wait_ge(g_rows, h * 32 + 32)
                em4 = EM.rearrange("p (d t i) -> p d t i", d=N_DIR, t=NT)
                nc.gpsimd.tensor_tensor(em4, rows_b[:, 0, :, :].rearrange("p d (t i) -> p d t i", t=NT),
                                        hcol[:, 0, :].rearrange("p (d t o) -> p d t o", d=N_DIR, o=1)
                                        .to_broadcast([P, N_DIR, NT, P]), ALU.subtract).then_inc(g_arg, 1)
                wait_turn(pool, g_arg, h * 2 + 1, const_in, 16 * CONST_DMAS)
                nc.gpsimd.tensor_scalar(EM, EM, 0.0, None, ALU.min).then_inc(g_arg, 1)
                pool.wait_ge(g_exp, h + 1)
                nc.gpsimd.tensor_tensor(em4, em4, incl.rearrange("p d (o i) -> p d o i", o=1)
                                        .to_broadcast([P, N_DIR, NT, P]), ALU.mult).then_inc(g_em, 1)
                pool.wait_ge(g_lt, h + 1)
                for lev in range(1, LEVELS):
                    nc.gpsimd.tensor_tensor(
                        levT[:, lev - 1, :].rearrange("p (d t i) -> p d t i", d=N_DIR, t=NT),
                        LT.rearrange("p (d t i) -> p d t i", d=N_DIR, t=NT),
                        level_mask(lev).to_broadcast([P, N_DIR, NT, P]), ALU.mult).then_inc(g_lev, 1)
                pool.wait_ge(g_col, h * 2 + 2)
                nc.gpsimd.tensor_tensor(dirs(qdT), qnT.unsqueeze(1).to_broadcast([P, N_DIR, T]), dirs(decay_b),
                                        ALU.mult).then_inc(g_qd, 1)

        def gdn_sync(sp):
            def weights(h):
                sp.dma_start(slot[:, 0, :], a["gdn_w"][bass.ds(h, 1), :, :].rearrange("a p n -> p (a n)")).then_inc(g_w, 16)

            def modulations(b, i):
                sp.dma_start(slot[:, 2 + i, :], a["ada_w"][bass.ds(b, 1)].rearrange("a p n -> (a p) n"))\
                    .then_inc(g_ada_in[i], 16)

            def rows_and_states(h):
                for q in range(2):
                    src = rows_d[0, q].rearrange("(d h) t -> h d t", d=N_DIR)[bass.ds(h, 1), :, :]
                    sp.dma_start(rows_b[:, q, :, :], src.to_broadcast([P, N_DIR, T])).then_inc(g_rows, 16)
                src = a["gdn_S"].rearrange("(d h) k v -> h k d v", d=N_DIR)[bass.ds(h, 1)]
                sp.dma_start(Ss[:, :, 0, :], src.rearrange("a k d v -> (a k) d v")).then_inc(g_state, 16)

            def store(h):
                wait_turn(sp, g_ssb, h * 10 + 10, rows_out, 32)
                dst = a["o_S"].rearrange("(d h) k v -> h k d v", d=N_DIR)[bass.ds(h, 1)]
                sp.dma_start(dst.rearrange("a k d v -> (a k) d v"), Sp[:, :, 1, :]).then_inc(g_stored, 16)

            sp.wait_ge(rows_out, 32)
            rows_and_states(0)
            for i in range(2):
                sp.wait_ge(ada_used, 7 + i)
                modulations(2 * GROUP + i, i)
            with sp.Fori(0, H - 1) as h:
                wait_turn(sp, g_proj, h * 4 + 4, rows_out, 32)
                weights(h + 1)
                for i in range(2):
                    wait_turn(sp, g_ada, h * 2 + 1 + i, rows_out, 32)
                    modulations(h * 2 + 2 * GROUP + 2 + i, i)
                store(h)
                wait_turn(sp, g_o, h * 2 + 1, rows_out, 32)
                wait_turn(sp, g_em, h + 1, rows_out, 32)
                wait_turn(sp, g_kb, h + 1, rows_out, 32)
                rows_and_states(h + 1)
            sp.wait_ge(g_ada, 2 * H)
            wout_sync(sp, 0)
            store(H - 1)

        def wout_sync(sp, layer):
            sp.dma_start(slot[:, 2:4, :], a["w_out"][layer].rearrange("p (s n) -> p s n", s=2)).then_inc(wout_in, 16)

        def wout_part(layer, c, heads):
            w = slot[:, 2:4, :].rearrange("p s n -> p (s n)").rearrange("p (h n) -> p h n", h=H)
            for h in heads:
                mm = nc.tensor.matmul(bank[:, c, 0:T], w[:, h, c * P:(c + 1) * P], yT[:, h, :],
                                      start=(h == 0), stop=(h == H - 1), skip_group_check=True)
            return mm

        def wout_begin(pe, layer, cs):
            pe.wait_ge(wout_in, 16 * (layer + 1))
            for c in cs:
                wout_part(layer, c, range(H - 1))

        def wout_end(pe, layer, begun):
            for c in range(KD):
                wout_part(layer, c, range(H - 1 if c in begun else 0, H)).then_inc(delta_mm, 1)

        m_w = sem("m_w")
        m_rows = sem("m_rows")
        m_state = sem("m_state")
        m_proj = sem("m_proj")
        m_ev = sem("m_ev")
        m_tr = sem("m_tr")
        m_qk = sem("m_qk")
        m_v = sem("m_v")
        m_col = sem("m_col")
        m_arg = sem("m_arg")
        m_exp = sem("m_exp")
        m_em = sem("m_em")
        m_pt = sem("m_pt")
        m_qd = sem("m_qd")
        m_kw = sem("m_kw")
        m_sps = sem("m_sps")
        m_ssb = sem("m_ssb")
        m_nd = sem("m_nd")
        m_abs = sem("m_abs")
        m_h = sem("m_h")
        m_sq = sem("m_sq")
        m_ss = sem("m_ss")
        m_rs = sem("m_rs")
        m_y = sem("m_y")
        m_dve = sem("m_dve")
        m_stored = sem("m_stored")

        A1 = P + 1
        VA = P + 4
        at[0] = 0
        mrows = take(3 * N_DIR * T).rearrange("p (q d t) -> p q d t", q=3, d=N_DIR)
        mqT = take(T)
        mkT = take(T)
        mvT = take(T)
        og = take(T)
        v_aug = take(NT * VA).rearrange("p (t e) -> p t e", t=NT)
        mEM = take(NU * P)
        PT = take(NU * P)
        mqd = take(N_DIR * T)
        kw = take(NU * P)
        hd = take(N_DIR * T)
        den = take(N_DIR * T)
        hs = take(T)
        msq = take(T)
        Cp = take(N_DIR * 2 * VA).rearrange("p (d s e) -> p d s e", d=N_DIR, s=2)
        Cs = take(N_DIR * 4 * VA).rearrange("p (d s e) -> p d s e", d=N_DIR, s=4)

        def cell_of(ch, j):
            kind, d, _ = CHAINS[ch]
            if kind == "s":
                return Cs[:, d, j, :]
            return None if j == 0 else Cp[:, d, j - 1, :]

        MCH = [(ch, j, s) for ch, j, _, s in STEPS]
        MLSTM_DVE = 5

        def mlstm_pe(pe, begun):
            def project(h, before=None):
                pe.wait_ge(m_w, h * 16 + 16)
                for s in range(4):
                    for k in range(KD):
                        mm = nc.tensor.matmul(bank[:, s, 0:T], slot[:, 0, (k * 4 + s) * P:(k * 4 + s + 1) * P],
                                              hnT[:, k, :], start=(k == 0), stop=(k == KD - 1))
                    mm.then_inc(m_proj, 1)
                    if s == 2 and before is not None:
                        squares_sum(before)

            def states(h):
                pe.wait_ge(m_ev, h * 4 + 3)
                for b, src in ((4, mkT), (5, mvT)):
                    for t in range(NT):
                        mm = nc.tensor.transpose(bank[:, b, t * P:(t + 1) * P], src[:, t * P:(t + 1) * P], ident)
                    mm.then_inc(m_tr, 1)
                for t in range(NT):
                    mm = nc.tensor.matmul(bank[:, 6, t * P:(t + 1) * P], mkT[:, t * P:(t + 1) * P],
                                          mqT[:, t * P:(t + 1) * P], start=True, stop=True)
                mm.then_inc(m_qk, 1)
                pe.wait_ge(m_kw, h + 1)
                pe.wait_ge(m_v, h + 1)
                pe.wait_ge(m_ones, 1)
                pe.wait_ge(m_ev, h * 4 + 4)
                for ch, j, s in MCH:
                    if s is None:
                        continue
                    _, d, cs = CHAINS[ch]
                    c = cs[j]
                    u, r = d * NT + c // 2, (c % 2) * CHUNK
                    if j > 0:
                        pe.wait_ge(m_ssb, h * 10 + STATE_AT[(ch, j - 1)] + 1)
                    nc.tensor.matmul(bank[:, ch, 0:A1], kw[r:r + CHUNK, u * P:(u + 1) * P],
                                     v_aug[r:r + CHUNK, c // 2, 0:A1], start=True, stop=True).then_inc(m_sps, 1)

            def outputs(h):
                pe.wait_ge(m_pt, h + 1)
                pe.wait_ge(m_qd, h + 1)
                pe.wait_ge(m_ssb, h * 10 + 10)
                for d in range(N_DIR):
                    for t in range(NT):
                        u = d * NT + t
                        nc.tensor.matmul(bank[:, 4 + d, t * P:(t + 1) * P], v_aug[:, t, 0:P], PT[:, u * P:(u + 1) * P],
                                         start=(t == 0), stop=False, skip_group_check=True)
                    nc.tensor.matmul(bank[:, 6 + d, 0:T], ones, PT[:, d * T:(d + 1) * T], start=True, stop=False,
                                     skip_group_check=True)
                    for ch, j, _ in MCH:
                        _, dd, cs = CHAINS[ch]
                        C = cell_of(ch, j)
                        if dd != d or C is None:
                            continue
                        lo = cs[j] * CHUNK
                        q = mqd[:, d * T + lo:d * T + lo + CHUNK]
                        nc.tensor.matmul(bank[:, 4 + d, lo:lo + CHUNK], C[:, 0:P], q, start=False, stop=False,
                                         skip_group_check=True)
                        mm = nc.tensor.matmul(bank[:, 6 + d, lo:lo + CHUNK], C[:, P:P + 1].to_broadcast([P, P]), q,
                                              start=False, stop=False, skip_group_check=True)
                mm.then_inc(m_nd, 1)

            def squares_sum(h):
                pe.wait_ge(m_sq, h + 1)
                nc.tensor.matmul(bank[:, 7, 0:T], ones, msq, start=True, stop=True).then_inc(m_ss, 1)

            pe.wait_ge(gate_dve, G0 + 1)
            project(0)
            pe.wait_ge(gate_act, A0 + 6)
            columns_pe(pe, (W[8], W[17]), 7)
            pe.wait_ge(cols_ready, 2)
            states(0)
            with pe.Fori(0, H - 1) as h:
                outputs(h)
                project(h + 1, h)
                states(h + 1)
                pe.wait_ge(m_rs, h * 2 + 1)
            outputs(H - 1)
            pe.wait_ge(m_y, 2 * (H - 1))
            wout_begin(pe, 1, begun[:2])
            squares_sum(H - 1)
            wout_begin(pe, 1, begun[2:])
            pe.wait_ge(m_y, 2 * H)

        def mlstm_act(act):
            def projected(h, parts):
                for s, dst, scale in ((0, mqT, float(P) ** -0.5), (1, mkT, 1.0), (2, mvT, 1.0))[parts]:
                    act.wait_ge(m_proj, h * 4 + s + 1)
                    nc.scalar.activation(dst, bank[:, s, 0:T], ACT.Copy, scale=scale).then_inc(m_ev, 1)

            def output_gate(h):
                act.wait_ge(m_proj, h * 4 + 4)
                nc.scalar.activation(og, bank[:, 3, 0:T], ACT.Exp, scale=-1.0).then_inc(m_ev, 1)

            def columns(h):
                act.wait_ge(cols_ready, 2)
                nc.scalar.activation(hcol[:, 0:2, :].rearrange("p q (d t) -> p q t d", d=N_DIR),
                                     cols[:, 0:2, :, :].rearrange("p q t (d h) -> p q t d h", h=H)[:, :, :, :, bass.ds(h, 1)]
                                     .rearrange("p q t d h -> p q t (d h)"), ACT.Copy).then_inc(m_col, 1)

            def decays(h):
                act.wait_ge(m_arg, h * 2 + 2)
                nc.scalar.activation(mEM, mEM, ACT.Exp).then_inc(m_exp, 1)

            def values(h):
                act.wait_ge(m_tr, h * 2 + 2)
                nc.scalar.activation(v_aug[:, :, 0:P], bank[:, 5, 0:T].rearrange("p (t e) -> p t e", t=NT),
                                     ACT.Copy).then_inc(m_v, 1)

            def outputs(h):
                act.wait_ge(m_nd, h + 1)
                nc.scalar.activation(dirs(den), bank[:, 6:8, 0:T], ACT.Abs).then_inc(m_abs, 1)
                act.wait_ge(m_h, h + 1)
                nc.scalar.activation(msq, hs, ACT.Square).then_inc(m_sq, 1)

            def root(h):
                act.wait_ge(m_ss, h + 1)
                nc.scalar.activation(rs[:, 0, :], bank[:, 7, 0:T], ACT.Ln, bias=eps_col,
                                     scale=1.0 / P).then_inc(m_rs, 1)
                act.wait_ge(m_rs, h * 2 + 1)
                nc.scalar.activation(rs[:, 0, :], rs[:, 0, :], ACT.Exp, scale=-0.5).then_inc(m_rs, 1)

            columns(0)
            projected(0, slice(0, 3))
            output_gate(0)
            values(0)
            decays(0)
            with act.Fori(0, H - 1) as h:
                outputs(h)
                projected(h + 1, slice(0, 1))
                columns(h + 1)
                projected(h + 1, slice(1, 2))
                root(h)
                projected(h + 1, slice(2, 3))
                act.wait_ge(m_y, h * 2 + 2)
                output_gate(h + 1)
                values(h + 1)
                decays(h + 1)
            outputs(H - 1)
            root(H - 1)

        def mlstm_dve(dve):
            def states(h, before=None):
                dve.wait_ge(m_col, h + 1)
                dve.wait_ge(m_tr, h * 2 + 2)
                nc.vector.tensor_tensor(
                    kw.rearrange("p (d t i) -> p d t i", d=N_DIR, t=NT),
                    bank[:, 4, 0:T].rearrange("p (o t i) -> p o t i", o=1, t=NT).to_broadcast([P, N_DIR, NT, P]),
                    hcol[:, 1, :].rearrange("p (d t o) -> p d t o", d=N_DIR, o=1).to_broadcast([P, N_DIR, NT, P]),
                    ALU.mult).then_inc(m_kw, 1)
                dve.wait_ge(m_state, h * 16 + 16)
                if before is not None:
                    dve.wait_ge(m_stored, before * 16 + 16)
                for ch, j, s in MCH:
                    if s is None:
                        continue
                    kind, d, cs = CHAINS[ch]
                    c = cs[j]
                    end = c * CHUNK + CHUNK - 1 if d == 0 else c * CHUNK
                    new = Cs[:, d, j + 1, 0:A1] if kind == "s" else Cp[:, d, j, 0:A1]
                    dve.wait_ge(m_sps, h * 10 + s + 1)
                    old = cell_of(ch, j)
                    src = bank[:, ch, 0:A1]
                    if old is None:
                        nc.vector.tensor_copy(new, src).then_inc(m_ssb, 1)
                    else:
                        if j > 0:
                            dve.wait_ge(m_ssb, h * 10 + STATE_AT[(ch, j - 1)] + 1)
                        nc.vector.scalar_tensor_tensor(out=new, in0=old[:, 0:A1], scalar=mrows[:, 1, d, end:end + 1],
                                                       in1=src, op0=ALU.mult, op1=ALU.add).then_inc(m_ssb, 1)
                dve.wait_ge(m_em, h + 1)
                dve.wait_ge(m_qk, h + 1)
                nc.vector.tensor_tensor(dirs(PT), bank[:, 6, 0:T].unsqueeze(1).to_broadcast([P, N_DIR, T]), dirs(mEM),
                                        ALU.mult).then_inc(m_pt, 1)
                dve.wait_ge(m_ev, h * 4 + 4)
                step = Chain(dve, m_dve, turn=h, per=MLSTM_DVE)
                step(nc.vector.tensor_scalar(og, og, 1.0, None, ALU.add))
                step(nc.vector.reciprocal(og, og))

            def outputs(h):
                step = Chain(dve, m_dve, base=2, turn=h, per=MLSTM_DVE)
                dve.wait_ge(m_abs, h + 1)
                step(nc.vector.tensor_tensor(dirs(den), dirs(den), mrows[:, 2, :, :], ALU.max))
                step(nc.vector.reciprocal(den, den))
                step(nc.vector.tensor_tensor(dirs(hd), bank[:, 4:6, 0:T], dirs(den), ALU.mult))
                nc.vector.tensor_tensor(hs, hd[:, 0:T], hd[:, T:2 * T], ALU.add).then_inc(m_h, 1)
                dve.wait_ge(m_h, h + 1)
                dve.wait_ge(m_rs, h * 2 + 2)
                nc.vector.scalar_tensor_tensor(out=hd[:, 0:T], in0=hs, scalar=head_g[:, 1:2], in1=rs[:, 0, :],
                                               op0=ALU.mult, op1=ALU.mult).then_inc(m_y, 1)
                dve.wait_ge(m_y, h * 2 + 1)
                nc.vector.tensor_tensor(yT[:, bass.ds(h, 1), :].rearrange("p a t -> p (a t)"), hd[:, 0:T], og,
                                        ALU.mult).then_inc(m_y, 1)

            states(0)
            with dve.Fori(0, H - 1) as h:
                outputs(h)
                states(h + 1, h)
            outputs(H - 1)
            dve.wait_ge(m_y, 2 * H)

        def mlstm_pool(pool):
            with pool.Fori(0, H) as h:
                em4 = mEM.rearrange("p (d t i) -> p d t i", d=N_DIR, t=NT)
                pool.wait_ge(m_col, h + 1)
                pool.wait_ge(m_rows, h * 48 + 48)
                nc.gpsimd.tensor_tensor(em4, hcol[:, 0, :].rearrange("p (d t o) -> p d t o", d=N_DIR, o=1)
                                        .to_broadcast([P, N_DIR, NT, P]),
                                        mrows[:, 0, :, :].rearrange("p d (t i) -> p d t i", t=NT),
                                        ALU.subtract).then_inc(m_arg, 1)
                wait_turn(pool, m_arg, h * 2 + 1, const_in, 16 * CONST_DMAS)
                nc.gpsimd.tensor_scalar(mEM, mEM, 0.0, None, ALU.min).then_inc(m_arg, 1)
                pool.wait_ge(m_exp, h + 1)
                nc.gpsimd.tensor_tensor(em4, em4, incl.rearrange("p d (o i) -> p d o i", o=1)
                                        .to_broadcast([P, N_DIR, NT, P]), ALU.mult).then_inc(m_em, 1)
                pool.wait_ge(m_ev, h * 4 + 1)
                nc.gpsimd.tensor_tensor(dirs(mqd), mqT.unsqueeze(1).to_broadcast([P, N_DIR, T]), mrows[:, 1, :, :],
                                        ALU.mult).then_inc(m_qd, 1)

        def mlstm_sync(sp):
            def weights(h):
                sp.dma_start(slot[:, 0, :], a["mlstm_w"][bass.ds(h, 1), :, :].rearrange("a p n -> p (a n)")).then_inc(m_w, 16)

            def rows_and_states(h):
                for q in range(3):
                    src = rows_d[1, q].rearrange("(d h) t -> h d t", d=N_DIR)[bass.ds(h, 1), :, :]
                    sp.dma_start(mrows[:, q, :, :], src.to_broadcast([P, N_DIR, T])).then_inc(m_rows, 16)
                src = a["mlstm_C"].rearrange("(d h) k v -> h k d v", d=N_DIR)[bass.ds(h, 1)]
                sp.dma_start(Cs[:, :, 0, 0:A1], src.rearrange("a k d v -> (a k) d v")).then_inc(m_state, 16)

            def store(h):
                wait_turn(sp, m_ssb, h * 10 + 10, rows_out, 80)
                dst = a["o_C"].rearrange("(d h) k v -> h k d v", d=N_DIR)[bass.ds(h, 1)]
                sp.dma_start(dst.rearrange("a k d v -> (a k) d v"), Cp[:, :, 1, 0:A1]).then_inc(m_stored, 16)

            sp.wait_ge(delta_mm, 2 * KD)
            weights(0)
            wout_sync(sp, 1)
            sp.wait_ge(gate_dve, G0 + 2)
            sp.dma_start(rows_d[1, 0], W[11]).then_inc(rows_out, 16)
            sp.wait_ge(gate_act, A0 + 6)
            sp.dma_start(rows_d[1, 1], W[15]).then_inc(rows_out, 16)
            sp.dma_start(rows_d[1, 2], W[16]).then_inc(rows_out, 16)
            sp.wait_ge(rows_out, 80)
            rows_and_states(0)
            with sp.Fori(0, H - 1) as h:
                wait_turn(sp, m_proj, h * 4 + 4, rows_out, 80)
                weights(h + 1)
                store(h)
                wait_turn(sp, m_h, h + 1, rows_out, 80)
                rows_and_states(h + 1)
            store(H - 1)

        at[0] = 0
        htok = take(NT * D).rearrange("p (s n) -> p s n", s=NT)
        XG = take(2 * D).rearrange("p (s n) -> p s n", s=2)
        xgT = take(D)
        sl = take(FF)
        hid = take(FF)
        hidT = take(FF)
        ysb = take(D)
        NE3 = NT * E
        rt = [take(NE3) for _ in range(9)]
        r4 = [take(NT * GROUPS) for _ in range(8)]
        r1 = [take(NT) for _ in range(8)]
        g_tok_k = [take(NT) for _ in range(2)]
        place_f = take(2 * NT)
        r16 = [take(E) for _ in range(4)]
        more_f = take(MAX_MORE * E)
        lists = take(2 * P)
        far_f = sb("far_f", [P, 2 * N_PASSES])
        place = sb("place", [P, 2 * NT], U32)
        expl = sb("expl", [P, 2, N_PASSES + 4], U32)
        gidx = sb("gidx", [P, 2], U32)
        sidx = sb("sidx", [P, 1], U32)
        lsrc = sb("lsrc", [P, 2, NT, 2])
        n_more = sb("n_more", [1, 1], I32)
        pass_f = sb("pass_f", [P, N_PASSES])
        pass_expert = sb("pass_expert", [1, N_PASSES], I32)
        yk = slot[:, 0:2, :].rearrange("p s n -> p (s n)")[:, 0:2 * NT * D].rearrange("p (k t n) -> p k t n", k=2, t=NT)

        e_tr = sem("e_tr")
        e_tok = sem("e_tok")
        e_hn_out = sem("e_hn_out")
        e_logit = sem("e_logit")
        e_shift = sem("e_shift")
        e_prob = sem("e_prob")
        e_count = sem("e_count")
        e_pos = sem("e_pos")
        e_place = sem("e_place")
        far_out = sem("far_out")
        list_clear = sem("list_clear")
        m_ones = sem("m_ones")
        xg_clear = sem("xg_clear")
        e_listed = [sem(f"e_listed{i}") for i in range(DEPTH)]
        e_list_in = sem("e_list_in")
        e_lt = sem("e_lt")
        e_expl = sem("e_expl")
        e_yk = [sem(f"e_yk{t}") for t in range(NT)]
        e_comb = sem("e_comb")
        PASS = ("gu_in0", "gu_in1", "d_in0", "d_in1", "got0", "got1", "put", "idx", "xp",
                "xg", "up", "silu", "hid", "ht_ps", "ht", "y_ps", "y_sb", "y_free")
        moe = [{name: sem(f"e{layer}_{name}") for name in PASS} for layer in range(DEPTH)]

        w_gate = [slot[:, 0, :].rearrange("p (k f) -> p k f", k=KD), slot[:, 5, :].rearrange("p (k f) -> p k f", k=KD)]
        w_up = [slot[:, 1, :].rearrange("p (k f) -> p k f", k=KD), slot[:, 2, :].rearrange("p (k f) -> p k f", k=KD)]
        w_down = [slot[:, 4, :].rearrange("p (k n) -> p k n", k=KF), slot[:, 3, :].rearrange("p (k n) -> p k n", k=KF)]

        def passes(eng, layer):
            eng.wait_ge(e_place, 3 * layer + 3)
            more = eng.value_load(n_more[0:1, 0:1], min_val=0, max_val=MAX_MORE - 1)
            return eng.snap(more + more % 2 + E)

        def route_pe(pe, layer):
            for t in range(NT):
                for k in range(KD):
                    if t == 0:
                        pe.wait_ge(hn_ready, 2 * KD * (2 * layer + 1) + 2 * (k + 1))
                    mm = nc.tensor.matmul(bank[:, 7, t * E:(t + 1) * E], hnT[:, k, t * P:(t + 1) * P],
                                          router[:, k, :], start=(k == 0), stop=(k == KD - 1))
            mm.then_inc(e_logit, 1)
            for t in range(NT):
                if t == 2:
                    pe.wait_ge(e_tok, 6 * layer + 2)
                for k in range(KD):
                    mm = nc.tensor.transpose(bank[:, 2 * (t % 2) + k // 4, (k % 4) * P:(k % 4 + 1) * P],
                                             hnT[:, k, t * P:(t + 1) * P], ident)
                mm.then_inc(e_tr, 1)
            pe.wait_ge(e_count, layer + 1)
            before = const[:, C_BEFORE:C_BEFORE + P]
            nc.tensor.matmul(bank[:, 6, 0:NE3], before, rt[6], start=True, stop=True)
            mm = nc.tensor.matmul(bank[:, 6, NE3:2 * NE3], ones, rt[6], start=True, stop=True)
            mm.then_inc(e_pos, 1)
            pe.wait_ge(e_list_in, 16 * (layer + 1))
            lv = lists[0:N_PASSES, :].rearrange("n (p k) -> n k p", k=2)
            for k in range(2):
                mm = nc.tensor.transpose(bank[:, 7, k * N_PASSES:(k + 1) * N_PASSES], lv[:, k, :],
                                         ident[0:N_PASSES, 0:N_PASSES])
            mm.then_inc(e_lt, 1)

        def route_act(act, layer):
            act.wait_ge(e_shift, layer + 1)
            nc.scalar.activation(rt[0], rt[0], ACT.Exp).then_inc(e_prob, 1)
            for t in range(NT):
                act.wait_ge(e_tr, 3 * layer + t + 1)
                for b in range(2):
                    nc.scalar.activation(htok[:, t, b * 512:(b + 1) * 512], bank[:, 2 * (t % 2) + b, :],
                                         ACT.Copy).then_inc(e_tok, 1)

        def route_dve(dve, layer, step):
            def te(x):
                return x.rearrange("p (t e) -> p t e", t=NT)

            def tg(x):
                return x.rearrange("p (t g) -> p t g", t=NT)

            def each(x, n=E):
                return x.unsqueeze(2).to_broadcast([P, NT, n])

            def row(c, n=E):
                return const[:, c:c + n].unsqueeze(1).to_broadcast([P, NT, n])

            TT = nc.vector.tensor_tensor
            RED = nc.vector.tensor_reduce
            dve.wait_ge(e_logit, layer + 1)
            step(RED(r1[0], te(bank[:, 7, 0:NE3]), AX_X, ALU.max))
            TT(te(rt[0]), te(bank[:, 7, 0:NE3]), each(r1[0]), ALU.subtract).then_inc(e_shift, 1)
            dve.wait_ge(e_prob, layer + 1)
            step(RED(r1[1], te(rt[0]), AX_X, ALU.add))
            step(nc.vector.reciprocal(r1[1], r1[1]))
            step(TT(te(rt[1]), te(rt[0]), each(r1[1]), ALU.mult))
            step(TT(te(rt[2]), te(rt[1]), router_b[:, :].unsqueeze(1).to_broadcast([P, NT, E]), ALU.add))
            v = rt[2].rearrange("p (n i) -> p n i", i=PER_GROUP)
            step(TT(r4[0], v[:, :, 0], v[:, :, 1], ALU.max))
            step(TT(r4[1], v[:, :, 0], v[:, :, 1], ALU.min))
            step(TT(r4[2], v[:, :, 2], v[:, :, 3], ALU.max))
            step(TT(r4[3], v[:, :, 2], v[:, :, 3], ALU.min))
            step(TT(r4[4], r4[0], r4[2], ALU.max))
            step(TT(r4[5], r4[0], r4[2], ALU.min))
            step(TT(r4[6], r4[1], r4[3], ALU.max))
            step(TT(r4[6], r4[5], r4[6], ALU.max))
            step(TT(r4[4], r4[4], r4[6], ALU.add))
            step(RED(r1[2], tg(r4[4]), AX_X, ALU.max))
            step(TT(tg(r4[5]), tg(r4[4]), each(r1[2], GROUPS), ALU.is_equal))
            step(TT(tg(r4[5]), tg(r4[5]), row(C_FIRST4, GROUPS), ALU.mult))
            step(RED(r1[2], tg(r4[5]), AX_X, ALU.max))
            step(TT(tg(r4[7]), tg(r4[5]), each(r1[2], GROUPS), ALU.is_equal))
            step(nc.vector.tensor_scalar(r4[5], r4[7], 1.0, 1e30, ALU.subtract, ALU.mult))
            v3 = rt[3].rearrange("p (n i) -> p n i", i=PER_GROUP)
            step(TT(v3, v, r4[7].unsqueeze(2).to_broadcast([P, NT * GROUPS, PER_GROUP]), ALU.mult))
            step(TT(v3, v3, r4[5].unsqueeze(2).to_broadcast([P, NT * GROUPS, PER_GROUP]), ALU.add))
            for k in range(2):
                step(RED(r1[2], te(rt[3]), AX_X, ALU.max))
                step(TT(te(rt[7]), te(rt[3]), each(r1[2]), ALU.is_equal))
                step(TT(te(rt[7]), te(rt[7]), row(C_FIRST16), ALU.mult))
                step(RED(r1[2], te(rt[7]), AX_X, ALU.max))
                step(TT(te(rt[4 + k]), te(rt[7]), each(r1[2]), ALU.is_equal))
                if k == 0:
                    step(nc.vector.scalar_tensor_tensor(out=rt[3], in0=rt[4], scalar=-2e30, in1=rt[3],
                                                        op0=ALU.mult, op1=ALU.add))
                step(TT(rt[8], rt[1], rt[4 + k], ALU.mult))
                step(RED(r1[3 + k], te(rt[8]), AX_X, ALU.add))
            TT(rt[6], rt[4], rt[5], ALU.add).then_inc(e_count, 1)
            step(TT(r1[5], r1[3], r1[4], ALU.add))
            step(nc.vector.reciprocal(r1[5], r1[5]))
            for k in range(2):
                step(TT(g_tok_k[k], r1[3 + k], r1[5], ALU.mult))
            dve.wait_ge(e_pos, layer + 1)
            tiles = [bank[:, 6, NE3 + t * E:NE3 + (t + 1) * E] for t in range(NT)]
            step(nc.vector.tensor_copy(rt[8][:, 0:E], bank[:, 6, 0:E]))
            step(nc.vector.tensor_copy(r16[3], tiles[0]))
            for t in range(1, NT):
                step(TT(rt[8][:, t * E:(t + 1) * E], bank[:, 6, t * E:(t + 1) * E], r16[3], ALU.add))
                step(TT(r16[3], tiles[t], r16[3], ALU.add))
            count = r16[3]
            step(nc.vector.tensor_scalar(r16[0], count, float(P + 1), None, ALU.is_ge))
            for m in range(2, NT):
                step(nc.vector.scalar_tensor_tensor(out=r16[0], in0=count, scalar=float(m * P + 1), in1=r16[0],
                                                    op0=ALU.is_ge, op1=ALU.add))
            step(nc.vector.tensor_tensor_scan(r16[1], ones[:, 0:E], r16[0], 0.0, ALU.mult, ALU.add))
            step(TT(r16[2], r16[1], r16[0], ALU.subtract))
            step(TT(r16[2], r16[2], const[:, C_INDEX16:C_INDEX16 + E], ALU.subtract))
            step(nc.vector.tensor_scalar(r16[2], r16[2], float(E - 1), float(P), ALU.add, ALU.mult))
            for k in range(TOP_K):
                step(TT(rt[7], rt[8], rt[4 + k], ALU.mult))
                step(RED(r1[6], te(rt[7]), AX_X, ALU.add))
                step(TT(te(rt[7]), te(rt[4 + k]), row(C_INDEX16), ALU.mult))
                step(RED(r1[7], te(rt[7]), AX_X, ALU.add))
                step(TT(te(rt[7]), te(rt[4 + k]), r16[2].unsqueeze(1).to_broadcast([P, NT, E]), ALU.mult))
                step(RED(r1[2], te(rt[7]), AX_X, ALU.add))
                out = place_f[:, k * NT:(k + 1) * NT]
                step(nc.vector.scalar_tensor_tensor(out=out, in0=r1[7], scalar=float(P), in1=r1[6],
                                                    op0=ALU.mult, op1=ALU.add))
                step(nc.vector.scalar_tensor_tensor(out=r1[2], in0=r1[6], scalar=float(P), in1=r1[2],
                                                    op0=ALU.is_ge, op1=ALU.mult))
                step(TT(out, out, r1[2], ALU.add))
                nc.vector.tensor_copy(place[:, k * NT:(k + 1) * NT], out).then_inc(e_place, 1)
            m3 = more_f.rearrange("p (q e) -> p q e", q=MAX_MORE)
            step(TT(m3, r16[1].unsqueeze(1).to_broadcast([P, MAX_MORE, E]),
                    const[:, C_MORE:C_MORE + MAX_MORE].unsqueeze(2).to_broadcast([P, MAX_MORE, E]), ALU.is_le))
            step(RED(pass_f[:, E:N_PASSES], m3, AX_X, ALU.add))
            step(nc.vector.tensor_scalar(pass_f[:, E:N_PASSES], pass_f[:, E:N_PASSES], float(E - 1), None, ALU.min))
            step(nc.vector.tensor_copy(pass_f[:, 0:E], const[:, C_INDEX16:C_INDEX16 + E]))
            step(nc.vector.tensor_copy(pass_expert[:, :], pass_f[0:1, :]))
            nc.vector.tensor_copy(n_more[0:1, 0:1], r16[1][0:1, E - 1:E]).then_inc(e_place, 1)
            dve.wait_ge(e_lt, layer + 1)
            nc.vector.tensor_copy(expl[:, :, 0:N_PASSES], bank[:, 7, 0:2 * N_PASSES].rearrange("p (k n) -> p k n", k=2))\
                .then_inc(e_expl, 1)

        def route_sync(sp, layer):
            for t in range(NT):
                sp.wait_ge(e_tok, 6 * layer + 2 * t + 2)
                sp.dma_start(hn_d[layer][t * P:(t + 1) * P, :], htok[:, t, :]).then_inc(e_hn_out, 16)

        def lists_sync(sp, layer):
            sp.wait_ge(e_listed[layer], 16 * 2 * NT)
            sp.dma_start(lists[0:N_PASSES, :], list_d[layer].rearrange("(n p) k -> n (p k)", p=P)).then_inc(e_list_in, 16)

        def moe_pe(pe, layer, n):
            e = moe[layer]

            def loads(q, par, each):
                return (q + 1 if par else q + 2) * (each // 2)

            def gate_up(p, par):
                pe.wait_ge(e["xg"], 2 * p + 2)
                pe.wait_ge(e[f"gu_in{par}"], loads(p, par, 32))
                for b, w in ((0, w_gate[par]), (1, w_up[par])):
                    for k in range(KD):
                        mm = nc.tensor.matmul(bank[:, b, :], xgT[:, k * P:(k + 1) * P], w[:, k, :],
                                              start=(k == 0), stop=(k == KD - 1))
                    mm.then_inc(e["up"], 1)

            def turn_tokens(p, par):
                pe.wait_ge(e[f"got{par}"], loads(p, par, 16))
                for k in range(KD):
                    mm = nc.tensor.transpose(bank[:, 2 + k // 4, (k % 4) * P:(k % 4 + 1) * P],
                                             XG[:, par, k * P:(k + 1) * P], ident)
                mm.then_inc(e["xp"], 1)

            def down(p, par):
                pe.wait_ge(e["ht"], p + 1)
                pe.wait_ge(e[f"d_in{par}"], loads(p, par, 16))
                for b in range(2):
                    for k in range(KF):
                        mm = nc.tensor.matmul(bank[:, 5 + b, :], hidT[:, k * P:(k + 1) * P],
                                              w_down[par][:, k, b * 512:(b + 1) * 512],
                                              start=(k == 0), stop=(k == KF - 1))
                    mm.then_inc(e["y_ps"], 1)

            def turn_hidden(p):
                pe.wait_ge(e["hid"], p + 1)
                for k in range(KF):
                    mm = nc.tensor.transpose(bank[:, 4, k * P:(k + 1) * P], hid[:, k * P:(k + 1) * P], ident)
                mm.then_inc(e["ht_ps"], 1)

            def outputs_taken(p):
                pe.wait_ge(e["y_sb"], 2 * p + 2)

            turn_tokens(0, 0)
            gate_up(0, 0)
            turn_tokens(1, 1)
            turn_hidden(0)
            with pe.Fori(1, n - 1, 2) as p:
                gate_up(p, 1)
                turn_tokens(p + 1, 0)
                down(p - 1, 0)
                turn_hidden(p)
                gate_up(p + 1, 0)
                turn_tokens(p + 2, 1)
                outputs_taken(p - 1)
                down(p, 1)
                turn_hidden(p + 1)
                outputs_taken(p)
            gate_up(n - 1, 1)
            down(n - 2, 0)
            turn_hidden(n - 1)
            outputs_taken(n - 2)
            down(n - 1, 1)

        def moe_act(act, layer, n):
            e = moe[layer]

            def tokens(p):
                act.wait_ge(e["xp"], p + 1)
                nc.scalar.activation(xgT[:, 0:512], bank[:, 2, :], ACT.Copy).then_inc(e["xg"], 1)

            def gate(p):
                act.wait_ge(e["up"], 2 * p + 1)
                nc.scalar.activation(sl, bank[:, 0, :], ACT.Silu).then_inc(e["silu"], 1)

            def out(p):
                act.wait_ge(e["y_ps"], 2 * p + 1)
                act.wait_ge(e["y_free"], p + 1)
                nc.scalar.activation(ysb[:, 0:512], bank[:, 5, :], ACT.Copy).then_inc(e["y_sb"], 1)

            def hidden(p):
                act.wait_ge(e["ht_ps"], p + 1)
                nc.scalar.activation(hidT, bank[:, 4, :], ACT.Copy).then_inc(e["ht"], 1)

            tokens(0)
            gate(0)
            tokens(1)
            hidden(0)
            with act.Fori(1, n - 1) as p:
                gate(p)
                tokens(p + 1)
                out(p - 1)
                hidden(p)
            gate(n - 1)
            out(n - 2)
            hidden(n - 1)
            out(n - 1)

        def moe_dve(dve, layer, n):
            e = moe[layer]

            def tokens(p):
                dve.wait_ge(e["xp"], p + 1)
                nc.vector.tensor_copy(xgT[:, 512:1024], bank[:, 3, :]).then_inc(e["xg"], 1)

            def product(p):
                dve.wait_ge(e["up"], 2 * p + 2)
                dve.wait_ge(e["silu"], p + 1)
                nc.vector.tensor_tensor(hid, sl, bank[:, 1, :], ALU.mult).then_inc(e["hid"], 1)

            def out(p):
                dve.wait_ge(e["y_ps"], 2 * p + 2)
                dve.wait_ge(e["y_free"], p + 1)
                nc.vector.tensor_copy(ysb[:, 512:1024], bank[:, 6, :]).then_inc(e["y_sb"], 1)

            tokens(0)
            product(0)
            tokens(1)
            with dve.Fori(1, n - 1) as p:
                product(p)
                tokens(p + 1)
                out(p - 1)
            product(n - 1)
            out(n - 2)
            out(n - 1)

        def moe_start_pool(pool, layer):
            pool.wait_ge(list_clear, 16 * DEPTH)
            for k in range(2):
                pool.wait_ge(e_place, 3 * layer + 1 + k)
                for t in range(NT):
                    i = k * NT + t
                    nc.gpsimd.indirect_dma_start(list_d[layer], bass.IndirectOffsetOnAxis(ap=place[:, i:i + 1], axis=0),
                                                 lsrc[:, k, t, :], None).then_inc(e_listed[layer], 16)
            nc.gpsimd.memset(XG[:, :, :], 0.0).then_inc(xg_clear, 1)
            pool.wait_ge(xg_clear, layer + 1)
            pool.wait_ge(e_expl, layer + 1)
            pool.wait_ge(e_hn_out, 16 * NT * (layer + 1))

        def moe_pool(pool, layer, n):
            e = moe[layer]

            def gather(p, par, idx_count):
                nc.gpsimd.tensor_copy(gidx[:, par:par + 1], expl[:, 0, bass.ds(p, 1)]).then_inc(e["idx"], 1)
                wait_turn(pool, e["idx"], idx_count, e_expl, layer + 1)
                nc.gpsimd.indirect_dma_start(XG[:, par, :], None, hn_d[layer],
                                             bass.IndirectOffsetOnAxis(ap=gidx[:, par:par + 1], axis=0),
                                             bounds_check=T - 1, oob_is_err=False).then_inc(e[f"got{par}"], 16)

            def scatter(p, idx_count):
                nc.gpsimd.tensor_copy(sidx[:, :], expl[:, 1, bass.ds(p, 1)]).then_inc(e["idx"], 1)
                wait_turn(pool, e["idx"], idx_count, e_expl, layer + 1)
                wait_turn(pool, e["y_sb"], p * 2 + 2, e_expl, layer + 1)
                nc.gpsimd.indirect_dma_start(out_d[layer], bass.IndirectOffsetOnAxis(ap=sidx[:, 0:1], axis=0),
                                             ysb, None, bounds_check=2 * T - 1, oob_is_err=False).then_inc(e["put"], 16)
                wait_turn(pool, e["put"], p * 16 + 16, e_expl, layer + 1)
                pool.sem_inc(e["y_free"], 1)

            pool.sem_inc(e["y_free"], 1)
            gather(0, 0, 1)
            gather(1, 1, 2)
            for p in (2, 3):
                pool.wait_ge(e["xp"], p - 1)
                gather(p, p % 2, p + 1)
            with pool.Fori(0, n - 4, 2) as p:
                for i in range(2):
                    wait_turn(pool, e["xp"], p + i + 3, e_expl, layer + 1)
                    gather(p + i + 4, i, p * 2 + 2 * i + 5)
                    scatter(p + i, p * 2 + 2 * i + 6)
            for i in range(4):
                scatter(n - 4 + i, n * 2 - 3 + i)

        def moe_weights(sp, layer):
            e = moe[layer]

            def expert(p):
                x = sp.value_load(pass_expert[0:1, bass.ds(p, 1)], min_val=0, max_val=E - 1)
                return sp.snap(x + layer * E)

            def gate_up(x, par):
                for dst, name in ((w_gate, "w_g"), (w_up, "w_u")):
                    sp.dma_start(dst[par].rearrange("p k f -> p (k f)"),
                                 a[name][bass.ds(x, 1)].rearrange("a p n -> (a p) n")).then_inc(e[f"gu_in{par}"], 16)

            def down(x, par):
                sp.dma_start(w_down[par].rearrange("p k n -> p (k n)"),
                             a["w_d"][bass.ds(x, 1)].rearrange("a p n -> (a p) n")).then_inc(e[f"d_in{par}"], 16)

            return e, expert, gate_up, down

        def moe_first_sync(sp, layer):
            e, expert, gate_up, down = moe_weights(sp, layer)
            for p in range(2):
                gate_up(layer * E + p, p)
                down(layer * E + p, p)
                if p == 0:
                    route_sync(sp, layer)

        def moe_sync(sp, layer, n):
            e, expert, gate_up, down = moe_weights(sp, layer)
            sp.wait_ge(e["up"], 2)
            gate_up(layer * E + 2, 0)
            with sp.Fori(1, n - 3, 2) as p:
                x = [expert(p + i) for i in range(1, 4)]
                wait_turn(sp, e["up"], p * 2 + 2, e_place, 3 * layer + 3)
                gate_up(x[1], 1)
                wait_turn(sp, e["y_ps"], p * 2, e_place, 3 * layer + 3)
                down(x[0], 0)
                wait_turn(sp, e["up"], p * 2 + 4, e_place, 3 * layer + 3)
                gate_up(x[2], 0)
                wait_turn(sp, e["y_ps"], p * 2 + 2, e_place, 3 * layer + 3)
                down(x[1], 1)
            wait_turn(sp, e["up"], n * 2 - 4, e_place, 3 * layer + 3)
            x = [expert(n - 2), expert(n - 1)]
            gate_up(x[1], 1)
            wait_turn(sp, e["y_ps"], n * 2 - 6, e_place, 3 * layer + 3)
            down(x[0], 0)
            wait_turn(sp, e["y_ps"], n * 2 - 4, e_place, 3 * layer + 3)
            down(x[1], 1)
            wait_turn(sp, e["up"], n * 2, e_place, 3 * layer + 3)
            wait_turn(sp, e["y_free"], n + 1, e_place, 3 * layer + 3)
            src = out_d[layer].rearrange("(k t p) n -> p k t n", k=2, t=NT)
            for t in range(NT):
                sp.dma_start(yk[:, :, t], src[:, :, t]).then_inc(e_yk[t], 16)

        def combine_dve(dve, layer, step):
            for t in range(NT):
                dve.wait_ge(e_yk[t], 16 * (layer + 1))
                step(nc.vector.tensor_scalar(yk[:, 0, t, :], yk[:, 0, t, :], g_tok_k[0][:, t:t + 1], None, ALU.mult))
                nc.vector.scalar_tensor_tensor(out=yk[:, 0, t, :], in0=yk[:, 1, t, :], scalar=g_tok_k[1][:, t:t + 1],
                                               in1=yk[:, 0, t, :], op0=ALU.mult, op1=ALU.add).then_inc(e_comb, 1)

        def combine_pe(pe, layer):
            for t in range(NT):
                pe.wait_ge(e_comb, 3 * layer + t + 1)
                for c in range(KD):
                    mm = nc.tensor.transpose(bank[:, c, t * P:(t + 1) * P], yk[:, 0, t, c * P:(c + 1) * P], ident)
                    if t == NT - 1:
                        mm.then_inc(delta_mm, 1)

        LOADS = (("const", const[:, :]), ("xT", xT[:, :, :]), ("posT", hnT[:, :, 0:T_SAMPLE]),
                 ("norm_g", norm_g[:, :, :]), ("ada_b", ada_b[:, :]), ("head_g", head_g[:, :]),
                 ("conv_w", conv_w[:, :, :, :]), ("w_gates", w_gates[:, :, :, :]), ("router", router[:, :, :]),
                 ("row_bias", row_bias[:, 0:4]), ("lsrc", lsrc[:, :, :, :]))
        CONST_DMAS = len(LOADS) + 2

        block = ctx.enter_context(nc.Block())

        @block.sync
        def _(sp):
            sp.dma_start(cond[:, :, :], a["cond"]).then_inc(cond_in, 16)
            for name, dst in LOADS:
                sp.dma_start(dst, a[name]).then_inc(const_in, 16)
            sp.dma_start(router_b[:, :], a["router_b"].to_broadcast([P, E])).then_inc(const_in, 16)
            sp.dma_start(m_fin[:, 1:2], a["mlstm_m"]).then_inc(const_in, 16)
            for i in range(6):
                sp.dma_start(slot[:, i, :], a["ada_w"][i]).then_inc(ada_in[i], 16)
            sp.wait_ge(ada_used, 1)
            sp.dma_start(slot[:, 0, :], a["gdn_w"][0]).then_inc(g_w, 16)
            for b in (6, 7):
                sp.wait_ge(ada_used, ADA_SLOT[b] + 1)
                sp.dma_start(slot[:, ADA_SLOT[b], :], a["ada_w"][b]).then_inc(ada_in[ADA_SLOT[b]], 16)
            sp.wait_ge(far_out, 1)
            for layer in range(DEPTH):
                sp.dma_start(list_d[layer].rearrange("(p n) k -> p (n k)", p=P), far_f[:, :]).then_inc(list_clear, 16)
            sp.wait_ge(gate_dve, 2)
            sp.dma_start(rows_d[0, 0], W[7]).then_inc(rows_out, 16)
            sp.dma_start(rows_d[0, 1], W[8]).then_inc(rows_out, 16)
            gdn_sync(sp)
            sp.wait_ge(delta_mm, KD)
            moe_first_sync(sp, 0)
            lists_sync(sp, 0)
            moe_sync(sp, 0, passes(sp, 0))
            mlstm_sync(sp)
            sp.wait_ge(delta_mm, 3 * KD)
            moe_first_sync(sp, 1)
            lists_sync(sp, 1)
            moe_sync(sp, 1, passes(sp, 1))
            sp.dma_start(a["o_m"], m_fin[:, 2:3]).then_inc(stored, 16)
            for ks in (slice(0, KD // 2), slice(KD // 2, KD)):
                sp.wait_ge(hn_scaled, 2 * KD * 2 * DEPTH + 2 * ks.stop)
                sp.dma_start(a["o_y"][:, ks], hnT[:, ks, :]).then_inc(stored, 16)
            sp.wait_ge(stored, 48)
            sp.wait_ge(g_stored, 16 * H)
            sp.wait_ge(m_stored, 16 * H)

        @block.tensor
        def _(pe):
            pe.wait_ge(const_in, 16 * CONST_DMAS)
            block_norm_pe(pe, 0)
            pe.wait_ge(cond_ready, 1)
            ada_products_pe(pe, 0)
            ada_turn_pe(pe, 0)
            for layer in range(DEPTH):
                begun = ((0, 1), (0, 1, 2, 3))[layer]
                if layer > 0:
                    block_norm_pe(pe, 2 * layer)
                gates_pe(pe, layer)
                if layer == 0:
                    ada_products_pe(pe, 1)
                    pe.wait_ge(gate_dve, 3)
                    columns_pe(pe, (W[7], W[8], W[12], W[11]), 2)
                    pe.wait_ge(cols_ready, 1)
                    ada_turn_pe(pe, 1)
                    pe.wait_ge(mod_ready, 2)
                    gdn_pe(pe)
                    wout_begin(pe, layer, begun)
                    pe.wait_ge(g_y, 2 * H + 2)
                else:
                    mlstm_pe(pe, begun)
                wout_end(pe, layer, begun)
                block_norm_pe(pe, 2 * layer + 1)
                route_pe(pe, layer)
                n = passes(pe, layer)
                pe.wait_ge(e_expl, layer + 1)
                moe_pe(pe, layer, n)
                pe.wait_ge(moe[layer]["y_sb"], n * 2)
                combine_pe(pe, layer)
            block_norm_pe(pe, 2 * DEPTH)

        @block.scalar
        def _(act):
            act.wait_ge(cond_in, 16)
            nc.scalar.activation(cond[:, :, :], cond[:, :, :], ACT.Silu).then_inc(cond_ready, 1)
            act.wait_ge(const_in, 16 * CONST_DMAS)
            block_norm_act(act, 0)
            gdn_gates_act(act)
            act.wait_ge(rows_out, 32)
            gdn_act(act)
            block_norm_act(act, 1)
            route_act(act, 0)
            moe_act(act, 0, passes(act, 0))
            block_norm_act(act, 2)
            mlstm_gates_act(act)
            act.wait_ge(rows_out, 80)
            mlstm_act(act)
            block_norm_act(act, 3)
            route_act(act, 1)
            moe_act(act, 1, passes(act, 1))
            block_norm_act(act, 4)

        @block.vector
        def _(dve):
            step = Chain(dve, dve_step)
            dve.wait_ge(const_in, 16 * CONST_DMAS)
            nc.vector.memset(m_fin[:, 0:1], 0.0).then_inc(g_y, 2)
            nc.vector.tensor_tensor(xT[:, :, T_PROMPT:T], xT[:, :, T_PROMPT:T], hnT[:, :, 0:T_SAMPLE],
                                    ALU.add).then_inc(moved, 1)
            ada_group_dve(dve, 0)
            dve.wait_ge(mod_ready, 1)
            dve.wait_ge(moved, 1)
            gains_dve(step, (0,))
            block_norm_dve(dve, 0)
            gdn_gates_dve(dve, step)
            ada_group_dve(dve, 1)
            dve.wait_ge(mod_ready, 2)
            gdn_dve(dve)
            dve.wait_ge(g_mod, H)
            gains_dve(step, range(1, 2 * DEPTH))
            residual_dve(dve, 0)
            dve.wait_ge(moved, moved_after(1))
            block_norm_dve(dve, 1)
            route_dve(dve, 0, step)
            moe_dve(dve, 0, passes(dve, 0))
            combine_dve(dve, 0, step)
            residual_dve(dve, 1)
            dve.wait_ge(moved, moved_after(2))
            block_norm_dve(dve, 2)
            mlstm_gates_dve(dve, step)
            mlstm_dve(dve)
            residual_dve(dve, 2)
            dve.wait_ge(moved, moved_after(3))
            block_norm_dve(dve, 3)
            route_dve(dve, 1, step)
            moe_dve(dve, 1, passes(dve, 1))
            combine_dve(dve, 1, step)
            residual_dve(dve, 3)
            dve.wait_ge(moved, moved_after(4))
            block_norm_dve(dve, 4)

        @block.gpsimd
        def _(pool):
            nc.gpsimd.memset(far_f[:, :], float(FAR)).then_inc(far_out, 1)
            gdn_pool(pool)
            moe_start_pool(pool, 0)
            moe_pool(pool, 0, passes(pool, 0))
            pool.wait_ge(cols_ready, 2)
            pool.wait_ge(rows_out, 80)
            nc.gpsimd.memset(v_aug[:, :, P:VA], 1.0).then_inc(m_ones, 1)
            mlstm_pool(pool)
            moe_start_pool(pool, 1)
            moe_pool(pool, 1, passes(pool, 1))


_OUTS = [("o_y", (P, KD, T)), ("o_S", (N_DIR * H, P, P)), ("o_C", (N_DIR * H, P, P + 1)), ("o_m", (N_DIR * H, 1))]


def laid_out(v):
    f = np.ascontiguousarray
    x = np.concatenate([v["x_prompt"][0], v["x_sample"][0]], 0)

    def heads(w):
        w = w[0][:, :4 * D].reshape(KD, P, 4, H, P)
        return f(w.transpose(3, 1, 0, 2, 4).reshape(H, P, KD * 4 * P))

    def gates(w):
        return w[0][:, 4 * D:].reshape(KD, P, 2 * N_DIR * H).transpose(1, 0, 2)

    def experts(w, k):
        return f(w.reshape(DEPTH * E, k, P, -1).transpose(0, 2, 1, 3).reshape(DEPTH * E, P, -1))

    norms = np.stack([v["norm1_g"][0], v["norm2_g"][0], v["norm1_g"][1], v["norm2_g"][1], v["final_norm_g"]])
    return {
        "const": constants(), "posT": grid_positions(),
        "xT": f(x.T.reshape(KD, P, T).transpose(1, 0, 2)),
        "cond": f(np.stack([v["c_ctx"], v["c"][0]], -1).reshape(KD, P, 2).transpose(1, 0, 2)),
        "norm_g": f(norms.reshape(-1, KD, P).transpose(2, 0, 1)),
        "ada_w": f(v["ada_w"].reshape(DEPTH, KD, P, 6 * D // 512, 512).transpose(0, 3, 2, 1, 4).reshape(ADA_BLOCKS, P, -1)),
        "ada_b": f(v["ada_b"].reshape(-1, P).T),
        "head_g": f(np.stack([v["gdn_norm_g"][0], v["mlstm_norm_g"][0]], -1)),
        "conv_w": f(v["gdn_conv_w"][0].reshape(3, 3, H, P).transpose(3, 2, 0, 1)),
        "w_gates": f(np.stack([gates(v["gdn_w_in"]), gates(v["mlstm_w_in"])], 1)),
        "router": f(v["router_w"].reshape(KD, P, E).transpose(1, 0, 2)),
        "router_b": f(v["router_bias"].reshape(1, E)),
        "row_bias": f(np.stack([v["gdn_a_log"].ravel(), v["gdn_dt_bias"].ravel(), v["mlstm_gate_b"][0, 0].ravel(),
                                v["mlstm_gate_b"][0, 1].ravel()], -1)),
        "lsrc": token_list_sources(),
        "mlstm_m": f(v["state_mlstm_m"].reshape(-1, 1)),
        "gdn_w": heads(v["gdn_w_in"]), "mlstm_w": heads(v["mlstm_w_in"]),
        "w_out": f(np.stack([w[0].reshape(H, P, D).transpose(1, 0, 2).reshape(P, -1)
                             for w in (v["gdn_w_out"], v["mlstm_w_out"])])),
        "gdn_S": f(v["state_gdn_S"].reshape(N_DIR * H, P, P)),
        "mlstm_C": f(np.concatenate([v["state_mlstm_C"].reshape(N_DIR * H, P, P),
                                     v["state_mlstm_n"].reshape(N_DIR * H, P, 1)], -1)),
        "w_g": experts(v["exp_w_gate"], KD), "w_u": experts(v["exp_w_up"], KD), "w_d": experts(v["exp_w_down"], KF),
    }


def kernel(**inputs):
    import concourse.bacc as bacc
    from concourse.bass_utils import run_bass_kernel_spmd

    nc = bacc.Bacc("TRN2", target_bir_lowering=False, num_devices=1)
    arrays, args = {}, {}
    for name, x in laid_out({k: np.asarray(x) for k, x in inputs.items()}).items():
        arrays[f"in_{name}"] = x
        args[name] = nc.dram_tensor(f"in_{name}", x.shape, mybir.dt.from_np(x.dtype), kind="ExternalInput").ap()
    for name, shape in _OUTS:
        args[name] = nc.dram_tensor(f"out_{name}", shape, F32, kind="ExternalOutput").ap()
    program(nc, args)
    r = run_bass_kernel_spmd(nc, [arrays], core_ids=[0]).results[0]
    y = np.ascontiguousarray(r["out_o_y"].transpose(2, 1, 0).reshape(T, D))
    C = r["out_o_C"].reshape(1, 1, N_DIR, H, P, P + 1)
    return (y[:T_PROMPT].reshape(1, T_PROMPT, D), y[T_PROMPT:].reshape(1, T_SAMPLE, D),
            r["out_o_S"].reshape(1, 1, N_DIR, H, P, P), np.ascontiguousarray(C[..., :P]),
            np.ascontiguousarray(C[..., P]), r["out_o_m"].reshape(1, 1, N_DIR, H))
```
